# Optimizing a Trainium2 kernel written in Bass

```python
import math
import jax
import jax.numpy as jnp
from jax import lax
import numpy as np

D_MODEL = 1024
BATCH = 1
SEQ = 128
DEPTH = 1
DEC_BATCH = 1
DEC_SEQ = 1024
PAST_LEN = 256

GRID_W = 64
CHUNK = 128
EPS = 1e-6
N_DIR = 2
SSD_D_INNER = 1024
SSD_HEADDIM = 64
SSD_HEADS = SSD_D_INNER // SSD_HEADDIM
SSD_GROUPS = 4
SSD_STATE = 64
SSD_CONV = 3
SSD_CONV_CH = SSD_D_INNER + 2 * SSD_GROUPS * SSD_STATE
ML_HEADS = 8
ML_DV = 128
ML_DK = 64
ML_V_WIDTH = ML_HEADS * ML_DV
ML_QK_WIDTH = ML_HEADS * ML_DK
D_FF = 2816
FFN_CONV = 3
IN_SPLITS = (SSD_D_INNER, SSD_CONV_CH, N_DIR * SSD_HEADS, ML_QK_WIDTH, ML_QK_WIDTH, ML_V_WIDTH,
             ML_V_WIDTH, N_DIR * ML_HEADS, N_DIR * ML_HEADS, 2 * D_MODEL)
IN_COLS = sum(IN_SPLITS)

kernel_name = 'hybrid_ssd_mlstm_diffusion_step'

def _split(x, sizes):
    offsets = [int(o) for o in np.cumsum(sizes)[:-1]]
    return jnp.split(x, offsets, axis=-1)

def _flip(t):
    return jnp.flip(t, axis=1)

def rmsnorm(x, w):
    xf = x.astype(jnp.float32)
    y = xf * lax.rsqrt(jnp.mean(xf * xf, axis=-1, keepdims=True) + EPS)
    return y.astype(x.dtype) * w

def dwconv1d(x, w, b):
    y = lax.conv_general_dilated(x, w[:, None, :], window_strides=(1,), padding='SAME',
                                 dimension_numbers=('NWC', 'WIO', 'NWC'),
                                 feature_group_count=x.shape[-1])
    return y + b

def dwconv2d(x, w, b):
    y = lax.conv_general_dilated(x, w[:, :, None, :], window_strides=(1, 1), padding='SAME',
                                 dimension_numbers=('NHWC', 'HWIO', 'NHWC'),
                                 feature_group_count=x.shape[-1])
    return y + b

def ssd_chunked(x, dt, A, Bm, Cm, s0):
    f32 = jnp.float32
    b, l, h, p = x.shape
    n = Bm.shape[-1]
    c = l // CHUNK
    xc = x.astype(f32).reshape(b, c, CHUNK, h, p)
    dtc = dt.astype(f32).reshape(b, c, CHUNK, h)
    Bc = Bm.astype(f32).reshape(b, c, CHUNK, h, n)
    Cc = Cm.astype(f32).reshape(b, c, CHUNK, h, n)
    acum = jnp.cumsum(dtc * A.astype(f32), axis=2)
    acum_h = jnp.swapaxes(acum, 2, 3)
    mask = jnp.tril(jnp.ones((CHUNK, CHUNK), dtype=bool))
    decay = jnp.exp(jnp.where(mask, acum_h[..., :, None] - acum_h[..., None, :], -jnp.inf))
    xdt = xc * dtc[..., None]
    scores = jnp.einsum('bcthn,bcshn->bchts', Cc, Bc) * decay
    y_diag = jnp.einsum('bchts,bcshp->bcthp', scores, xdt)
    to_end = jnp.exp(acum[:, :, -1:, :] - acum)
    chunk_states = jnp.einsum('bcshn,bcshp->bchpn', Bc * to_end[..., None], xdt)
    chunk_decay = jnp.exp(acum[:, :, -1, :])

    def step(s, inp):
        dec, st = inp
        return dec[..., None, None] * s + st, s

    s_fin, starts = lax.scan(step, s0.astype(f32),
                             (jnp.moveaxis(chunk_decay, 1, 0), jnp.moveaxis(chunk_states, 1, 0)))
    starts = jnp.moveaxis(starts, 0, 1)
    y_off = jnp.einsum('bcthn,bchpn->bcthp', Cc * jnp.exp(acum)[..., None], starts)
    y = (y_diag + y_off).reshape(b, l, h, p)
    return y.astype(x.dtype), s_fin

def mlstm_chunked(q, k, v, i_pre, f_pre, C0, n0, m0):
    f32 = jnp.float32
    b, l, h, dk = q.shape
    dv = v.shape[-1]
    c = l // CHUNK
    qc = q.astype(f32).reshape(b, c, CHUNK, h, dk)
    kc = k.astype(f32).reshape(b, c, CHUNK, h, dk)
    vc = v.astype(f32).reshape(b, c, CHUNK, h, dv)
    ig = jnp.moveaxis(i_pre.astype(f32).reshape(b, c, CHUNK, h), 2, 3)
    logf = jax.nn.log_sigmoid(jnp.moveaxis(f_pre.astype(f32).reshape(b, c, CHUNK, h), 2, 3))
    bcum = jnp.cumsum(logf, axis=-1)
    mask = jnp.tril(jnp.ones((CHUNK, CHUNK), dtype=bool))
    log_d = jnp.where(mask, bcum[..., :, None] - bcum[..., None, :] + ig[..., None, :], -jnp.inf)
    log_end = bcum[..., -1:] - bcum + ig
    m_loc = jnp.max(log_end, axis=-1)
    w_end = jnp.exp(log_end - m_loc[..., None])
    C_loc = jnp.einsum('bchs,bcshv,bcshk->bchvk', w_end, vc, kc)
    n_loc = jnp.einsum('bchs,bcshk->bchk', w_end, kc)
    b_tot = bcum[..., -1]

    def step(carry, inp):
        Cp, np_, mp = carry
        bt, ml, Cl, nl = inp
        m_new = jnp.maximum(bt + mp, ml)
        a_old = jnp.exp(bt + mp - m_new)
        a_loc = jnp.exp(ml - m_new)
        C_new = a_old[..., None, None] * Cp + a_loc[..., None, None] * Cl
        n_new = a_old[..., None] * np_ + a_loc[..., None] * nl
        return (C_new, n_new, m_new), (Cp, np_, mp)

    (C_fin, n_fin, m_fin), (Cs, ns, ms) = lax.scan(
        step, (C0.astype(f32), n0.astype(f32), m0.astype(f32)),
        (jnp.moveaxis(b_tot, 1, 0), jnp.moveaxis(m_loc, 1, 0),
         jnp.moveaxis(C_loc, 1, 0), jnp.moveaxis(n_loc, 1, 0)))
    Cs = jnp.moveaxis(Cs, 0, 1)
    ns = jnp.moveaxis(ns, 0, 1)
    ms = jnp.moveaxis(ms, 0, 1)
    log_inter = bcum + ms[..., None]
    m_t = jnp.maximum(log_inter, jnp.max(log_d, axis=-1))
    w_intra = jnp.exp(log_d - m_t[..., None])
    w_inter = jnp.exp(log_inter - m_t)
    s_qk = jnp.einsum('bcthk,bcshk->bchts', qc, kc) * w_intra
    num = (jnp.einsum('bchts,bcshv->bchtv', s_qk, vc)
           + w_inter[..., None] * jnp.einsum('bcthk,bchvk->bchtv', qc, Cs))
    den = jnp.sum(s_qk, axis=-1) + w_inter * jnp.einsum('bcthk,bchk->bcht', qc, ns)
    den = jnp.maximum(jnp.abs(den), jnp.exp(-m_t))
    hout = num / den[..., None]
    hout = jnp.moveaxis(hout, 2, 3).reshape(b, l, h, dv)
    return hout.astype(v.dtype), C_fin, n_fin, m_fin

def mixer(u, lp, ssd_s0, ml_C0, ml_n0, ml_m0):
    b, l, _ = u.shape
    proj = u @ lp['w_in']
    z, xbc, dt_raw, q, k, v, o, i_raw, f_raw, gates = _split(proj, IN_SPLITS)
    xbc = jax.nn.silu(dwconv1d(xbc, lp['ssd_conv_w'], lp['ssd_conv_b']))
    xs, Bm, Cm = _split(xbc, (SSD_D_INNER, SSD_GROUPS * SSD_STATE, SSD_GROUPS * SSD_STATE))
    xs = xs.reshape(b, l, SSD_HEADS, SSD_HEADDIM)
    rep = SSD_HEADS // SSD_GROUPS
    Bm = jnp.repeat(Bm.reshape(b, l, SSD_GROUPS, SSD_STATE), rep, axis=2)
    Cm = jnp.repeat(Cm.reshape(b, l, SSD_GROUPS, SSD_STATE), rep, axis=2)
    dt = jax.nn.softplus(dt_raw.reshape(b, l, N_DIR, SSD_HEADS) + lp['ssd_dt_bias'])
    A = -jnp.exp(lp['ssd_a_log'])
    y_f, s_f = ssd_chunked(xs, dt[:, :, 0], A[0], Bm, Cm, ssd_s0[:, 0])
    y_b, s_b = ssd_chunked(_flip(xs), _flip(dt[:, :, 1]), A[1], _flip(Bm), _flip(Cm), ssd_s0[:, 1])
    y = y_f + _flip(y_b) + lp['ssd_d'][:, None] * xs
    y = rmsnorm(y.reshape(b, l, SSD_D_INNER) * jax.nn.silu(z), lp['ssd_norm'])
    y_ssd = y @ lp['w_o_ssd']
    q = q.reshape(b, l, ML_HEADS, ML_DK) * (ML_DK ** -0.5)
    k = k.reshape(b, l, ML_HEADS, ML_DK)
    v = v.reshape(b, l, ML_HEADS, ML_DV)
    ig = i_raw.reshape(b, l, N_DIR, ML_HEADS) + lp['ml_i_bias']
    fg = f_raw.reshape(b, l, N_DIR, ML_HEADS) + lp['ml_f_bias']
    h_f, C_f, n_f, m_f = mlstm_chunked(q, k, v, ig[:, :, 0], fg[:, :, 0],
                                       ml_C0[:, 0], ml_n0[:, 0], ml_m0[:, 0])
    h_b, C_b, n_b, m_b = mlstm_chunked(_flip(q), _flip(k), _flip(v), _flip(ig[:, :, 1]), _flip(fg[:, :, 1]),
                                       ml_C0[:, 1], ml_n0[:, 1], ml_m0[:, 1])
    hm = rmsnorm(h_f + _flip(h_b), lp['ml_norm'].reshape(ML_HEADS, ML_DV))
    hm = hm.reshape(b, l, ML_V_WIDTH) * jax.nn.sigmoid(o)
    y_ml = hm @ lp['w_o_ml']
    g_ssd, g_ml = _split(gates, (D_MODEL, D_MODEL))
    out = (jax.nn.sigmoid(g_ssd) * y_ssd + jax.nn.sigmoid(g_ml) * y_ml) @ lp['w_out']
    new_states = (jnp.stack([s_f, s_b], axis=1), jnp.stack([C_f, C_b], axis=1),
                  jnp.stack([n_f, n_b], axis=1), jnp.stack([m_f, m_b], axis=1))
    return out, new_states

def conv_ffn(u, lp, on_grid):
    g, val = _split(u @ lp['w_up'], (D_FF, D_FF))
    if on_grid:
        b, l, _ = g.shape
        rows = l // GRID_W
        g = dwconv2d(g.reshape(b, rows, GRID_W, D_FF), lp['ffn_conv_w'], lp['ffn_conv_b']).reshape(b, l, D_FF)
    else:
        g = dwconv1d(g, lp['ffn_conv_w'][1], lp['ffn_conv_b'])
    return (jax.nn.silu(g) * val) @ lp['w_down']

def trunk_layer(h, mod, lp, states, on_grid):
    shift1, scale1, gate1, shift2, scale2, gate2 = jnp.split(mod, 6, axis=-1)
    u = rmsnorm(h, lp['norm_mix']) * (1.0 + scale1) + shift1
    mix, new_states = mixer(u, lp, states[0], states[1], states[2], states[3])
    h = h + gate1 * mix
    u = rmsnorm(h, lp['norm_ffn']) * (1.0 + scale2) + shift2
    h = h + gate2 * conv_ffn(u, lp, on_grid)
    return h, new_states

def setup_inputs(seed: int = 0) -> dict:
    key = jax.random.key(seed)
    ks = jax.random.split(key, 32)

    def nrm(k, shape, scale):
        return jax.random.normal(k, shape, jnp.float32) * scale

    def gain(k, shape):
        return 1.0 + 0.05 * jax.random.normal(k, shape, jnp.float32)

    dt0 = jnp.exp(jax.random.uniform(ks[13], (DEPTH, N_DIR, SSD_HEADS), jnp.float32,
                                     math.log(1e-3), math.log(1e-1)))
    return {
        'x_prompt': nrm(ks[0], (BATCH, SEQ, D_MODEL), 1.0),
        'x_sample': nrm(ks[1], (DEC_BATCH, DEC_SEQ, D_MODEL), 1.0),
        'state_ssd': nrm(ks[2], (DEC_BATCH, DEPTH, N_DIR, SSD_HEADS, SSD_HEADDIM, SSD_STATE), 0.5),
        'state_mlstm_C': nrm(ks[3], (DEC_BATCH, DEPTH, N_DIR, ML_HEADS, ML_DV, ML_DK), 0.1),
        'state_mlstm_n': nrm(ks[4], (DEC_BATCH, DEPTH, N_DIR, ML_HEADS, ML_DK), 0.1),
        'state_mlstm_m': nrm(ks[5], (DEC_BATCH, DEPTH, N_DIR, ML_HEADS), 1.0),
        'c': nrm(ks[6], (DEC_BATCH, D_MODEL), 1.0),
        'c_ctx': nrm(ks[7], (D_MODEL,), 1.0),
        'w_ada': nrm(ks[8], (DEPTH, D_MODEL, 6 * D_MODEL), D_MODEL ** -0.5),
        'b_ada': nrm(ks[9], (DEPTH, 6 * D_MODEL), 0.02),
        'norm_mix': gain(ks[10], (DEPTH, D_MODEL)),
        'w_in': nrm(ks[11], (DEPTH, D_MODEL, IN_COLS), D_MODEL ** -0.5),
        'ssd_conv_w': nrm(ks[12], (DEPTH, SSD_CONV, SSD_CONV_CH), SSD_CONV ** -0.5),
        'ssd_conv_b': nrm(ks[15], (DEPTH, SSD_CONV_CH), 0.02),
        'ssd_dt_bias': dt0 + jnp.log(-jnp.expm1(-dt0)),
        'ssd_a_log': jnp.log(jax.random.uniform(ks[14], (DEPTH, N_DIR, SSD_HEADS), jnp.float32, 1.0, 16.0)),
        'ssd_d': gain(ks[16], (DEPTH, SSD_HEADS)),
        'ssd_norm': gain(ks[17], (DEPTH, SSD_D_INNER)),
        'w_o_ssd': nrm(ks[18], (DEPTH, SSD_D_INNER, D_MODEL), SSD_D_INNER ** -0.5),
        'ml_i_bias': nrm(ks[19], (DEPTH, N_DIR, ML_HEADS), 0.1),
        'ml_f_bias': 3.0 + nrm(ks[20], (DEPTH, N_DIR, ML_HEADS), 0.5),
        'ml_norm': gain(ks[21], (DEPTH, ML_V_WIDTH)),
        'w_o_ml': nrm(ks[22], (DEPTH, ML_V_WIDTH, D_MODEL), ML_V_WIDTH ** -0.5),
        'w_out': nrm(ks[23], (DEPTH, D_MODEL, D_MODEL), D_MODEL ** -0.5),
        'norm_ffn': gain(ks[24], (DEPTH, D_MODEL)),
        'w_up': nrm(ks[25], (DEPTH, D_MODEL, 2 * D_FF), D_MODEL ** -0.5),
        'ffn_conv_w': nrm(ks[26], (DEPTH, FFN_CONV, FFN_CONV, D_FF), 1.0 / FFN_CONV),
        'ffn_conv_b': nrm(ks[27], (DEPTH, D_FF), 0.02),
        'w_down': nrm(ks[28], (DEPTH, D_FF, D_MODEL), D_FF ** -0.5),
        'final_norm': gain(ks[29], (D_MODEL,)),
    }

def reference(x_prompt, x_sample, state_ssd, state_mlstm_C, state_mlstm_n, state_mlstm_m, c, c_ctx,
              w_ada, b_ada, norm_mix, w_in, ssd_conv_w, ssd_conv_b, ssd_dt_bias, ssd_a_log, ssd_d,
              ssd_norm, w_o_ssd, ml_i_bias, ml_f_bias, ml_norm, w_o_ml, w_out, norm_ffn, w_up,
              ffn_conv_w, ffn_conv_b, w_down, final_norm):
    dtype = x_prompt.dtype
    nb = x_prompt.shape[0]
    zero_states = (jnp.zeros((nb, N_DIR, SSD_HEADS, SSD_HEADDIM, SSD_STATE), dtype),
                   jnp.zeros((nb, N_DIR, ML_HEADS, ML_DV, ML_DK), dtype),
                   jnp.zeros((nb, N_DIR, ML_HEADS, ML_DK), dtype),
                   jnp.zeros((nb, N_DIR, ML_HEADS), dtype))
    ctx_cond = jax.nn.silu(c_ctx)[None, None, :]
    lat_cond = jax.nn.silu(c)[:, None, :]
    h_ctx = x_prompt
    h_lat = x_sample
    ssd_list, C_list, n_list, m_list = [], [], [], []
    for layer in range(DEPTH):
        lp = {
            'norm_mix': norm_mix[layer], 'w_in': w_in[layer],
            'ssd_conv_w': ssd_conv_w[layer], 'ssd_conv_b': ssd_conv_b[layer],
            'ssd_dt_bias': ssd_dt_bias[layer], 'ssd_a_log': ssd_a_log[layer], 'ssd_d': ssd_d[layer],
            'ssd_norm': ssd_norm[layer], 'w_o_ssd': w_o_ssd[layer],
            'ml_i_bias': ml_i_bias[layer], 'ml_f_bias': ml_f_bias[layer], 'ml_norm': ml_norm[layer],
            'w_o_ml': w_o_ml[layer], 'w_out': w_out[layer], 'norm_ffn': norm_ffn[layer],
            'w_up': w_up[layer], 'ffn_conv_w': ffn_conv_w[layer], 'ffn_conv_b': ffn_conv_b[layer],
            'w_down': w_down[layer],
        }
        mod_ctx = ctx_cond @ w_ada[layer] + b_ada[layer]
        mod_lat = lat_cond @ w_ada[layer] + b_ada[layer]
        h_ctx, st = trunk_layer(h_ctx, mod_ctx, lp, zero_states, False)
        ssd_list.append(st[0])
        C_list.append(st[1])
        n_list.append(st[2])
        m_list.append(st[3])
        cached = (state_ssd[:, layer], state_mlstm_C[:, layer], state_mlstm_n[:, layer], state_mlstm_m[:, layer])
        h_lat, _ = trunk_layer(h_lat, mod_lat, lp, cached, True)
    y_prompt = rmsnorm(h_ctx, final_norm)
    y_sample = rmsnorm(h_lat, final_norm)
    new_state_ssd = jnp.stack(ssd_list, axis=1).astype(dtype)
    new_state_mlstm_C = jnp.stack(C_list, axis=1).astype(dtype)
    new_state_mlstm_n = jnp.stack(n_list, axis=1).astype(dtype)
    new_state_mlstm_m = jnp.stack(m_list, axis=1).astype(dtype)
    return (y_prompt, y_sample, new_state_ssd, new_state_mlstm_C, new_state_mlstm_n, new_state_mlstm_m)


_drawn_inputs = setup_inputs


def setup_inputs(seed=0):
    import zlib

    import numpy as np

    out = dict(_drawn_inputs(seed))
    spreads = {}
    factors = {'state_mlstm_C': 8.0,
     'state_mlstm_n': 8.0,
     'state_mlstm_m': 8.0,
     'ssd_d': 8.0,
     'ssd_norm': 3.84,
     'ml_norm': 5.835,
     'ffn_conv_b': 7.472,
     'norm_ffn': 3.165}
    for name, (base, spread) in spreads.items():
        noise = np.random.default_rng([zlib.crc32(name.encode()), seed]).standard_normal(out[name].shape)
        drawn = base * np.exp(spread * noise) if base else spread * noise
        out[name] = jnp.asarray(drawn.astype(out[name].dtype))
    for name, factor in factors.items():
        out[name] = (out[name] * factor).astype(out[name].dtype)
    return out
```

```python
from contextlib import ExitStack

import numpy as np

import concourse.bass as bass
from concourse import mybir

F32 = mybir.dt.float32
F32R = mybir.dt.float32r
BF16 = mybir.dt.bfloat16
ACT = mybir.ActivationFunctionType
ALU = mybir.AluOpType
AX = mybir.AxisListType

P = 128
D = 1024
KD = D // P
CTX = 128
LAT = 1024
T = CTX + LAT
C = 128
NC = T // C
EPS = 1e-6
SH, SP, SG, SN = 16, 64, 4, 64
HG = SH // SG
MH, DV, DK = 8, 128, 64
DV1 = DV + 1
XBC = 1536
XT = XBC // P
FF = 2816
FT = FF // P
GRID_W = 64
ROWS = LAT // GRID_W
NEG = -1.0e30
TB = 384
BLOCKS = tuple((b, b * TB, TB) for b in range(T // TB))
PARTS = ((0, slice(0, CTX), lambda x: x[:, 0, 0:CTX]),
         (1, slice(CTX, TB), lambda x: x[:, 0, CTX:TB]),
         (1, slice(TB, T), lambda x: x[:, 1:3, :]))

PC = {}
_at = 0
for _n, _w in (("norm_mix", KD), ("b_ada", 48), ("norm_ffn", KD), ("ssd_norm", KD), ("ml_norm", KD),
               ("conv_b", XT), ("conv_w", 3 * XT), ("ffn_b", FT), ("ffn_w", 9 * FT), ("final_norm", KD),
               ("gate_bias", 1), ("i_bias", 1), ("a_log", 1), ("m0", 1)):
    PC[_n] = _at
    _at += _w
NPAR = _at

CC = {}
_at = 0
for _n, _w in (("ident", P), ("le", P), ("gt", P), ("ge", P), ("lt", P), ("ones", P), ("row127", P),
               ("row0", P), ("sign", 1), ("fwd", 1), ("bwd", 1), ("eps", 1), ("half0", 1), ("half1", 1), ("i16", 16)):
    CC[_n] = _at
    _at += _w
NCON = _at

TA, TI, TX, TQ, TK, TG = 0, 1, 2, 14, 18, 22
NT = 38


def build(nc, a, o):
    scr = {
        "xbc": nc.dram_tensor("scr_xbc", [XT, P, T], F32).ap(),
        "qk": nc.dram_tensor("scr_qk", [8, P, T], F32).ap(),
        "gate": nc.dram_tensor("scr_gate", [16, P, T], F32).ap(),
        "zvo": nc.dram_tensor("scr_zvo", [3, NC, P, D], F32).ap(),
        "yn": nc.dram_tensor("scr_yn", [P, KD, T], F32).ap(),
        "hm": nc.dram_tensor("scr_hm", [P, KD, T], F32).ap(),
    }
    with ExitStack() as ctx:
        o = {**o, **{f"{n}_out": nc.alloc_semaphore(f"{n}_out") for n in ("ssd", "ml", "m", "y0", "y1")}}
        par = ctx.enter_context(nc.sbuf_tensor("par", [P, NPAR], F32))
        mod = ctx.enter_context(nc.sbuf_tensor("mod", [P, 48, 2], F32))
        k = {"par": par, "mod": mod}
        with ExitStack() as mix:
            k["con"] = mix.enter_context(nc.sbuf_tensor("con", [P, NCON], F32))
            g = {n: mix.enter_context(nc.sbuf_tensor(n, [P, NC, w], F32)) for n, w in
                 (("dt_ig", 48), ("dec", 48), ("ecum", 48), ("eend", 48), ("em", 16), ("dbc", 48))}
            g["negm"] = mix.enter_context(nc.sbuf_tensor("negm", [48, T], F32))
            with ExitStack() as pro:
                rows = {n: pro.enter_context(nc.sbuf_tensor(n, [48, T], F32)) for n in ("row_a", "row_b")}
                with ExitStack() as proj:
                    cond = proj.enter_context(nc.sbuf_tensor("cond", [P, KD, 2], F32))
                    uh = proj.enter_context(nc.sbuf_tensor("uh", [P, KD, T], F32R))
                    ul = proj.enter_context(nc.sbuf_tensor("ul", [P, KD, T], F32R))
                    norm_mix(nc, a, k, cond, uh, ul)
                    proj_ch(nc, a, k, cond, uh, ul, rows, scr)
                    proj_tok(nc, a, uh, ul, scr)
                gates(nc, k, rows, g, o)
            ssd(nc, a, k, g, scr, o)
            mlstm(nc, a, k, g, scr, o)
        h = ctx.enter_context(nc.sbuf_tensor("h", [P, KD, T], F32))
        with ExitStack() as ff:
            uh = ff.enter_context(nc.sbuf_tensor("uh2", [P, KD, T], F32R))
            ul = ff.enter_context(nc.sbuf_tensor("ul2", [P, KD, T], F32R))
            out_proj(nc, a, k, h, uh, ul, scr)
            norm_ffn(nc, a, k, h, uh, ul)
            ffn(nc, a, k, h, uh, ul)
        final_norm(nc, a, k, h, o)


def col(k, name, i=0, n=1, rows=slice(0, P)):
    return k["par"][rows, PC[name] + i:PC[name] + i + n]


def const(k, name, rows=slice(0, P), n=None):
    n = n or (P if CC[name] < 8 * P else 1)
    return k["con"][rows, CC[name]:CC[name] + n]


class Chain:

    def __init__(self, eng, sem):
        self.eng, self.sem, self.n = eng, sem, 0

    def __call__(self, ins):
        self.n += 1
        ins.then_inc(self.sem, 1)
        self.eng.wait_ge(self.sem, self.n)


def open_sems(nc, ctx, *names):
    sems = [nc.alloc_semaphore(n) for n in names]
    ctx.callback(clear_sems, nc, sems)
    return sems


def clear_sems(nc, sems):
    nc.clear_and_free_semaphores(sems)
    nc.all_engine_barrier()


def spread(x, shape):
    return x.to_broadcast(shape)


def blocks(x):
    return x.rearrange("p (b n) -> p b n", n=TB)


def part(x, t):
    x = x[:, t]
    return blocks(x) if t.stop == T else x


def split_product(pe, acc, wh, wl, ah, al, kt, last_k, first=True):
    ins = None
    for w, act, s, e in ((wh, ah, True, False), (wh, al, False, False), (wl, ah, False, True)):
        for bank, t0, n in BLOCKS:
            ins = pe.matmul(acc[:, bank, 0:n], w, act[:, kt, t0:t0 + n],
                            start=(first and s), stop=(last_k and e))
    return ins


def norm_mix(nc, a, k, cond, uh, ul):
    with ExitStack() as ctx:
        RING = 4
        x = ctx.enter_context(nc.sbuf_tensor("x", [P, KD, T], F32))
        wa = ctx.enter_context(nc.sbuf_tensor("wa", [P, RING, KD, P], F32))
        sq = ctx.enter_context(nc.sbuf_tensor("sq", [P, 2, T], F32))
        xn = ctx.enter_context(nc.sbuf_tensor("xn", [P, 2, T], F32))
        u = ctx.enter_context(nc.sbuf_tensor("u", [P, 2, T], F32))
        rstd = ctx.enter_context(nc.sbuf_tensor("rstd", [P, T], F32))
        scl = ctx.enter_context(nc.sbuf_tensor("scl", [P, KD, 2], F32))
        craw = ctx.enter_context(nc.sbuf_tensor("craw", [P, KD, 2], F32))
        ss_bank = ctx.enter_context(nc.psum_tensor("ss", [P, 3, 512], F32))
        ss = ss_bank[:, :, 0:TB]
        pmod = ctx.enter_context(nc.psum_tensor("pmod", [P, 48, 2], F32))
        (par_in, con_in, cond_in, sq_ready, sq_used, ss_done, root, rstd_ready, mod_done, cond_ready,
         scl_ready, xn_ready, u_ready, hi_done, lo_done, chain) = open_sems(
            nc, ctx, "par_in", "con_in", "cond_in", "sq_ready", "sq_used", "ss_done", "root", "rstd_ready",
            "mod_done", "cond_ready", "scl_ready", "xn_ready", "u_ready", "hi_done", "lo_done", "chain_nm")
        x_in = open_sems(nc, ctx, *[f"x_in{i}" for i in range(KD)])
        wa_in = open_sems(nc, ctx, *[f"wa_in{i}" for i in range(RING)])
        mod_used, = open_sems(nc, ctx, "mod_used")
        block = ctx.enter_context(nc.Block())
        NA = 16

        @block.sync
        def _(sp):
            sp.dma_start(craw[:, :, :], a["cond"]).then_inc(cond_in, 16)
            sp.dma_start(k["con"][:, :], a["consts"]).then_inc(con_in, 16)
            sp.dma_start(k["par"][:, :], a["params"]).then_inc(par_in, 16)
            for i in range(KD):
                sp.dma_start(x[:, i, :], a["xT"][:, i, :]).then_inc(x_in[i], 16)
            for j in range(NA):
                if j >= RING:
                    sp.wait_ge(mod_done, j - RING + 1)
                sp.dma_start(wa[:, j % RING, :, :], a["w_ada"][j]).then_inc(wa_in[j % RING], 16)

        @block.scalar
        def _(act):
            act.wait_ge(cond_in, 16)
            act.activation(cond[:, :, :], craw[:, :, :], ACT.Silu).then_inc(cond_ready, 1)
            for i in range(KD):
                act.wait_ge(x_in[i], 16)
                if i >= 2:
                    act.wait_ge(sq_used, i - 1)
                act.activation(sq[:, i % 2, :], x[:, i, :], ACT.Square).then_inc(sq_ready, 1)
            act.wait_ge(ss_done, 1)
            act.wait_ge(con_in, 16)
            act.activation(blocks(rstd[:, :]), ss, ACT.Sqrt, bias=const(k, "eps"), scale=1.0 / D).then_inc(root, 1)
            act.wait_ge(scl_ready, 2)
            for i in range(KD):
                act.wait_ge(xn_ready, i + 1)
                if i >= 2:
                    act.wait_ge(lo_done, i - 1)
                for s, (t0, t1) in enumerate(((0, CTX), (CTX, T))):
                    act.activation(u[:, i % 2, t0:t1], xn[:, i % 2, t0:t1], ACT.Identity,
                                   bias=k["mod"][:, i, s:s + 1], scale=scl[:, i, s:s + 1]).then_inc(u_ready, 1)
                act.wait_ge(u_ready, 2 * i + 2)
                act.activation(uh[:, i, :], u[:, i % 2, :], ACT.Copy).then_inc(hi_done, 1)

        @block.tensor
        def _(pe):
            pe.wait_ge(con_in, 16)
            for i in range(KD):
                pe.wait_ge(sq_ready, i + 1)
                for bank, t0, n in BLOCKS:
                    m = pe.matmul(ss[:, bank, 0:n], const(k, "ones"), sq[:, i % 2, t0:t0 + n],
                                  start=(i == 0), stop=(i == KD - 1))
                m.then_inc(sq_used, 1)
                if i == KD - 1:
                    pe.wait_ge(sq_used, KD)
                    m = pe.matmul(pmod[:, 47, :], const(k, "ones"), k["con"][:, 0:2], start=True, stop=True)
                    m.then_inc(ss_done, 1)
            pe.wait_ge(cond_ready, 1)
            for j in range(NA):
                pe.wait_ge(wa_in[j % RING], 16 * (j // RING + 1))
                for i in range(KD):
                    m = pe.matmul(pmod[:, j, :], wa[:, j % RING, i, :], cond[:, i, :],
                                  start=(i == 0), stop=(i == KD - 1))
                m.then_inc(mod_done, 1)

        @block.vector
        def _(dve):
            link = Chain(dve, chain)
            dve.wait_ge(root, 1)
            dve.reciprocal(rstd[:, :], rstd[:, :]).then_inc(rstd_ready, 1)
            dve.wait_ge(par_in, 16)
            dve.wait_ge(mod_done, NA)
            link(dve.tensor_tensor(k["mod"][:, 0:NA, :], pmod[:, 0:NA, :],
                                   spread(col(k, "b_ada", 0, NA).unsqueeze(2), [P, NA, 2]), ALU.add))
            for s in range(2):
                dve.scalar_tensor_tensor(out=scl[:, :, s], in0=k["mod"][:, KD:2 * KD, s], scalar=1.0,
                                         in1=col(k, "norm_mix", 0, KD), op0=ALU.add,
                                         op1=ALU.mult).then_inc(scl_ready, 1)
            dve.wait_ge(rstd_ready, 1)
            for i in range(KD):
                if i >= 2:
                    dve.wait_ge(u_ready, 2 * (i - 1))
                dve.tensor_tensor(xn[:, i % 2, :], x[:, i, :], rstd[:, :], ALU.mult).then_inc(xn_ready, 1)

        @block.gpsimd
        def _(pool):
            for i in range(KD):
                pool.wait_ge(hi_done, i + 1)
                pool.tensor_tensor(ul[:, i, :], u[:, i % 2, :], uh[:, i, :].bitcast(F32),
                                   ALU.subtract).then_inc(lo_done, 1)
            pool.wait_ge(lo_done, KD)


def proj_ch(nc, a, k, cond, uh, ul, rows, scr):
    with ExitStack() as ctx:
        RING, ORING, PADT = 4, 3, T + 4
        raw = ctx.enter_context(nc.sbuf_tensor("raw", [P, RING, KD, P], F32))
        wh = ctx.enter_context(nc.sbuf_tensor("wh", [P, 2, KD, P], F32R))
        wl = ctx.enter_context(nc.sbuf_tensor("wl", [P, 2, KD, P], F32R))
        pad = ctx.enter_context(nc.sbuf_tensor("pad", [P, 2, PADT], F32))
        cv = ctx.enter_context(nc.sbuf_tensor("cv", [P, 2, PADT], F32))
        ob = ctx.enter_context(nc.sbuf_tensor("ob", [P, ORING, T], F32))
        acc = [ctx.enter_context(nc.psum_tensor(f"acc{i}", [P, 3, 512], F32))[:, :, 0:TB] for i in range(2)]
        pmod = ctx.enter_context(nc.psum_tensor("pmod2", [P, 48, 2], F32))
        (hi_done, lo_done, tile_done, evac_done, mod_done, pad_zero, pad_ready, conv_done, silu_done,
         ob_ready, chain) = open_sems(
            nc, ctx, "w_hi_done", "w_lo_done", "tile_done", "evac_done", "mod2_done", "pad_zero", "pad_ready",
            "conv_done", "silu_done", "ob_ready", "chain_pc")
        raw_in = open_sems(nc, ctx, *[f"raw_in{i}" for i in range(RING)])
        stored = open_sems(nc, ctx, *[f"stored{i}" for i in range(ORING)])
        block = ctx.enter_context(nc.Block())

        jobs = []
        for i in range(NT):
            jobs.append(("w", i))
            if i < 32:
                jobs.append(("ada", 16 + i))
        slot = {job: n for n, job in enumerate(jobs)}
        outs = [i for i in range(NT) if i >= TX]

        def out_slot(i):
            return (i - TX) % ORING, (i - TX) // ORING

        @block.sync
        def _(sp):
            for n, (kind, i) in enumerate(jobs):
                if n >= RING:
                    was, j = jobs[n - RING]
                    if was == "w":
                        sp.wait_ge(hi_done, j + 1)
                        sp.wait_ge(lo_done, j + 1)
                    else:
                        sp.wait_ge(mod_done, j - 15)
                src = a["w_in_ch"][i] if kind == "w" else a["w_ada"][i]
                sp.dma_start(raw[:, n % RING, :, :], src).then_inc(raw_in[n % RING], 16)

        def arrived(eng, job):
            n = slot[job]
            eng.wait_ge(raw_in[n % RING], 16 * (n // RING + 1))
            return raw[:, n % RING, :, :]

        @block.tensor
        def _(pe):
            for kind, i in jobs:
                if kind == "w":
                    pe.wait_ge(hi_done, i + 1)
                    pe.wait_ge(lo_done, i + 1)
                    if i >= 2:
                        pe.wait_ge(evac_done, i - 1)
                    for kt in range(KD):
                        m = split_product(pe, acc[i % 2], wh[:, i % 2, kt, :], wl[:, i % 2, kt, :], uh, ul, kt,
                                          kt == KD - 1, kt == 0)
                    m.then_inc(tile_done, 1)
                else:
                    w = arrived(pe, (kind, i))
                    for kt in range(KD):
                        m = pe.matmul(pmod[:, i, :], w[:, kt, :], cond[:, kt, :], start=(kt == 0),
                                      stop=(kt == KD - 1))
                    m.then_inc(mod_done, 1)

        @block.scalar
        def _(act):
            def high(i):
                w = arrived(act, ("w", i))
                if i >= 2:
                    act.wait_ge(tile_done, i - 1)
                act.activation(wh[:, i % 2, :, :], w, ACT.Copy).then_inc(hi_done, 1)

            def out_free(i):
                s, n = out_slot(i)
                if n:
                    act.wait_ge(stored[s], 16 * n)

            def silu(i):
                act.wait_ge(conv_done, i - TX + 1)
                out_free(i)
                s, _ = out_slot(i)
                b = col(k, "conv_b", i - TX)
                act.activation(ob[:, s, 0:CTX], cv[:, i % 2, 1:1 + CTX], ACT.Silu, bias=b)
                act.activation(ob[:, s, CTX:T], cv[:, i % 2, CTX + 3:T + 3], ACT.Silu,
                               bias=b).then_inc(ob_ready, 1)

            high(0)
            for i in range(NT):
                if i + 1 < NT:
                    high(i + 1)
                act.wait_ge(tile_done, i + 1)
                if i < TX:
                    dst = rows["row_a" if i == TA else "row_b"]
                    act.activation(blocks(dst[:, :]), acc[i % 2][0:48, :, :], ACT.Copy).then_inc(evac_done, 1)
                elif i < TQ:
                    if i == TX:
                        act.wait_ge(pad_zero, 1)
                    if i >= TX + 2:
                        act.wait_ge(conv_done, i - TX - 1)
                    for s, t, view in PARTS:
                        row = pad[:, i % 2, 1 + 2 * s:1 + 2 * s + T]
                        act.activation(part(row, t), view(acc[i % 2]), ACT.Copy).then_inc(pad_ready, 1)
                    act.wait_ge(pad_ready, 3 * (i - TX) + 3)
                    act.sem_inc(evac_done, 1)
                    if i > TX:
                        silu(i - 1)
                else:
                    if i == TQ:
                        silu(i - 1)
                    out_free(i)
                    s, _ = out_slot(i)
                    fn = ACT.Sigmoid if i >= TG else ACT.Copy
                    sc = DK ** -0.5 if i < TK else 1.0
                    act.activation(blocks(ob[:, s, :]), acc[i % 2], fn, scale=sc).then_inc(ob_ready, 1)
                    act.wait_ge(ob_ready, i - TX + 1)
                    act.sem_inc(evac_done, 1)

        @block.vector
        def _(dve):
            link = Chain(dve, chain)
            dve.memset(pad[:, :, :], 0.0).then_inc(pad_zero, 1)

            def low(i):
                w = arrived(dve, ("w", i))
                dve.wait_ge(hi_done, i + 1)
                dve.tensor_tensor(wl[:, i % 2, :, :], w, wh[:, i % 2, :, :].bitcast(F32),
                                  ALU.subtract).then_inc(lo_done, 1)

            def conv(i):
                dve.wait_ge(pad_ready, 3 * (i - TX) + 3)
                if i >= TX + 2:
                    dve.wait_ge(ob_ready, i - TX - 1)
                x, y = pad[:, i % 2, :], cv[:, i % 2, 1:PADT - 1]
                n = PADT - 2
                w = [col(k, "conv_w", 3 * (i - TX) + j) for j in range(3)]
                link(dve.tensor_scalar(y, x[:, 1:1 + n], w[1], None, ALU.mult))
                link(dve.scalar_tensor_tensor(out=y, in0=x[:, 0:n], scalar=w[0], in1=y, op0=ALU.mult, op1=ALU.add))
                dve.scalar_tensor_tensor(out=y, in0=x[:, 2:2 + n], scalar=w[2], in1=y, op0=ALU.mult,
                                         op1=ALU.add).then_inc(conv_done, 1)

            low(0)
            for i in range(NT):
                if i + 1 < NT:
                    low(i + 1)
                if TX <= i < TQ:
                    conv(i)
            dve.wait_ge(mod_done, 32)
            dve.tensor_tensor(k["mod"][:, 16:48, :], pmod[:, 16:48, :],
                              spread(col(k, "b_ada", 16, 32).unsqueeze(2), [P, 32, 2]), ALU.add).then_inc(chain, 1)
            dve.wait_ge(chain, link.n + 1)

        @block.gpsimd
        def _(pool):
            for n, i in enumerate(outs):
                s, _ = out_slot(i)
                pool.wait_ge(ob_ready, n + 1)
                if i < TQ:
                    dst = scr["xbc"][i - TX]
                elif i < TG:
                    dst = scr["qk"][i - TQ]
                else:
                    dst = scr["gate"][i - TG]
                pool.dma_start(dst, ob[:, s, :]).then_inc(stored[s], 16)
            for s in range(ORING):
                pool.wait_ge(stored[s], 16 * len([i for i in outs if out_slot(i)[0] == s]))


def proj_tok(nc, a, uh, ul, scr):
    with ExitStack() as ctx:
        NB, W, OR = 6, 512, 4
        raw = ctx.enter_context(nc.sbuf_tensor("rawn", [P, 2, KD, W], F32))
        wh = ctx.enter_context(nc.sbuf_tensor("whn", [P, 2, KD, W], F32R))
        wl = ctx.enter_context(nc.sbuf_tensor("wln", [P, 2, KD, W], F32R))
        ob = ctx.enter_context(nc.sbuf_tensor("obn", [P, OR, W], F32))
        NP = 8
        acc = ctx.enter_context(nc.psum_tensor("accn", [P, NP, W], F32))
        hi_done, lo_done, blk_done, tok_done, ob_ready = open_sems(
            nc, ctx, "n_hi_done", "n_lo_done", "blk_done", "tok_done", "n_ob_ready")
        raw_in = open_sems(nc, ctx, *[f"n_raw_in{i}" for i in range(2)])
        stored = open_sems(nc, ctx, *[f"n_stored{i}" for i in range(OR)])
        block = ctx.enter_context(nc.Block())
        H = KD // 2

        @block.sync
        def _(sp):
            for b in range(NB):
                if b >= 2:
                    sp.wait_ge(hi_done, 2 * (b - 1))
                    sp.wait_ge(lo_done, 2 * (b - 1))
                sp.dma_start(raw[:, b % 2, :, :], a["w_in_tok"][b]).then_inc(raw_in[b % 2], 16)

        @block.tensor
        def _(pe):
            for b in range(NB):
                for c in range(NC):
                    n = b * NC + c
                    if n >= NP:
                        pe.wait_ge(ob_ready, n - NP + 1)
                    for kt in range(KD):
                        if c == 0 and kt % H == 0:
                            pe.wait_ge(hi_done, 2 * b + kt // H + 1)
                            pe.wait_ge(lo_done, 2 * b + kt // H + 1)
                        for q, (x, w) in enumerate(((uh, wh), (uh, wl), (ul, wh))):
                            m = pe.matmul(acc[:, n % NP, :], x[:, kt, c * C:(c + 1) * C], w[:, b % 2, kt, :],
                                          start=(kt == 0 and q == 0), stop=(kt == KD - 1 and q == 2))
                    m.then_inc(tok_done, 1)

        @block.scalar
        def _(act):
            def high(b):
                act.wait_ge(raw_in[b % 2], 16 * (b // 2 + 1))
                if b >= 2:
                    act.wait_ge(tok_done, NC * (b - 1))
                for j in range(2):
                    act.activation(wh[:, b % 2, j * H:(j + 1) * H, :], raw[:, b % 2, j * H:(j + 1) * H, :],
                                   ACT.Copy).then_inc(hi_done, 1)

            high(0)
            for b in range(NB):
                if b + 1 < NB:
                    high(b + 1)
                fn = (ACT.Silu, ACT.Copy, ACT.Sigmoid)[b // 2]
                for c in range(NC):
                    n = b * NC + c
                    act.wait_ge(tok_done, n + 1)
                    if n >= OR:
                        act.wait_ge(stored[n % OR], 16 * (n // OR))
                    act.activation(ob[:, n % OR, :], acc[:, n % NP, :], fn).then_inc(ob_ready, 1)

        @block.vector
        def _(dve):
            for b in range(NB):
                for j in range(2):
                    dve.wait_ge(hi_done, 2 * b + j + 1)
                    dve.tensor_tensor(wl[:, b % 2, j * H:(j + 1) * H, :], raw[:, b % 2, j * H:(j + 1) * H, :],
                                      wh[:, b % 2, j * H:(j + 1) * H, :].bitcast(F32),
                                      ALU.subtract).then_inc(lo_done, 1)

        @block.gpsimd
        def _(pool):
            for n in range(NB * NC):
                b, c = n // NC, n % NC
                pool.wait_ge(ob_ready, n + 1)
                dst = scr["zvo"][b // 2][c][:, (b % 2) * W:(b % 2 + 1) * W]
                pool.dma_start(dst, ob[:, n % OR, :]).then_inc(stored[n % OR], 16)
            for s in range(OR):
                pool.wait_ge(stored[s], 16 * len(range(s, NB * NC, OR)))


def gates(nc, k, rows, g, o):
    with ExitStack() as ctx:
        ML = slice(32, 48)
        tmp = {n: ctx.enter_context(nc.sbuf_tensor("g_" + n, [48, T], F32)) for n in
               ("x", "e", "u", "l", "sp", "g2", "mf", "mb", "mm", "d", "w")}
        pm = ctx.enter_context(nc.sbuf_tensor("g_pm", [48, 2, NC], F32))
        pp = ctx.enter_context(nc.sbuf_tensor("g_pp", [48, NC], F32))
        mn = ctx.enter_context(nc.sbuf_tensor("g_mn", [48, NC], F32))
        ac = ctx.enter_context(nc.sbuf_tensor("g_ac", [48, 1], F32))
        end = ctx.enter_context(nc.sbuf_tensor("g_end", [P, NC, 48], F32))
        ps = {n: ctx.enter_context(nc.psum_tensor("pg_" + n, [P, 512], F32)) for n in
              ("t1", "t2", "cum", "end", "m", "dbc")}
        v = {n: p[:, 0:NC * 48].rearrange("p (c r) -> p c r", c=NC) for n, p in ps.items()}
        v["m"] = ps["m"][:, 0:NC * 16].rearrange("p (c r) -> p c r", c=NC)
        chain, act_c, ex, u1, ln, a_exp, rows_done, tok_t, tok_c, cums, ecs, dbcs = open_sems(
            nc, ctx, "chain_g", "chain_ga", "g_exp", "g_u1", "g_ln", "g_aexp", "rows_done", "tok_t", "tok_c", "cums", "ecs",
            "dbcs")
        block = ctx.enter_context(nc.Block())
        idn = const(k, "ident", slice(0, 48), 48)

        @block.scalar
        def _(act):
            act.activation(ac[0:32, :], col(k, "a_log", rows=slice(0, 32)), ACT.Exp).then_inc(a_exp, 1)
            act.wait_ge(ex, 1)
            act.activation(tmp["e"][:, :], tmp["e"][:, :], ACT.Exp, scale=-1.0).then_inc(u1, 1)
            act.wait_ge(ln, 1)
            act.activation(tmp["l"][:, :], tmp["u"][:, :], ACT.Ln).then_inc(ln, 1)
            act.wait_ge(cums, 1)
            act.activation(g["ecum"][:, :, :], v["cum"], ACT.Exp).then_inc(ecs, 1)
            act.activation(end[:, :, :], v["end"], ACT.Exp).then_inc(ecs, 1)
            act.activation(g["em"][:, :, :], v["m"], ACT.Exp).then_inc(ecs, 1)

        @block.vector
        def _(dve):
            link = Chain(dve, chain)
            X, E, U, L, SPR, G2 = (tmp[n][:, :] for n in ("x", "e", "u", "l", "sp", "g2"))
            sgn = const(k, "sign", slice(0, 48))
            dve.memset(pm[:, :, :], 0.0)
            link(dve.tensor_scalar(X, rows["row_a"][:, :], col(k, "gate_bias", rows=slice(0, 48)), sgn,
                                   ALU.add, ALU.mult))
            dve.scalar_tensor_tensor(out=E, in0=X, scalar=-1.0, in1=X, op0=ALU.mult, op1=ALU.max).then_inc(ex, 1)
            dve.wait_ge(u1, 1)
            dve.tensor_scalar(U, E, 1.0, None, ALU.add).then_inc(ln, 1)
            dve.wait_ge(ln, 2)
            link(dve.scalar_tensor_tensor(out=SPR, in0=U, scalar=-1.0, in1=E, op0=ALU.add, op1=ALU.subtract))
            link(dve.reciprocal(U, U))
            link(dve.tensor_tensor(SPR, SPR, U, ALU.mult))
            link(dve.tensor_tensor(SPR, L, SPR, ALU.subtract))
            link(dve.scalar_tensor_tensor(out=SPR, in0=X, scalar=0.0, in1=SPR, op0=ALU.max, op1=ALU.add))
            dve.wait_ge(a_exp, 1)
            link(dve.tensor_scalar(G2[0:32, :], SPR[0:32, :], ac[0:32, :], -1.0, ALU.mult, ALU.mult))
            link(dve.tensor_scalar(G2[ML, :], SPR[ML, :], -1.0, None, ALU.mult))
            link(dve.tensor_scalar(SPR[ML, :], rows["row_b"][ML, :], col(k, "i_bias", rows=ML), None, ALU.add))
            ig, lf = SPR[ML, :], G2[ML, :]
            MF, MB = tmp["mf"][ML, :], tmp["mb"][ML, :]
            m0 = col(k, "m0", rows=ML)
            for dst, st in ((MF, 1), (MB, -1)):
                for t0, t1, init in ((0, CTX, 0.0), (CTX, T, m0)):
                    link(dve.tensor_tensor_scan(dst[:, t0:t1][:, ::st], lf[:, t0:t1][:, ::st],
                                                ig[:, t0:t1][:, ::st], init, ALU.add, ALU.max))
            fw, bw = const(k, "fwd", ML), const(k, "bwd", ML)
            link(dve.tensor_copy(pm[ML, 0, 1:2], m0))
            link(dve.tensor_copy(pm[ML, 1, NC - 1:NC], m0))
            link(dve.tensor_copy(pm[ML, 0, 2:NC], MF[:, 2 * C - 1:T - C:C]))
            link(dve.tensor_copy(pm[ML, 1, 1:NC - 1], MB[:, 2 * C:T:C]))

            def by_direction(dst, f, b):
                link(dve.tensor_scalar(dst, f, fw, None, ALU.mult))
                link(dve.scalar_tensor_tensor(out=dst, in0=b, scalar=bw, in1=dst, op0=ALU.mult, op1=ALU.add))

            MM = tmp["mm"][ML, :]
            by_direction(MM, MF, MB)
            by_direction(pp[ML, :], pm[ML, 0, :], pm[ML, 1, :])
            by_direction(mn[ML, :], MF[:, C - 1:T:C], MB[:, 0:T:C])
            cs = [16, NC, C]
            link(dve.tensor_tensor(tmp["d"][ML, :].rearrange("p (c t) -> p c t", c=NC),
                                   spread(pp[ML, :].unsqueeze(2), cs),
                                   MM.rearrange("p (c t) -> p c t", c=NC), ALU.subtract))
            link(dve.tensor_tensor(tmp["w"][ML, :].rearrange("p (c t) -> p c t", c=NC),
                                   ig.rearrange("p (c t) -> p c t", c=NC),
                                   spread(mn[ML, :].unsqueeze(2), cs), ALU.subtract))
            dve.tensor_scalar(g["negm"][ML, :], MM, -1.0, None, ALU.mult).then_inc(rows_done, 1)
            dve.wait_ge(tok_t, 1)
            dve.tensor_copy(g["dt_ig"][:, :, :], v["t1"]).then_inc(tok_c, 1)
            dve.tensor_copy(g["dec"][:, :, :], v["t2"]).then_inc(tok_c, 1)
            dve.wait_ge(tok_c, 2)
            dve.wait_ge(ecs, 3)
            dve.tensor_copy(g["eend"][:, :, 32:48], end[:, :, 32:48]).then_inc(dbcs, 1)
            dve.tensor_tensor(g["eend"][:, :, 0:32], end[:, :, 0:32], g["dt_ig"][:, :, 0:32],
                              ALU.mult).then_inc(dbcs, 1)
            dve.wait_ge(dbcs, 3)
            dve.tensor_copy(g["dbc"][:, :, :], v["dbc"]).then_inc(dbcs, 1)
            dve.wait_ge(dbcs, 4)

        @block.tensor
        def _(pe):
            pe.wait_ge(rows_done, 1)
            for c in range(NC):
                t = slice(c * C, (c + 1) * C)
                pe.transpose(v["t1"][:, c, :], tmp["sp"][:, t], idn)
                pe.transpose(v["t2"][:, c, :], tmp["g2"][:, t], idn)
                m = pe.transpose(v["m"][:, c, :], g["negm"][ML, t], k["con"][ML, CC["i16"]:CC["i16"] + 16])
            m.then_inc(tok_t, 1)
            pe.wait_ge(tok_c, 2)
            dec, i16 = g["dec"], k["con"][ML, CC["i16"]:CC["i16"] + 16]
            for out, masks, own in (("cum", ("le", "ge"), "d"), ("end", ("gt", "lt"), "w")):
                first = True
                for cols, mask in ((slice(0, 16), masks[0]), (slice(16, 32), masks[1]),
                                   (slice(32, 40), masks[0]), (slice(40, 48), masks[1])):
                    pe.matmul(v[out][:, :, cols], const(k, mask), dec[:, :, cols], start=first, stop=False,
                              skip_group_check=True)
                    first = False
                for c in range(NC):
                    m = pe.matmul(v[out][:, c, 32:48], tmp[own][ML, c * C:(c + 1) * C], i16, start=False,
                                  stop=(c == NC - 1), skip_group_check=True)
            m.then_inc(cums, 1)
            pe.wait_ge(ecs, 3)
            first = True
            for cols, row in ((slice(0, 16), "row127"), (slice(16, 32), "row0"), (slice(32, 40), "row127"),
                              (slice(40, 48), "row0")):
                m = pe.matmul(v["dbc"][:, :, cols], const(k, row), g["ecum"][:, :, cols], start=first,
                              stop=(cols.start == 40), skip_group_check=True)
                first = False
            m.then_inc(dbcs, 1)

        @block.sync
        def _(sp):
            sp.wait_ge(rows_done, 1)
            with nc.allow_non_contiguous_dma(reason="eight single values"):
                sp.dma_start(o["m"][0:8, :], tmp["mf"][32:40, CTX - 1:CTX]).then_inc(o["m_out"], 16)
                sp.dma_start(o["m"][8:16, :], tmp["mb"][40:48, 0:1]).then_inc(o["m_out"], 16)
            sp.wait_ge(o["m_out"], 32)


def head_decay(g, d, c, gp):
    r = slice(64 * gp, 64 * gp + 64)
    v = g["dbc"][r, c, d * SH:(d + 1) * SH].rearrange("p (a b h) -> p a b h", a=2, b=2)[:, :, gp, :]
    return spread(v.unsqueeze(3), [64, 2, HG, SP])


def state_view(s, gp):
    return s[64 * gp:64 * gp + 64, :].rearrange("p (a h x) -> p a h x", a=2, h=HG)


def ssd(nc, a, k, g, scr, o):
    with ExitStack() as ctx:
        x = ctx.enter_context(nc.sbuf_tensor("x_tok", [P, NC, D], F32))
        b = ctx.enter_context(nc.sbuf_tensor("b_tok", [P, NC, SG * SN], F32))
        snap = ctx.enter_context(nc.sbuf_tensor("snap", [P, NC - 1, 512], F32))
        ssd_backward(nc, a, k, g, scr, o, x, b, snap)
        ssd_forward(nc, a, k, g, scr, x, b, snap)


def ssd_backward(nc, a, k, g, scr, o, x, b, snap):
    with ExitStack() as ctx:
        xc = ctx.enter_context(nc.sbuf_tensor("xc", [P, 2, 10, C], F32))
        xw = ctx.enter_context(nc.sbuf_tensor("xw", [P, 2, D], F32))
        fin = ctx.enter_context(nc.sbuf_tensor("fin", [P, 2, 512], F32))
        tr = [ctx.enter_context(nc.psum_tensor(f"tr{i}", [P, 3, 512], F32)) for i in range(2)]
        st = ctx.enter_context(nc.psum_tensor("st", [P, 2, 512], F32))
        tr_done, x_tok, b_tok, xw_ready, st_done, st_used, s0_in, chain = open_sems(
            nc, ctx, "tr_done", "x_tokd", "b_tokd", "xw_ready", "st_done", "st_used", "s0_in", "chain_sb")
        xc_in = open_sems(nc, ctx, "xc_in0", "xc_in1")
        block = ctx.enter_context(nc.Block())
        order = [0] + list(range(NC - 1, 0, -1))
        jobs = [(0, 0), (0, 1)] + [(c, 1) for c in range(NC - 1, 1, -1)]
        at = {c: n for n, c in enumerate(order)}

        @block.sync
        def _(sp):
            sp.dma_start(snap[:, NC - 2, :], a["s_ssd"][:, 1, :]).then_inc(s0_in, 16)
            for n, c in enumerate(order):
                if n >= 2:
                    sp.wait_ge(tr_done, n - 1)
                sp.dma_start(xc[:, n % 2, :, :],
                             scr["xbc"][0:10, :, c * C:(c + 1) * C].rearrange("i p t -> p i t")
                             ).then_inc(xc_in[n % 2], 16)
            sp.wait_ge(st_used, 2)
            sp.dma_start(o["ssd"], fin[:, :, :]).then_inc(o["ssd_out"], 16)
            sp.wait_ge(o["ssd_out"], 16)

        @block.tensor
        def _(pe):
            def turn(n):
                pe.wait_ge(xc_in[n % 2], 16 * (n // 2 + 1))
                if n >= 2:
                    pe.wait_ge(x_tok, n - 1)
                    pe.wait_ge(b_tok, n - 1)
                for i in range(10):
                    m = pe.transpose(tr[n % 2][:, i // 4, (i % 4) * P:(i % 4 + 1) * P], xc[:, n % 2, i, :],
                                     const(k, "ident"))
                m.then_inc(tr_done, 1)

            def state(n):
                c, d = jobs[n]
                pe.wait_ge(xw_ready, n + 1)
                pe.wait_ge(b_tok, at[c] + 1)
                if n >= 2:
                    pe.wait_ge(st_used, n - 1)
                for q in range(SG):
                    m = pe.matmul(st[64 * (q % 2):64 * (q % 2) + 64, n % 2, 256 * (q // 2):256 * (q // 2) + 256],
                                  b[:, c, q * SN:(q + 1) * SN], xw[:, n % 2, q * 256:(q + 1) * 256],
                                  start=True, stop=True, skip_group_check=True)
                m.then_inc(st_done, 1)

            turn(0)
            turn(1)
            state(0)
            state(1)
            for n in range(2, NC):
                turn(n)
                state(n)

        @block.scalar
        def _(act):
            for n, c in enumerate(order):
                act.wait_ge(tr_done, n + 1)
                act.activation(x[:, c, :].rearrange("p (b n) -> p b n", b=2), tr[n % 2][:, 0:2, :],
                               ACT.Copy).then_inc(x_tok, 1)

        @block.gpsimd
        def _(pool):
            for n, (c, d) in enumerate(jobs):
                pool.wait_ge(x_tok, at[c] + 1)
                if n >= 2:
                    pool.wait_ge(st_done, n - 1)
                w = spread(g["eend"][:, c, d * SH:(d + 1) * SH].unsqueeze(2), [P, SH, SP])
                pool.tensor_tensor(xw[:, n % 2, :].rearrange("p (h x) -> p h x", h=SH),
                                   x[:, c, :].rearrange("p (h x) -> p h x", h=SH), w,
                                   ALU.mult).then_inc(xw_ready, 1)

        @block.vector
        def _(dve):
            link = Chain(dve, chain)
            dve.wait_ge(s0_in, 16)

            def b_copy(n):
                dve.wait_ge(tr_done, n + 1)
                dve.tensor_copy(b[:, order[n], :], tr[n % 2][:, 2, 0:256]).then_inc(b_tok, 1)

            b_copy(0)
            b_copy(1)
            for n, (c, d) in enumerate(jobs):
                if n + 2 < NC:
                    b_copy(n + 2)
                dve.wait_ge(st_done, n + 1)
                if c == 0:
                    dve.tensor_copy(fin[:, d, :], st[:, n % 2, :]).then_inc(st_used, 1)
                else:
                    for gp in range(2):
                        link(dve.tensor_tensor(state_view(snap[:, c - 2, :], gp), state_view(snap[:, c - 1, :], gp),
                                               head_decay(g, 1, c, gp), ALU.mult))
                    dve.tensor_tensor(snap[:, c - 2, :], snap[:, c - 2, :], st[:, n % 2, :],
                                      ALU.add).then_inc(st_used, 1)
                    dve.wait_ge(st_used, n + 1)


def ssd_forward(nc, a, k, g, scr, x, b, snap):
    with ExitStack() as ctx:
        U = NC * SG
        bc = ctx.enter_context(nc.sbuf_tensor("bc", [P, 2, 4, C], F32))
        cm = ctx.enter_context(nc.sbuf_tensor("cm", [P, 2, 2, 2, C], F32))
        z = ctx.enter_context(nc.sbuf_tensor("z", [P, 2, D], F32))
        rm = ctx.enter_context(nc.sbuf_tensor("rm", [P, 2, 2, HG, C], F32))
        dtm = ctx.enter_context(nc.sbuf_tensor("dtm", [P, 2, HG, C], F32))
        dtt = ctx.enter_context(nc.sbuf_tensor("dtt", [P, HG, C], F32))
        e = ctx.enter_context(nc.sbuf_tensor("e", [P, 2, HG, C], F32))
        wm = ctx.enter_context(nc.sbuf_tensor("wm", [P, 2, HG, C], F32))
        dful = ctx.enter_context(nc.sbuf_tensor("dful", [P, D], F32))
        xd = ctx.enter_context(nc.sbuf_tensor("xd", [P, 2, 512], F32))
        xw = ctx.enter_context(nc.sbuf_tensor("xwf", [P, D], F32))
        t1 = ctx.enter_context(nc.sbuf_tensor("t1", [P, 2, 512], F32))
        t2 = ctx.enter_context(nc.sbuf_tensor("t2", [P, 512], F32))
        yz = ctx.enter_context(nc.sbuf_tensor("yz", [P, 2, D], F32))
        sqb = ctx.enter_context(nc.sbuf_tensor("sqb", [P, D], F32))
        ss = ctx.enter_context(nc.sbuf_tensor("ss_y", [P, NC], F32))
        rs = ctx.enter_context(nc.sbuf_tensor("rs_y", [P, NC], F32))
        sf = ctx.enter_context(nc.sbuf_tensor("sf", [P, 2, 512], F32))
        yo = ctx.enter_context(nc.sbuf_tensor("yo", [P, 2, KD, C], F32))
        arg = ctx.enter_context(nc.psum_tensor("arg", [P, 2, HG, C], F32))
        sc = ctx.enter_context(nc.psum_tensor("sc", [P, SG, C], F32))
        misc = ctx.enter_context(nc.psum_tensor("misc", [P, 512], F32))
        fb = ctx.enter_context(nc.psum_tensor("fb", [P, 2, 512], F32))
        yd = ctx.enter_context(nc.psum_tensor("yd", [P, 2, 512], F32))
        (rm_ready, dt_ready, arg_done, exp_done, sc_done, wm_done, fb_done, fb_used, y_done, y_used, xd_ready,
         xw_ready, sf_done, yz_done, ss_done, rs_done, yn_done, misc_done, misc_used, s0_in, d_in, yo_ready,
         chain, act_c, pool_c, out_sem) = open_sems(
            nc, ctx, *["f_" + n for n in (
                "rm_ready", "dt_ready", "arg_done", "exp_done", "sc_done", "wm_done", "fb_done", "fb_used",
                "y_done", "y_used", "xd_ready", "xw_ready", "sf_done", "yz_done", "ss_done", "rs_done",
                "yn_done", "misc_done", "misc_used", "s0_in", "d_in", "yo_ready", "chain", "act", "pool", "out")])
        bc_in = open_sems(nc, ctx, "bc_in0", "bc_in1")
        cm_ready, = open_sems(nc, ctx, "cm_ready")
        z_in = open_sems(nc, ctx, "z_in0", "z_in1")
        yo_out = open_sems(nc, ctx, "yo_out0", "yo_out1")
        block = ctx.enter_context(nc.Block())

        uses = []
        for u in range(U + 6):
            c, r = u // SG, u % SG
            if r == 1 and 1 <= c <= NC - 2:
                uses.append(("st", c))
            if r == 3 and 1 <= c <= NC:
                uses.append(("tr0", c - 1))
            if r == 0 and 2 <= c <= NC + 1:
                uses.append(("tr1", c - 2))
        misc_at = {name: n for n, name in enumerate(uses)}

        def store(sp, c):
            sp.wait_ge(yo_ready, 2 * (c + 1))
            sp.dma_start(scr["yn"][:, :, c * C:(c + 1) * C], yo[:, c % 2, :, :]).then_inc(yo_out[c % 2], 16)

        @block.sync
        def _(sp):
            sp.dma_start(sf[:, 1, :], a["s_ssd"][:, 0, :]).then_inc(s0_in, 16)
            sp.dma_start(dful[:, :], a["ssd_d"]).then_inc(d_in, 16)
            for c in range(NC):
                if c >= 2:
                    sp.wait_ge(sc_done, c - 1)
                    sp.wait_ge(cm_ready, 2 * (c - 1))
                sp.dma_start(bc[:, c % 2, :, :],
                             scr["xbc"][8:12, :, c * C:(c + 1) * C].rearrange("i p t -> p i t")
                             ).then_inc(bc_in[c % 2], 16)
                if c >= 2:
                    sp.wait_ge(yz_done, 2 * (c - 1))
                sp.dma_start(z[:, c % 2, :], scr["zvo"][0][c]).then_inc(z_in[c % 2], 16)
                if c >= 3:
                    store(sp, c - 3)
            for c in range(NC - 3, NC):
                store(sp, c)
            for s in range(2):
                sp.wait_ge(yo_out[s], 16 * len(range(s, NC, 2)))

        @block.gpsimd
        def _(pool):
            for u in range(U):
                c, q = u // SG, u % SG
                if u >= 2:
                    pool.wait_ge(arg_done, u - 1)
                hs = [P, HG, C]
                for d, mask in enumerate(("le", "ge")):
                    pool.tensor_tensor(rm[:, u % 2, d, :, :],
                                       spread(g["dec"][:, c, d * SH + q * HG:d * SH + (q + 1) * HG].unsqueeze(2), hs),
                                       spread(const(k, mask).unsqueeze(1), hs), ALU.mult).then_inc(rm_ready, 1)
                if u >= 2:
                    pool.wait_ge(wm_done, u - 1)
                dt = [spread(g["dt_ig"][:, c, d * SH + q * HG:d * SH + (q + 1) * HG].unsqueeze(2), hs)
                      for d in range(2)]
                pool.tensor_tensor(dtm[:, u % 2, :, :], dt[0], spread(const(k, "le").unsqueeze(1), hs), ALU.mult)
                if u:
                    pool.wait_ge(dt_ready, u)
                pool.tensor_tensor(dtt[:, :, :], dt[1], spread(const(k, "ge").unsqueeze(1), hs),
                                   ALU.mult).then_inc(pool_c, 1)
                pool.wait_ge(pool_c, u + 1)
                pool.tensor_tensor(dtm[:, u % 2, :, :], dtm[:, u % 2, :, :], dtt[:, :, :],
                                   ALU.add).then_inc(dt_ready, 1)
                if u % 2 == 1:
                    v = u // 2
                    if v == 0:
                        pool.wait_ge(d_in, 16)
                    if v >= 2:
                        pool.wait_ge(yz_done, v - 1)
                    hf = slice((v % 2) * 512, (v % 2) * 512 + 512)
                    pool.tensor_tensor(xd[:, v % 2, :], x[:, c, hf], dful[:, hf], ALU.mult).then_inc(xd_ready, 1)
                if u % SG == 1 and 1 <= c <= NC - 2:
                    if c >= 2:
                        pool.wait_ge(misc_done, misc_at["st", c - 1] + 1)
                    w = spread(g["eend"][:, c, 0:SH].unsqueeze(2), [P, SH, SP])
                    pool.tensor_tensor(xw[:, :].rearrange("p (h x) -> p h x", h=SH),
                                       x[:, c, :].rearrange("p (h x) -> p h x", h=SH), w,
                                       ALU.mult).then_inc(xw_ready, 1)

        @block.tensor
        def _(pe):
            def shared(name):
                n = misc_at[name]
                if n:
                    pe.wait_ge(misc_used, n)

            for u in range(U + 6):
                c, r = u // SG, u % SG
                if u < U:
                    if r == 0:
                        pe.wait_ge(bc_in[c % 2], 16 * (c // 2 + 1))
                        pe.wait_ge(cm_ready, 2 * (c + 1))
                        if c:
                            pe.wait_ge(wm_done, SG * c)
                        for q in range(SG):
                            m = pe.matmul(sc[:, q, :], bc[:, c % 2, q // 2, :], cm[:, c % 2, q % 2, q // 2, :],
                                          start=True, stop=True)
                        m.then_inc(sc_done, 1)
                    if r % 2 == 0:
                        v = u // 2
                        if v >= 3:
                            pe.wait_ge(fb_used, v - 2)
                        if c == 0:
                            pe.sem_inc(fb_done, 1)
                        else:
                            if c == 1:
                                pe.wait_ge(s0_in, 16)
                            else:
                                pe.wait_ge(sf_done, c - 1)
                            for d in range(2):
                                s = sf[:, c % 2, :] if d == 0 else snap[:, c - 1, :]
                                for gp in range(2):
                                    gh = v % 2
                                    m = pe.matmul(fb[:, d, gp * 256:gp * 256 + 256], cm[:, c % 2, gp, gh, :],
                                                  s[:, gh * 256:gh * 256 + 256], start=True, stop=True,
                                                  skip_group_check=True)
                            m.then_inc(fb_done, 1)
                    pe.wait_ge(rm_ready, 2 * u + 2)
                    if u >= 2:
                        pe.wait_ge(exp_done, u - 1)
                    for d, mask in enumerate(("gt", "lt")):
                        m = pe.matmul(arg[:, u % 2, :, :], const(k, mask), rm[:, u % 2, d, :, :], start=(d == 0),
                                      stop=(d == 1))
                    m.then_inc(arg_done, 1)
                if 1 <= u <= U:
                    w = u - 1
                    cw, q, v = w // SG, w % SG, w // 2
                    pe.wait_ge(wm_done, w + 1)
                    if w % 2 == 0 and v >= 2:
                        pe.wait_ge(y_used, v - 1)
                    for i in range(HG):
                        hd = q * HG + i
                        m = pe.matmul(yd[:, v % 2, (hd % 8) * SP:(hd % 8 + 1) * SP], wm[:, w % 2, i, :],
                                      x[:, cw, hd * SP:(hd + 1) * SP], start=True, stop=True,
                                      skip_group_check=True)
                    m.then_inc(y_done, 1)
                if r == 1 and 1 <= c <= NC - 2:
                    pe.wait_ge(xw_ready, c)
                    shared(("st", c))
                    for q in range(SG):
                        m = pe.matmul(misc[64 * (q % 2):64 * (q % 2) + 64, 256 * (q // 2):256 * (q // 2) + 256],
                                      b[:, c, q * SN:(q + 1) * SN], xw[:, q * 256:(q + 1) * 256], start=True,
                                      stop=True, skip_group_check=True)
                    m.then_inc(misc_done, 1)
                for name, j, r0, back in (("tr0", 0, 3, 1), ("tr1", 1, 0, 2)):
                    if r == r0 and back <= c <= NC - 1 + back:
                        cc = c - back
                        pe.wait_ge(yn_done, cc + 1)
                        shared((name, cc))
                        for i in range(4):
                            m = pe.transpose(misc[:, i * P:(i + 1) * P],
                                             yz[:, cc % 2, (4 * j + i) * P:(4 * j + i + 1) * P], const(k, "ident"))
                        m.then_inc(misc_done, 1)

        @block.scalar
        def _(act):
            link = Chain(act, act_c)

            def one_group(c):
                act.wait_ge(bc_in[c % 2], 16 * (c // 2 + 1))
                if c >= 2:
                    act.wait_ge(sc_done, c - 1)
                    act.wait_ge(fb_done, 2 * (c - 1))
                for half in range(2):
                    act.activation(cm[:, c % 2, half, :, :], bc[:, c % 2, 2:4, :], ACT.Copy,
                                   scale=const(k, f"half{half}")).then_inc(cm_ready, 1)

            one_group(0)
            for u in range(U + 6):
                c, r = u // SG, u % SG
                if r == 2 and c + 1 < NC:
                    one_group(c + 1)
                if u < U:
                    act.wait_ge(arg_done, u + 1)
                    if u >= 2:
                        act.wait_ge(wm_done, u - 1)
                    act.activation(e[:, u % 2, :, :], arg[:, u % 2, :, :], ACT.Exp).then_inc(exp_done, 1)
                if r == 1 and 1 <= c <= NC:
                    cc = c - 1
                    act.wait_ge(yz_done, 2 * cc + 2)
                    link(act.activation(sqb[:, :], yz[:, cc % 2, :], ACT.Square, accum_out=ss[:, cc:cc + 1]))
                    link(act.activation(rs[:, cc:cc + 1], ss[:, cc:cc + 1], ACT.Ln, bias=const(k, "eps"),
                                        scale=1.0 / D))
                    act.activation(rs[:, cc:cc + 1], rs[:, cc:cc + 1], ACT.Exp, scale=-0.5).then_inc(rs_done, 1)

        @block.vector
        def _(dve):
            link = Chain(dve, chain)
            for u in range(U + 6):
                c, r = u // SG, u % SG
                if u < U:
                    if u % 2 == 0 and c >= 1:
                        v = u // 2
                        dve.wait_ge(fb_done, v + 1)
                        hs = [P, 8, SP]
                        for d, dst in ((0, t1[:, v % 2, :]), (1, t2[:, :])):
                            w = spread(g["ecum"][:, c, d * SH + 8 * (v % 2):d * SH + 8 * (v % 2) + 8].unsqueeze(2), hs)
                            ins = dve.tensor_tensor(dst.rearrange("p (h x) -> p h x", h=8),
                                                    fb[:, d, :].rearrange("p (h x) -> p h x", h=8), w, ALU.mult)
                            ins.then_inc(chain, 1)
                            link.n += 1
                        dve.wait_ge(chain, link.n)
                        link(dve.tensor_tensor(t1[:, v % 2, :], t1[:, v % 2, :], t2[:, :], ALU.add))
                        dve.sem_inc(fb_used, 1)
                    dve.wait_ge(exp_done, u + 1)
                    dve.wait_ge(dt_ready, u + 1)
                    if u >= 2:
                        dve.wait_ge(y_done, u - 1)
                    if r == 0:
                        dve.wait_ge(sc_done, c + 1)
                    link(dve.tensor_tensor(wm[:, u % 2, :, :], e[:, u % 2, :, :], dtm[:, u % 2, :, :], ALU.mult))
                    dve.tensor_tensor(wm[:, u % 2, :, :], wm[:, u % 2, :, :],
                                      spread(sc[:, r, :].unsqueeze(1), [P, HG, C]), ALU.mult).then_inc(wm_done, 1)
                if u % 2 == 0 and 2 <= u <= U:
                    v = u // 2 - 1
                    cc, half = v // 2, slice((v % 2) * 512, (v % 2) * 512 + 512)
                    dve.wait_ge(y_done, 2 * v + 2)
                    dve.wait_ge(xd_ready, v + 1)
                    if cc == 0:
                        link(dve.tensor_tensor(t1[:, v % 2, :], xd[:, v % 2, :], yd[:, v % 2, :], ALU.add))
                        dve.sem_inc(y_used, 1)
                    else:
                        link(dve.tensor_tensor(t1[:, v % 2, :], t1[:, v % 2, :], yd[:, v % 2, :], ALU.add))
                        dve.sem_inc(y_used, 1)
                        link(dve.tensor_tensor(t1[:, v % 2, :], t1[:, v % 2, :], xd[:, v % 2, :], ALU.add))
                    dve.wait_ge(z_in[cc % 2], 16 * (cc // 2 + 1))
                    if cc >= 2:
                        dve.wait_ge(misc_done, misc_at["tr1", cc - 2] + 1)
                    dve.tensor_tensor(yz[:, cc % 2, half], t1[:, v % 2, :], z[:, cc % 2, half],
                                      ALU.mult).then_inc(yz_done, 1)
                if r == 2 and 1 <= c <= NC:
                    cc = c - 1
                    dve.wait_ge(rs_done, cc + 1)
                    dve.tensor_scalar(yz[:, cc % 2, :], yz[:, cc % 2, :], rs[:, cc:cc + 1], None,
                                      ALU.mult).then_inc(yn_done, 1)
                if r == 2 and 1 <= c <= NC - 2:
                    if c == 1:
                        dve.wait_ge(s0_in, 16)
                    else:
                        dve.wait_ge(fb_done, 2 * c)
                    for gp in range(2):
                        link(dve.tensor_tensor(state_view(sf[:, (c + 1) % 2, :], gp),
                                               state_view(sf[:, c % 2, :], gp), head_decay(g, 0, c, gp), ALU.mult))
                    dve.wait_ge(misc_done, misc_at["st", c] + 1)
                    dve.tensor_tensor(sf[:, (c + 1) % 2, :], sf[:, (c + 1) % 2, :], misc[:, :],
                                      ALU.add).then_inc(sf_done, 1)
                    dve.wait_ge(sf_done, c)
                    dve.sem_inc(misc_used, 1)
                for name, j, r0 in (("tr0", 0, 0), ("tr1", 1, 1)):
                    if r == r0 and 2 <= c <= NC + 1:
                        cc = c - 2
                        dve.wait_ge(misc_done, misc_at[name, cc] + 1)
                        if cc >= 2:
                            dve.wait_ge(yo_out[cc % 2], 16 * (cc // 2))
                        ins = dve.tensor_tensor(yo[:, cc % 2, 4 * j:4 * j + 4, :],
                                                misc[:, :].rearrange("p (i t) -> p i t", i=4),
                                                spread(col(k, "ssd_norm", 4 * j, 4).unsqueeze(2), [P, 4, C]),
                                                ALU.mult)
                        ins.then_inc(yo_ready, 1)
                        dve.wait_ge(yo_ready, 2 * cc + j + 1)
                        dve.sem_inc(misc_used, 1)


def ml_decay(g, d, c, hp, n, half):
    r = slice(64 * half, 64 * half + 64)
    v = g["dbc"][r, c, 32 + 8 * d:40 + 8 * d].rearrange("p (a b) -> p a b", b=2)[:, hp:hp + n, half]
    return spread(v.unsqueeze(2), [64, n, DV1])


def mlstm(nc, a, k, g, scr, o):
    with ExitStack() as ctx:
        v = ctx.enter_context(nc.sbuf_tensor("v_one", [P, NC, MH, DV1], F32))
        kt = ctx.enter_context(nc.sbuf_tensor("k_tok", [P, NC, MH * DK], F32))
        snap = ctx.enter_context(nc.sbuf_tensor("snap_c", [P, NC - 1, 4, DV1], F32))
        mlstm_backward(nc, a, k, g, scr, o, v, kt, snap)
        mlstm_forward(nc, a, k, g, scr, v, kt, snap)


def mlstm_backward(nc, a, k, g, scr, o, v, kt, snap):
    with ExitStack() as ctx:
        kc = ctx.enter_context(nc.sbuf_tensor("kc", [P, 2, 4, C], F32))
        vw = ctx.enter_context(nc.sbuf_tensor("vw", [P, 2, MH, DV1], F32))
        fin = ctx.enter_context(nc.sbuf_tensor("fin_c", [P, 2, 4, DV1], F32))
        tr = ctx.enter_context(nc.psum_tensor("trk", [P, 2, 512], F32))
        st = ctx.enter_context(nc.psum_tensor("stc", [P, 2, 2, 512], F32))
        tr_done, k_tok, one, vw_ready, st_done, st_used, c0_in, chain = open_sems(
            nc, ctx, *["mb_" + n for n in ("tr_done", "k_tok", "one", "vw_ready", "st_done", "st_used", "c0_in",
                                           "chain")])
        kc_in = open_sems(nc, ctx, "kc_in0", "kc_in1")
        v_in = open_sems(nc, ctx, *[f"v_in{i}" for i in range(NC)])
        block = ctx.enter_context(nc.Block())
        order = [0] + list(range(NC - 1, 0, -1))
        jobs = [(0, 0), (0, 1)] + [(c, 1) for c in range(NC - 1, 1, -1)]
        at = {c: n for n, c in enumerate(order)}

        @block.sync
        def _(sp):
            sp.dma_start(snap[:, NC - 2, :, :], a["s_ml"][:, 1, :, :]).then_inc(c0_in, 16)
            for n, c in enumerate(order):
                if n >= 2:
                    sp.wait_ge(tr_done, n - 1)
                sp.dma_start(kc[:, n % 2, :, :],
                             scr["qk"][4:8, :, c * C:(c + 1) * C].rearrange("i p t -> p i t")
                             ).then_inc(kc_in[n % 2], 16)
                sp.dma_start(v[:, c, :, 0:DV], scr["zvo"][1][c].rearrange("p (h x) -> p h x", h=MH)
                             ).then_inc(v_in[c], 16)
            sp.wait_ge(st_used, 2)
            sp.dma_start(o["ml"], fin[:, :, :, :]).then_inc(o["ml_out"], 16)
            sp.wait_ge(o["ml_out"], 16)

        @block.tensor
        def _(pe):
            def turn(n):
                pe.wait_ge(kc_in[n % 2], 16 * (n // 2 + 1))
                if n >= 2:
                    pe.wait_ge(k_tok, n - 1)
                for i in range(4):
                    m = pe.transpose(tr[:, n % 2, i * P:(i + 1) * P], kc[:, n % 2, i, :], const(k, "ident"))
                m.then_inc(tr_done, 1)

            def state(n):
                c, d = jobs[n]
                pe.wait_ge(vw_ready, n + 1)
                pe.wait_ge(k_tok, at[c] + 1)
                if n >= 2:
                    pe.wait_ge(st_used, n - 1)
                for h in range(MH):
                    hp, r = h // 2, slice(64 * (h % 2), 64 * (h % 2) + 64)
                    m = pe.matmul(st[r, n % 2, hp // 2, (hp % 2) * DV1:(hp % 2 + 1) * DV1],
                                  kt[:, c, h * DK:(h + 1) * DK], vw[:, n % 2, h, :], start=True, stop=True,
                                  skip_group_check=True)
                m.then_inc(st_done, 1)

            turn(0)
            turn(1)
            state(0)
            state(1)
            for n in range(2, NC):
                turn(n)
                state(n)

        @block.scalar
        def _(act):
            for n, c in enumerate(order):
                act.wait_ge(tr_done, n + 1)
                act.activation(kt[:, c, :], tr[:, n % 2, :], ACT.Copy).then_inc(k_tok, 1)

        @block.gpsimd
        def _(pool):
            pool.memset(v[:, :, :, DV:DV1], 1.0).then_inc(one, 1)
            pool.wait_ge(one, 1)
            for n, (c, d) in enumerate(jobs):
                pool.wait_ge(v_in[c], 16)
                if n >= 2:
                    pool.wait_ge(st_done, n - 1)
                w = spread(g["eend"][:, c, 32 + 8 * d:40 + 8 * d].unsqueeze(2), [P, MH, DV1])
                pool.tensor_tensor(vw[:, n % 2, :, :], v[:, c, :, :], w, ALU.mult).then_inc(vw_ready, 1)

        @block.vector
        def _(dve):
            link = Chain(dve, chain)
            dve.wait_ge(c0_in, 16)
            for n, (c, d) in enumerate(jobs):
                dve.wait_ge(st_done, n + 1)
                if c == 0:
                    for j in range(2):
                        link(dve.tensor_copy(fin[:, d, 2 * j:2 * j + 2, :],
                                             st[:, n % 2, j, 0:2 * DV1].rearrange("p (a x) -> p a x", a=2)))
                else:
                    for half in range(2):
                        r = slice(64 * half, 64 * half + 64)
                        link(dve.tensor_tensor(snap[r, c - 2, :, :], snap[r, c - 1, :, :],
                                               ml_decay(g, 1, c, 0, 4, half), ALU.mult))
                    for j in range(2):
                        link(dve.tensor_tensor(snap[:, c - 2, 2 * j:2 * j + 2, :], snap[:, c - 2, 2 * j:2 * j + 2, :],
                                               st[:, n % 2, j, 0:2 * DV1].rearrange("p (a x) -> p a x", a=2),
                                               ALU.add))
                dve.sem_inc(st_used, 1)


def mlstm_forward(nc, a, k, g, scr, v, kt, snap):
    with ExitStack() as ctx:
        U = NC * 4
        qk = ctx.enter_context(nc.sbuf_tensor("qk", [P, 2, 8, C], F32))
        qm = ctx.enter_context(nc.sbuf_tensor("qm", [P, 2, 2, 4, C], F32))
        og = ctx.enter_context(nc.sbuf_tensor("og", [P, 2, D], F32))
        lm = ctx.enter_context(nc.sbuf_tensor("lm", [P, 2, 4, C], F32))
        e = ctx.enter_context(nc.sbuf_tensor("e_m", [P, 2, 4, C], F32))
        wm = ctx.enter_context(nc.sbuf_tensor("wm_m", [P, 2, 4, C], F32))
        qw = ctx.enter_context(nc.sbuf_tensor("qw", [P, 2, 2, 4, C], F32))
        vw = ctx.enter_context(nc.sbuf_tensor("vwf", [P, MH, DV1], F32))
        hb = ctx.enter_context(nc.sbuf_tensor("hb", [P, 2, 2, MH, DV1], F32))
        hs = ctx.enter_context(nc.sbuf_tensor("hs", [P, 2, D], F32))
        sqb = ctx.enter_context(nc.sbuf_tensor("sqm", [P, D], F32))
        den = ctx.enter_context(nc.sbuf_tensor("den", [P, 2, MH], F32))
        ss = ctx.enter_context(nc.sbuf_tensor("ss_m", [P, 2, MH], F32))
        cf = ctx.enter_context(nc.sbuf_tensor("cf", [P, 2, 4, DV1], F32))
        ho = ctx.enter_context(nc.sbuf_tensor("ho", [P, 2, KD, C], F32))
        selm = ctx.enter_context(nc.sbuf_tensor("selm", [48, 16, P], F32))
        selq = ctx.enter_context(nc.sbuf_tensor("selq", [48, 8, P], F32))
        wir = ctx.enter_context(nc.sbuf_tensor("wir", [48, T], F32))
        negi = ctx.enter_context(nc.sbuf_tensor("negi", [P, P], BF16))
        mk = ctx.enter_context(nc.sbuf_tensor("mk", [P, 2, 4, C], BF16))
        arg = ctx.enter_context(nc.psum_tensor("arg_m", [P, 2, 4, C], F32))
        sc = ctx.enter_context(nc.psum_tensor("sc_m", [P, 2, 4, C], F32))
        qb = ctx.enter_context(nc.psum_tensor("qb", [P, 4, C], F32))
        misc = ctx.enter_context(nc.psum_tensor("misc_m", [P, 512], F32))
        num = ctx.enter_context(nc.psum_tensor("num", [P, 2, 512], F32))
        (lm_ready, arg_done, exp_done, sc_done, wm_done, qb_done, qw_done, num_done, h_copied, vw_ready, cf_done,
         hm_done, ss_done, rs_done, hn_done, misc_done, misc_used, c0_in, sel_in, wi_done, wi_row, mk_ready,
         ho_ready, chain, act_c, pool_c, sq_done) = open_sems(
            nc, ctx, *["m_" + n for n in (
                "lm_ready", "arg_done", "exp_done", "sc_done", "wm_done", "qb_done", "qw_done", "num_done",
                "h_copied", "vw_ready", "cf_done", "hm_done", "ss_done", "rs_done", "hn_done", "misc_done",
                "misc_used", "c0_in", "sel_in", "wi_done", "wi_row", "mk_ready", "ho_ready", "chain", "act", "pool",
                "sq_done")])
        qk_in = open_sems(nc, ctx, "qk_in0", "qk_in1")
        qm_ready, = open_sems(nc, ctx, "qm_ready")
        og_in = open_sems(nc, ctx, "og_in0", "og_in1")
        ho_out = open_sems(nc, ctx, "ho_out0", "ho_out1")
        block = ctx.enter_context(nc.Block())
        ML = slice(32, 48)

        uses = []
        for w in range(U + 6):
            c, r = w // 4, w % 4
            if r in (1, 2) and 1 <= c <= NC - 2:
                uses.append((f"st{r - 1}", c))
            if r == 3 and 1 <= c <= NC:
                uses.append(("tr0", c - 1))
            if r == 0 and 2 <= c <= NC + 1:
                uses.append(("tr1", c - 2))
        misc_at = {name: n for n, name in enumerate(uses)}

        def store(sp, c):
            sp.wait_ge(ho_ready, 2 * (c + 1))
            sp.dma_start(scr["hm"][:, :, c * C:(c + 1) * C], ho[:, c % 2, :, :]).then_inc(ho_out[c % 2], 16)

        @block.sync
        def _(sp):
            sp.dma_start(selm[:, :, :], a["selm"]).then_inc(sel_in, 16)
            sp.dma_start(selq[:, :, :], a["selq"]).then_inc(sel_in, 16)
            sp.dma_start(cf[:, 1, :, :], a["s_ml"][:, 0, :, :]).then_inc(c0_in, 16)
            for c in range(NC):
                if c >= 2:
                    sp.wait_ge(sc_done, 2 * (c - 1))
                    sp.wait_ge(qm_ready, 2 * (c - 1))
                sp.dma_start(qk[:, c % 2, :, :],
                             scr["qk"][:, :, c * C:(c + 1) * C].rearrange("i p t -> p i t")
                             ).then_inc(qk_in[c % 2], 16)
                if c >= 2:
                    sp.wait_ge(hn_done, c - 1)
                sp.dma_start(og[:, c % 2, :], scr["zvo"][2][c]).then_inc(og_in[c % 2], 16)
                if c >= 3:
                    store(sp, c - 3)
            for c in range(NC - 3, NC):
                store(sp, c)
            for s in range(2):
                sp.wait_ge(ho_out[s], 16 * len(range(s, NC, 2)))

        @block.gpsimd
        def _(pool):
            for w in range(U + 6):
                c, r = w // 4, w % 4
                if w < U:
                    hg, d = r // 2, r % 2
                    if w >= 2:
                        pool.wait_ge(arg_done, w - 1)
                    f = g["dec"][:, c, 32 + 8 * d + 4 * hg:36 + 8 * d + 4 * hg]
                    pool.tensor_tensor(lm[:, w % 2, :, :], spread(f.unsqueeze(2), [P, 4, C]),
                                       spread(const(k, "le" if d == 0 else "ge").unsqueeze(1), [P, 4, C]),
                                       ALU.mult).then_inc(lm_ready, 1)
                if r == 0 and 1 <= c <= NC - 2:
                    if c >= 2:
                        pool.wait_ge(misc_done, misc_at["st1", c - 1] + 1)
                    pool.tensor_tensor(vw[:, :, :], v[:, c, :, :],
                                       spread(g["eend"][:, c, 32:40].unsqueeze(2), [P, MH, DV1]),
                                       ALU.mult).then_inc(vw_ready, 1)

        @block.tensor
        def _(pe):
            for c in range(NC):
                if c >= 1:
                    pe.wait_ge(wi_row, c)
                pe.transpose(misc[0:48, 0:C], g["ecum"][:, c, :], const(k, "ident")).then_inc(wi_done, 1)
            pe.wait_ge(wi_row, NC)

            def shared(name):
                n = misc_at[name]
                if n:
                    pe.wait_ge(misc_used, n)

            pe.wait_ge(mk_ready, 3)
            pe.wait_ge(sel_in, 32)
            for w in range(U + 6):
                c, r = w // 4, w % 4
                if w < U:
                    hg, d, s = r // 2, r % 2, c % 2
                    if d == 0:
                        x = w // 2
                        if r == 0:
                            pe.wait_ge(qk_in[s], 16 * (c // 2 + 1))
                            pe.wait_ge(qm_ready, 2 * (c + 1))
                        if x >= 2:
                            pe.wait_ge(wm_done, 2 * (x - 1))
                        for i in range(4):
                            h = 4 * hg + i
                            m = pe.matmul(sc[:, x % 2, i, :], qk[:, s, 4 + h // 2, :], qm[:, s, h % 2, h // 2, :],
                                          start=True, stop=True)
                        m.then_inc(sc_done, 1)
                    if r < 2 and c >= 1:
                        n = 2 * (c - 1) + r
                        if n:
                            pe.wait_ge(qw_done, n + 2)
                        for hp in range(4):
                            m = pe.matmul(qb[:, hp, :], selq[ML, 4 * r + hp, :], wir[ML, c * C:(c + 1) * C],
                                          start=True, stop=True, skip_group_check=True)
                        m.then_inc(qb_done, 1)
                    pe.wait_ge(lm_ready, w + 1)
                    if w >= 2:
                        pe.wait_ge(exp_done, w - 1)
                    pe.matmul(arg[:, w % 2, :, :], const(k, "gt" if d == 0 else "lt"), lm[:, w % 2, :, :],
                              start=True, stop=False, skip_group_check=True)
                    for i in range(4):
                        pe.matmul(arg[:, w % 2, i, :], selm[ML, 8 * d + 4 * hg + i, :],
                                  g["negm"][ML, c * C:(c + 1) * C], start=False, stop=False, skip_group_check=True)
                    pe.matmul(arg[:, w % 2, :, :], negi[:, :], mk[:, d, :, :], start=False, stop=True,
                              skip_group_check=True).then_inc(arg_done, 1)
                if 1 <= w <= U:
                    wn = w - 1
                    cn, hg, d = wn // 4, (wn % 4) // 2, wn % 2
                    pe.wait_ge(wm_done, wn + 1)
                    if cn >= 1:
                        pe.wait_ge(qw_done, 2 * cn + d + 1)
                        if cn == 1:
                            pe.wait_ge(c0_in, 16)
                        else:
                            pe.wait_ge(cf_done, 2 * (cn - 1))
                    for j in range(2):
                        n = 2 * wn + j
                        if n >= 2:
                            pe.wait_ge(h_copied, n - 1)
                        for i in range(2):
                            h = 4 * hg + 2 * j + i
                            dst = num[:, n % 2, i * DV1:(i + 1) * DV1]
                            m = pe.matmul(dst, wm[:, wn % 2, 2 * j + i, :], v[:, cn, h, :], start=True,
                                          stop=(cn == 0), skip_group_check=True)
                            if cn >= 1:
                                st = cf[:, cn % 2, h // 2, :] if d == 0 else snap[:, cn - 1, h // 2, :]
                                m = pe.matmul(dst, qw[:, d, h % 2, h // 2, :], st, start=False, stop=True,
                                              skip_group_check=True)
                        m.then_inc(num_done, 1)
                if r in (1, 2) and 1 <= c <= NC - 2:
                    j = r - 1
                    pe.wait_ge(vw_ready, c)
                    shared((f"st{j}", c))
                    for h in range(4 * j, 4 * j + 4):
                        p0 = slice(64 * (h % 2), 64 * (h % 2) + 64)
                        i = (h // 2) % 2
                        m = pe.matmul(misc[p0, i * DV1:(i + 1) * DV1], kt[:, c, h * DK:(h + 1) * DK], vw[:, h, :],
                                      start=True, stop=True, skip_group_check=True)
                    m.then_inc(misc_done, 1)
                for name, j, r0, back in (("tr0", 0, 3, 1), ("tr1", 1, 0, 2)):
                    if r == r0 and back <= c <= NC - 1 + back:
                        cc = c - back
                        pe.wait_ge(hn_done, cc + 1)
                        shared((name, cc))
                        for i in range(4):
                            m = pe.transpose(misc[:, i * P:(i + 1) * P],
                                             hs[:, cc % 2, (4 * j + i) * P:(4 * j + i + 1) * P], const(k, "ident"))
                        m.then_inc(misc_done, 1)

        @block.scalar
        def _(act):
            link = Chain(act, act_c)
            for c in range(NC):
                act.wait_ge(wi_done, c + 1)
                act.activation(wir[ML, c * C:(c + 1) * C], misc[ML, 0:C], ACT.Copy).then_inc(wi_row, 1)

            def one_head(c):
                act.wait_ge(qk_in[c % 2], 16 * (c // 2 + 1))
                if c >= 2:
                    act.wait_ge(sc_done, 2 * (c - 1))
                    act.wait_ge(qw_done, 2 * (c - 1))
                for half in range(2):
                    act.activation(qm[:, c % 2, half, :, :], qk[:, c % 2, 0:4, :], ACT.Copy,
                                   scale=const(k, f"half{half}")).then_inc(qm_ready, 1)

            one_head(0)
            for w in range(U + 6):
                c, r = w // 4, w % 4
                if r == 2 and c + 1 < NC:
                    one_head(c + 1)
                if w < U:
                    hg, d = r // 2, r % 2
                    act.wait_ge(arg_done, w + 1)
                    if w >= 2:
                        act.wait_ge(wm_done, w - 1)
                    for i in range(4):
                        j = 32 + 8 * d + 4 * hg + i
                        m = act.activation(e[:, w % 2, i, :], arg[:, w % 2, i, :], ACT.Exp,
                                           bias=g["dt_ig"][:, c, j:j + 1])
                    m.then_inc(exp_done, 1)
                if 1 <= w <= U:
                    wn = w - 1
                    cn, hg, d = wn // 4, (wn % 4) // 2, wn % 2
                    if cn >= 2 and wn % 4 == 0:
                        act.wait_ge(hm_done, cn - 1)
                    for j in range(2):
                        n = 2 * wn + j
                        act.wait_ge(num_done, n + 1)
                        act.activation(hb[:, cn % 2, d, 4 * hg + 2 * j:4 * hg + 2 * j + 2, :],
                                       num[:, n % 2, 0:2 * DV1].rearrange("p (a x) -> p a x", a=2),
                                       ACT.Copy).then_inc(h_copied, 1)
                if r == 2 and 1 <= c <= NC:
                    cc = c - 1
                    act.wait_ge(ss_done, cc + 1)
                    link(act.activation(ss[:, cc % 2, :], ss[:, cc % 2, :], ACT.Ln, bias=const(k, "eps"),
                                        scale=1.0 / DV))
                    act.activation(ss[:, cc % 2, :], ss[:, cc % 2, :], ACT.Exp, scale=-0.5).then_inc(rs_done, 1)

        @block.vector
        def _(dve):
            link = Chain(dve, chain)
            dve.tensor_scalar(negi[:, :], const(k, "ident"), NEG, None, ALU.mult).then_inc(mk_ready, 1)
            for d, mask in enumerate(("gt", "lt")):
                dve.tensor_copy(mk[:, d, :, :], spread(const(k, mask).unsqueeze(1), [P, 4, C])).then_inc(mk_ready, 1)
            for w in range(U + 6):
                c, r = w // 4, w % 4
                if w < U:
                    hg, d, s = r // 2, r % 2, c % 2
                    if r < 2:
                        if c >= 1:
                            dve.wait_ge(qb_done, 2 * (c - 1) + r + 1)
                            if c >= 2:
                                dve.wait_ge(num_done, 2 * (4 * (c - 1) + 2 + r) + 2)
                            for half in range(2):
                                m = dve.tensor_tensor(qw[:, r, half, :, :], qm[:, s, half, :, :], qb[:, :, :],
                                                      ALU.mult)
                            m.then_inc(qw_done, 1)
                        else:
                            dve.sem_inc(qw_done, 1)
                    dve.wait_ge(exp_done, w + 1)
                    if w >= 2:
                        dve.wait_ge(num_done, 2 * (w - 1))
                    dve.wait_ge(sc_done, w // 2 + 1)
                    dve.tensor_tensor(wm[:, w % 2, :, :], e[:, w % 2, :, :], sc[:, (w // 2) % 2, :, :],
                                      ALU.mult).then_inc(wm_done, 1)
                if r == 1 and 1 <= c <= NC:
                    cc = c - 1
                    q = cc % 2
                    dve.wait_ge(h_copied, 8 * (cc + 1))
                    dn = hb[:, q, :, :, DV]
                    link(dve.scalar_tensor_tensor(out=den[:, :, :], in0=dn, scalar=-1.0, in1=dn, op0=ALU.mult,
                                                  op1=ALU.max))
                    link(dve.tensor_tensor(den[:, :, :], den[:, :, :],
                                           g["em"][:, cc, :].rearrange("p (d h) -> p d h", d=2), ALU.max))
                    link(dve.reciprocal(den[:, :, :], den[:, :, :]))
                    h3 = hs[:, q, :].rearrange("p (h x) -> p h x", h=MH)
                    s3 = sqb[:, :].rearrange("p (h x) -> p h x", h=MH)
                    if cc >= 2:
                        dve.wait_ge(misc_done, misc_at["tr1", cc - 2] + 1)
                    link(dve.tensor_tensor(h3, hb[:, q, 0, :, 0:DV], spread(den[:, 0, :].unsqueeze(2), [P, MH, DV]),
                                           ALU.mult))
                    link(dve.tensor_tensor(s3, hb[:, q, 1, :, 0:DV], spread(den[:, 1, :].unsqueeze(2), [P, MH, DV]),
                                           ALU.mult))
                    dve.sem_inc(hm_done, 1)
                    link(dve.tensor_tensor(hs[:, q, :], hs[:, q, :], sqb[:, :], ALU.add))
                    link(dve.tensor_tensor(sqb[:, :], hs[:, q, :], hs[:, q, :], ALU.mult))
                    dve.tensor_reduce(ss[:, q, :], s3, AX.X, ALU.add).then_inc(ss_done, 1)
                    dve.wait_ge(ss_done, cc + 1)
                if r == 2 and 1 <= c <= NC:
                    cc = c - 1
                    q = cc % 2
                    h3 = hs[:, q, :].rearrange("p (h x) -> p h x", h=MH)
                    dve.wait_ge(rs_done, cc + 1)
                    link(dve.tensor_tensor(h3, h3, spread(ss[:, q, :].unsqueeze(2), [P, MH, DV]), ALU.mult))
                    dve.wait_ge(og_in[q], 16 * (cc // 2 + 1))
                    dve.tensor_tensor(hs[:, q, :], hs[:, q, :], og[:, q, :], ALU.mult).then_inc(hn_done, 1)
                if r in (2, 3) and 1 <= c <= NC - 2:
                    j = r - 2
                    dst = cf[:, (c + 1) % 2, 2 * j:2 * j + 2, :]
                    if c == 1:
                        dve.wait_ge(c0_in, 16)
                    else:
                        dve.wait_ge(num_done, 8 * c)
                    for half in range(2):
                        p0 = slice(64 * half, 64 * half + 64)
                        link(dve.tensor_tensor(cf[p0, (c + 1) % 2, 2 * j:2 * j + 2, :], cf[p0, c % 2, 2 * j:2 * j + 2, :],
                                               ml_decay(g, 0, c, 2 * j, 2, half), ALU.mult))
                    dve.wait_ge(misc_done, misc_at[f"st{j}", c] + 1)
                    link(dve.tensor_tensor(dst, dst, misc[:, 0:2 * DV1].rearrange("p (a x) -> p a x", a=2), ALU.add))
                    dve.sem_inc(misc_used, 1)
                    dve.sem_inc(cf_done, 1)
                for name, j, r0 in (("tr0", 0, 0), ("tr1", 1, 1)):
                    if r == r0 and 2 <= c <= NC + 1:
                        cc = c - 2
                        dve.wait_ge(misc_done, misc_at[name, cc] + 1)
                        if cc >= 2:
                            dve.wait_ge(ho_out[cc % 2], 16 * (cc // 2))
                        dve.tensor_tensor(ho[:, cc % 2, 4 * j:4 * j + 4, :],
                                          misc[:, :].rearrange("p (i t) -> p i t", i=4),
                                          spread(col(k, "ml_norm", 4 * j, 4).unsqueeze(2), [P, 4, C]),
                                          ALU.mult).then_inc(ho_ready, 1)
                        dve.wait_ge(ho_ready, 2 * cc + j + 1)
                        dve.sem_inc(misc_used, 1)


def out_proj(nc, a, k, h, ah, al, scr):
    with ExitStack() as ctx:
        NT3 = 3 * KD
        raw = ctx.enter_context(nc.sbuf_tensor("raw_o", [P, 4, KD, P], F32))
        wh = ctx.enter_context(nc.sbuf_tensor("wh_o", [P, 2, KD, P], F32R))
        wl = ctx.enter_context(nc.sbuf_tensor("wl_o", [P, 2, KD, P], F32R))
        xr = ctx.enter_context(nc.sbuf_tensor("xr", [P, 2, T], F32))
        gt = ctx.enter_context(nc.sbuf_tensor("gt", [P, 2, T], F32))
        tm = ctx.enter_context(nc.sbuf_tensor("tm", [P, T], F32))
        acc = [ctx.enter_context(nc.psum_tensor(f"acc_o{i}", [P, 3, 512], F32))[:, :, 0:TB] for i in range(2)]
        w_hi, w_lo, a_hi, a_lo, tile_done, out_done, chain = open_sems(
            nc, ctx, "o_w_hi", "o_w_lo", "o_a_hi", "o_a_lo", "o_tile", "o_out", "chain_o")
        raw_in = open_sems(nc, ctx, *[f"o_raw{i}" for i in range(4)])
        xr_in = open_sems(nc, ctx, "o_xr0", "o_xr1")
        gt_in = open_sems(nc, ctx, "o_gt0", "o_gt1")
        block = ctx.enter_context(nc.Block())

        @block.sync
        def _(sp):
            def weight(i):
                if i >= 4:
                    sp.wait_ge(w_lo, i - 3)
                sp.dma_start(raw[:, i % 4, :, :], a["w_o"][i]).then_inc(raw_in[i % 4], 16)

            def operand(i):
                if i >= 2:
                    sp.wait_ge(a_lo, i - 1)
                src = scr["yn" if i < KD else "hm"][:, i % KD, :]
                sp.dma_start(xr[:, i % 2, :], src).then_inc(xr_in[i % 2], 16)

            for load, i0, i1 in ((weight, 0, 4), (operand, 0, KD), (weight, 4, 10), (operand, KD, KD + 2),
                                 (weight, 10, 12), (operand, KD + 2, 2 * KD), (weight, 12, NT3)):
                for i in range(i0, i1):
                    load(i)

        @block.gpsimd
        def _(pool):
            for i in range(NT3):
                if i >= 2:
                    pool.wait_ge(out_done, i - 1)
                src = scr["gate"][i] if i < 2 * KD else a["xT"][:, i - 2 * KD, :]
                pool.dma_start(gt[:, i % 2, :], src).then_inc(gt_in[i % 2], 16)

        @block.scalar
        def _(act):
            def weight(i):
                act.wait_ge(raw_in[i % 4], 16 * (i // 4 + 1))
                if i >= 2:
                    act.wait_ge(tile_done, i - 1)
                act.activation(wh[:, i % 2, :, :], raw[:, i % 4, :, :], ACT.Copy).then_inc(w_hi, 1)

            weight(0)
            for i in range(NT3):
                if i % KD == 0:
                    gi = i // KD
                    if gi:
                        act.wait_ge(tile_done, i)
                    if gi == 2:
                        act.wait_ge(out_done, i)
                    for q in range(KD):
                        n = i + q
                        if gi < 2:
                            act.wait_ge(xr_in[n % 2], 16 * (n // 2 + 1))
                        act.activation(ah[:, q, :], xr[:, n % 2, :] if gi < 2 else h[:, q, :],
                                       ACT.Copy).then_inc(a_hi, 1)
                if i + 1 < NT3:
                    weight(i + 1)

        @block.tensor
        def _(pe):
            for i in range(NT3):
                pe.wait_ge(w_hi, i + 1)
                pe.wait_ge(w_lo, i + 1)
                if i >= 2:
                    pe.wait_ge(out_done, i - 1)
                for kt in range(KD):
                    if i % KD == 0:
                        pe.wait_ge(a_lo, i + kt + 1)
                    m = split_product(pe, acc[i % 2], wh[:, i % 2, kt, :], wl[:, i % 2, kt, :], ah, al, kt,
                                      kt == KD - 1, kt == 0)
                m.then_inc(tile_done, 1)

        @block.vector
        def _(dve):
            link = Chain(dve, chain)

            def weight(i):
                dve.wait_ge(w_hi, i + 1)
                dve.tensor_tensor(wl[:, i % 2, :, :], raw[:, i % 4, :, :], wh[:, i % 2, :, :].bitcast(F32),
                                  ALU.subtract).then_inc(w_lo, 1)

            weight(0)
            for i in range(NT3):
                gi, q = i // KD, i % KD
                if q == 0:
                    for j in range(KD):
                        n = i + j
                        dve.wait_ge(a_hi, n + 1)
                        dve.tensor_tensor(al[:, j, :], xr[:, n % 2, :] if gi < 2 else h[:, j, :],
                                          ah[:, j, :].bitcast(F32), ALU.subtract).then_inc(a_lo, 1)
                    if gi == 2:
                        dve.wait_ge(a_lo, NT3)
                if i + 1 < NT3:
                    weight(i + 1)
                dve.wait_ge(tile_done, i + 1)
                dve.wait_ge(gt_in[i % 2], 16 * (i // 2 + 1))
                gate, dst = blocks(gt[:, i % 2, :]), blocks(h[:, q, :])
                if gi == 0:
                    link(dve.tensor_tensor(dst, acc[i % 2], gate, ALU.mult))
                elif gi == 1:
                    link(dve.tensor_tensor(blocks(tm[:, :]), acc[i % 2], gate, ALU.mult))
                    link(dve.tensor_tensor(h[:, q, :], h[:, q, :], tm[:, :], ALU.add))
                else:
                    for s, t, view in PARTS:
                        link(dve.scalar_tensor_tensor(out=part(h[:, q, :], t), in0=view(acc[i % 2]),
                                                      scalar=k["mod"][:, 16 + q, s:s + 1],
                                                      in1=part(gt[:, i % 2, :], t), op0=ALU.mult, op1=ALU.add))
                dve.sem_inc(out_done, 1)


def norm_ffn(nc, a, k, h, uh, ul):
    with ExitStack() as ctx:
        sq = ctx.enter_context(nc.sbuf_tensor("sq2", [P, 2, T], F32))
        u = ctx.enter_context(nc.sbuf_tensor("u2", [P, 2, T], F32))
        rstd = ctx.enter_context(nc.sbuf_tensor("rstd2", [P, T], F32))
        scl = ctx.enter_context(nc.sbuf_tensor("scl2", [P, KD, 2], F32))
        one = ctx.enter_context(nc.sbuf_tensor("one2", [P, P + 1], F32))
        ss_bank = ctx.enter_context(nc.psum_tensor("ss2", [P, 3, 512], F32))
        ss = ss_bank[:, :, 0:TB]
        one_set, sq_ready, sq_used, root, rstd_ready, scl_ready, xn_ready, u_ready, hi_done, lo_done = open_sems(
            nc, ctx, *["n2_" + n for n in ("one", "sq_ready", "sq_used", "root", "rstd", "scl", "xn", "u", "hi",
                                           "lo")])
        block = ctx.enter_context(nc.Block())

        @block.scalar
        def _(act):
            for i in range(KD):
                if i >= 2:
                    act.wait_ge(sq_used, i - 1)
                act.activation(sq[:, i % 2, :], h[:, i, :], ACT.Square).then_inc(sq_ready, 1)
            act.wait_ge(sq_used, KD)
            act.wait_ge(one_set, 2)
            act.activation(blocks(rstd[:, :]), ss, ACT.Sqrt, bias=one[:, P:P + 1], scale=1.0 / D).then_inc(root, 1)
            act.wait_ge(scl_ready, 2)
            for i in range(KD):
                act.wait_ge(xn_ready, i + 1)
                if i >= 2:
                    act.wait_ge(lo_done, i - 1)
                for s, (t0, t1) in enumerate(((0, CTX), (CTX, T))):
                    act.activation(u[:, i % 2, t0:t1], sq[:, i % 2, t0:t1], ACT.Identity,
                                   bias=k["mod"][:, 24 + i, s:s + 1], scale=scl[:, i, s:s + 1]).then_inc(u_ready, 1)
                act.wait_ge(u_ready, 2 * i + 2)
                act.activation(uh[:, i, :], u[:, i % 2, :], ACT.Copy).then_inc(hi_done, 1)

        @block.tensor
        def _(pe):
            pe.wait_ge(one_set, 1)
            for i in range(KD):
                pe.wait_ge(sq_ready, i + 1)
                for bank, t0, n in BLOCKS:
                    m = pe.matmul(ss[:, bank, 0:n], one[:, 0:P], sq[:, i % 2, t0:t0 + n], start=(i == 0),
                                  stop=(i == KD - 1))
                m.then_inc(sq_used, 1)

        @block.vector
        def _(dve):
            dve.memset(one[:, 0:P], 1.0).then_inc(one_set, 1)
            dve.memset(one[:, P:P + 1], EPS).then_inc(one_set, 1)
            for s in range(2):
                dve.scalar_tensor_tensor(out=scl[:, :, s], in0=k["mod"][:, 32:40, s], scalar=1.0,
                                         in1=col(k, "norm_ffn", 0, KD), op0=ALU.add,
                                         op1=ALU.mult).then_inc(scl_ready, 1)
            dve.wait_ge(root, 1)
            dve.reciprocal(rstd[:, :], rstd[:, :]).then_inc(rstd_ready, 1)
            dve.wait_ge(rstd_ready, 1)
            for i in range(KD):
                if i >= 2:
                    dve.wait_ge(u_ready, 2 * (i - 1))
                dve.tensor_tensor(sq[:, i % 2, :], h[:, i, :], rstd[:, :], ALU.mult).then_inc(xn_ready, 1)

        @block.gpsimd
        def _(pool):
            for i in range(KD):
                pool.wait_ge(hi_done, i + 1)
                pool.tensor_tensor(ul[:, i, :], u[:, i % 2, :], uh[:, i, :].bitcast(F32),
                                   ALU.subtract).then_inc(lo_done, 1)
            pool.wait_ge(lo_done, KD)


def ffn(nc, a, k, h, uh, ul):
    with ExitStack() as ctx:
        NG, NU, RING, AR = FT // 2, 2 * FT, 2, 3
        PR, PW = ROWS + 2, GRID_W + 2
        raw = ctx.enter_context(nc.sbuf_tensor("raw_u", [P, RING, KD, P], F32))
        wh = ctx.enter_context(nc.sbuf_tensor("wh_u", [P, 2, KD, P], F32R))
        wl = ctx.enter_context(nc.sbuf_tensor("wl_u", [P, 2, KD, P], F32R))
        dr = ctx.enter_context(nc.sbuf_tensor("raw_d", [P, 2, D], F32))
        dh = ctx.enter_context(nc.sbuf_tensor("wh_d", [P, 2, D], F32R))
        dl = ctx.enter_context(nc.sbuf_tensor("wl_d", [P, 2, D], F32R))
        fh = ctx.enter_context(nc.sbuf_tensor("fh", [P, AR, T], F32R))
        fl = ctx.enter_context(nc.sbuf_tensor("fl", [P, AR, T], F32R))
        gp = ctx.enter_context(nc.sbuf_tensor("gp", [P, PR, PW], F32))
        gc = ctx.enter_context(nc.sbuf_tensor("gc", [P, CTX + 2], F32))
        y = ctx.enter_context(nc.sbuf_tensor("y", [P, 2, T], F32))
        acc = [ctx.enter_context(nc.psum_tensor(f"acc_u{i}", [P, 3, 512], F32))[:, :, 0:TB] for i in range(2)]
        dacc = ctx.enter_context(nc.psum_tensor("dacc", [P, 2, 512], F32))
        (w_hi, w_lo, d_in, d_hi, d_lo, up_done, g_evac, pad_zero, conv_done, silu_done, act_done, f_hi, f_lo,
         piece_done, piece_used, down_done, chain) = open_sems(
            nc, ctx, *["u_" + n for n in (
                "w_hi", "w_lo", "d_in", "d_hi", "d_lo", "up_done", "g_evac", "pad_zero", "conv_done", "silu_done",
                "act_done", "f_hi", "f_lo", "piece_done", "piece_used", "down_done", "chain")])
        raw_in = open_sems(nc, ctx, *[f"u_raw{i}" for i in range(RING)])
        block = ctx.enter_context(nc.Block())

        @block.sync
        def _(sp):
            for i in range(NU):
                if i >= RING:
                    sp.wait_ge(w_lo, i - RING + 1)
                sp.dma_start(raw[:, i % RING, :, :], a["w_up"][i]).then_inc(raw_in[i % RING], 16)
                if i % 4 == 1:
                    if i // 4:
                        sp.wait_ge(d_lo, i // 4)
                    sp.dma_start(dr[:, :, :], a["w_down"][i // 4]).then_inc(d_in, 16)

        @block.tensor
        def _(pe):
            def up(i):
                pe.wait_ge(w_hi, i + 1)
                pe.wait_ge(w_lo, i + 1)
                f = i // 2
                if f >= 1:
                    if i % 2 == 0:
                        pe.wait_ge(g_evac, f)
                    else:
                        pe.wait_ge(act_done, f)
                for kt in range(KD):
                    m = split_product(pe, acc[i % 2], wh[:, i % 2, kt, :], wl[:, i % 2, kt, :], uh, ul, kt,
                                      kt == KD - 1, kt == 0)
                m.then_inc(up_done, 1)

            def down(j):
                pe.wait_ge(d_hi, j + 1)
                pe.wait_ge(d_lo, j + 1)
                pe.wait_ge(f_hi, 2 * j + 2)
                pe.wait_ge(f_lo, 2 * j + 2)
                for m_ in range(KD):
                    for bank, t0, n in BLOCKS:
                        q = (j * KD + m_) * 3 + bank
                        if q >= 2:
                            pe.wait_ge(piece_used, q - 1)
                        cols = slice(m_ * P, m_ * P + P)
                        for r in range(2):
                            s = (2 * j + r) % AR
                            for p_, (w, x) in enumerate(((dh, fh), (dh, fl), (dl, fh))):
                                m = pe.matmul(dacc[:, q % 2, 0:n], w[:, r, cols], x[:, s, t0:t0 + n],
                                              start=(r == 0 and p_ == 0), stop=(r == 1 and p_ == 2))
                        m.then_inc(piece_done, 1)

            for i in range(NG):
                up(4 * i)
                up(4 * i + 1)
                if i:
                    down(i - 1)
                up(4 * i + 2)
                up(4 * i + 3)
            down(NG - 1)

        @block.scalar
        def _(act):
            def high(i):
                act.wait_ge(raw_in[i % RING], 16 * (i // RING + 1))
                if i >= 2:
                    act.wait_ge(up_done, i - 1)
                act.activation(wh[:, i % 2, :, :], raw[:, i % RING, :, :], ACT.Copy).then_inc(w_hi, 1)

            def high_down(j):
                act.wait_ge(d_in, 16 * (j + 1))
                if j:
                    act.wait_ge(piece_done, 3 * KD * j)
                act.activation(dh[:, :, :], dr[:, :, :], ACT.Copy).then_inc(d_hi, 1)

            def evac(f):
                act.wait_ge(up_done, 2 * f + 1)
                if f == 0:
                    act.wait_ge(pad_zero, 2)
                else:
                    act.wait_ge(conv_done, f)
                act.activation(gc[:, 1:1 + CTX], PARTS[0][2](acc[0]), ACT.Copy)
                r = (TB - CTX) // GRID_W
                act.activation(gp[:, 1:1 + r, 1:1 + GRID_W],
                               PARTS[1][2](acc[0]).rearrange("p (r w) -> p r w", w=GRID_W), ACT.Copy)
                for b in (1, 2):
                    r0 = 1 + (b * TB - CTX) // GRID_W
                    m = act.activation(gp[:, r0:r0 + TB // GRID_W, 1:1 + GRID_W],
                                       acc[0][:, b, :].rearrange("p (r w) -> p r w", w=GRID_W), ACT.Copy)
                m.then_inc(g_evac, 1)

            def silu(f):
                act.wait_ge(conv_done, f + 1)
                act.activation(y[:, f % 2, :], y[:, f % 2, :], ACT.Silu,
                               bias=col(k, "ffn_b", f)).then_inc(silu_done, 1)

            def act_high(f):
                act.wait_ge(act_done, f + 1)
                if f >= AR:
                    act.wait_ge(piece_done, 3 * KD * ((f - AR) // 2 + 1))
                act.activation(fh[:, f % AR, :], y[:, f % 2, :], ACT.Copy).then_inc(f_hi, 1)

            high(0)
            high(1)
            for f in range(FT):
                evac(f)
                if 2 * f + 2 < NU:
                    high(2 * f + 2)
                silu(f)
                if 2 * f + 3 < NU:
                    high(2 * f + 3)
                act_high(f)
                if f % 2 == 1:
                    high_down(f // 2)

        @block.vector
        def _(dve):
            link = Chain(dve, chain)
            dve.memset(gp[:, :, :], 0.0).then_inc(pad_zero, 1)
            dve.memset(gc[:, :], 0.0).then_inc(pad_zero, 1)

            def conv(f):
                dve.wait_ge(g_evac, f + 1)
                if f >= 2:
                    dve.wait_ge(f_lo, f - 1)
                yc = y[:, f % 2, 0:CTX]
                yl = y[:, f % 2, CTX:T].rearrange("p (r w) -> p r w", w=GRID_W)
                for n, (dx, tap) in enumerate(((0, 3), (1, 4), (2, 5))):
                    w = col(k, "ffn_w", 9 * f + tap)
                    x = gc[:, dx:dx + CTX]
                    link(dve.tensor_scalar(yc, x, w, None, ALU.mult) if n == 0 else
                         dve.scalar_tensor_tensor(out=yc, in0=x, scalar=w, in1=yc, op0=ALU.mult, op1=ALU.add))
                for tap in range(9):
                    w = col(k, "ffn_w", 9 * f + tap)
                    x = gp[:, tap // 3:tap // 3 + ROWS, tap % 3:tap % 3 + GRID_W]
                    if tap == 0:
                        link(dve.tensor_scalar(yl, x, w, None, ALU.mult))
                    else:
                        ins = dve.scalar_tensor_tensor(out=yl, in0=x, scalar=w, in1=yl, op0=ALU.mult, op1=ALU.add)
                        if tap < 8:
                            link(ins)
                ins.then_inc(conv_done, 1)

            def low(i):
                dve.wait_ge(w_hi, i + 1)
                dve.tensor_tensor(wl[:, i % 2, :, :], raw[:, i % RING, :, :], wh[:, i % 2, :, :].bitcast(F32),
                                  ALU.subtract).then_inc(w_lo, 1)

            def times_value(f):
                dve.wait_ge(silu_done, f + 1)
                dve.wait_ge(up_done, 2 * f + 2)
                yb = blocks(y[:, f % 2, :])
                dve.tensor_tensor(yb, yb, acc[1], ALU.mult).then_inc(act_done, 1)

            def low_down(j):
                dve.wait_ge(d_hi, j + 1)
                dve.tensor_tensor(dl[:, :, :], dr[:, :, :], dh[:, :, :].bitcast(F32),
                                  ALU.subtract).then_inc(d_lo, 1)

            def add_down(j):
                for m_ in range(KD):
                    for bank, t0, n in BLOCKS:
                        q = (j * KD + m_) * 3 + bank
                        dve.wait_ge(piece_done, q + 1)
                        for s_, p0, p1 in (((0, 0, CTX), (1, CTX, TB)) if bank == 0 else ((1, 0, TB),)):
                            x = h[:, m_, t0 + p0:t0 + p1]
                            ins = dve.scalar_tensor_tensor(out=x, in0=dacc[:, q % 2, p0:p1],
                                                           scalar=k["mod"][:, 40 + m_, s_:s_ + 1], in1=x,
                                                           op0=ALU.mult, op1=ALU.add)
                        ins.then_inc(piece_used, 1)

            low(0)
            low(1)
            for f in range(FT):
                conv(f)
                if 2 * f + 2 < NU:
                    low(2 * f + 2)
                times_value(f)
                if 2 * f + 3 < NU:
                    low(2 * f + 3)
                if f % 2 == 0 and f >= 2:
                    add_down(f // 2 - 1)
                if f % 2 == 1:
                    low_down(f // 2)
            add_down(NG - 1)

        @block.gpsimd
        def _(pool):
            for f in range(FT):
                pool.wait_ge(f_hi, f + 1)
                if f >= AR:
                    pool.wait_ge(piece_done, 3 * KD * ((f - AR) // 2 + 1))
                pool.tensor_tensor(fl[:, f % AR, :], y[:, f % 2, :], fh[:, f % AR, :].bitcast(F32),
                                   ALU.subtract).then_inc(f_lo, 1)
            pool.wait_ge(f_lo, FT)


def final_norm(nc, a, k, h, o):
    with ExitStack() as ctx:
        sq = ctx.enter_context(nc.sbuf_tensor("sq3", [P, 2, T], F32))
        out = ctx.enter_context(nc.sbuf_tensor("out3", [P, 2, T], F32))
        rstd = ctx.enter_context(nc.sbuf_tensor("rstd3", [P, T], F32))
        one = ctx.enter_context(nc.sbuf_tensor("one3", [P, P + 1], F32))
        ss_bank = ctx.enter_context(nc.psum_tensor("ss3", [P, 3, 512], F32))
        ss = ss_bank[:, :, 0:TB]
        one_set, sq_ready, sq_used, root, rstd_ready, y_ready = open_sems(
            nc, ctx, *["n3_" + n for n in ("one", "sq_ready", "sq_used", "root", "rstd", "y")])
        y_out = o["y0_out"], o["y1_out"]
        block = ctx.enter_context(nc.Block())

        @block.scalar
        def _(act):
            for i in range(KD):
                if i >= 2:
                    act.wait_ge(sq_used, i - 1)
                act.activation(sq[:, i % 2, :], h[:, i, :], ACT.Square).then_inc(sq_ready, 1)
            act.wait_ge(sq_used, KD)
            act.wait_ge(one_set, 2)
            act.activation(blocks(rstd[:, :]), ss, ACT.Sqrt, bias=one[:, P:P + 1], scale=1.0 / D).then_inc(root, 1)

        @block.tensor
        def _(pe):
            pe.wait_ge(one_set, 1)
            for i in range(KD):
                pe.wait_ge(sq_ready, i + 1)
                for bank, t0, n in BLOCKS:
                    m = pe.matmul(ss[:, bank, 0:n], one[:, 0:P], sq[:, i % 2, t0:t0 + n], start=(i == 0),
                                  stop=(i == KD - 1))
                m.then_inc(sq_used, 1)

        @block.vector
        def _(dve):
            dve.memset(one[:, 0:P], 1.0).then_inc(one_set, 1)
            dve.memset(one[:, P:P + 1], EPS).then_inc(one_set, 1)
            dve.wait_ge(root, 1)
            dve.reciprocal(rstd[:, :], rstd[:, :]).then_inc(rstd_ready, 1)
            dve.wait_ge(rstd_ready, 1)
            for i in range(KD):
                if i >= 2:
                    dve.wait_ge(y_out[i % 2], 16 * (i // 2))
                dve.scalar_tensor_tensor(out=out[:, i % 2, :], in0=h[:, i, :], scalar=col(k, "final_norm", i),
                                         in1=rstd[:, :], op0=ALU.mult, op1=ALU.mult).then_inc(y_ready, 1)

        @block.sync
        def _(sp):
            for i in range(KD):
                sp.wait_ge(y_ready, i + 1)
                sp.dma_start(o["y"][:, i, :], out[:, i % 2, :]).then_inc(y_out[i % 2], 16)
            for s in range(2):
                sp.wait_ge(y_out[s], 16 * (KD // 2))


def constants():
    i, j = np.arange(P)[:, None], np.arange(P)[None, :]
    con = np.zeros((P, NCON), np.float32)
    for name, m in (("ident", i == j), ("le", i <= j), ("gt", i > j), ("ge", i >= j), ("lt", i < j),
                    ("ones", i >= 0), ("row127", i == P - 1), ("row0", i == 0)):
        con[:, CC[name]:CC[name] + P] = np.broadcast_to(m, (P, P))
    r = np.arange(P)
    con[:, CC["sign"]] = np.where(r < 32, 1.0, -1.0)
    con[:, CC["fwd"]] = (r >= 32) & (r < 40)
    con[:, CC["bwd"]] = (r >= 40) & (r < 48)
    con[:, CC["eps"]] = EPS
    con[:, CC["half0"]] = r < 64
    con[:, CC["half1"]] = r >= 64
    for q in range(16):
        con[32 + q, CC["i16"] + q] = 1.0
    selm = np.zeros((48, 16, P), np.float32)
    selq = np.zeros((48, 8, P), np.float32)
    for q in range(16):
        selm[32 + q, q, :] = 1.0
        selq[32 + q, q // 2, 64 * (q % 2):64 * (q % 2) + 64] = 1.0
    return con, selm, selq


def tiles(w, cols, width):
    w = np.ascontiguousarray(w[:, cols] if cols is not None else w)
    return w.reshape(-1, P, w.shape[1] // width, width).transpose(2, 1, 0, 3)


def lay_out(i):
    f = {n: np.asarray(v) for n, v in i.items()}
    x = np.concatenate([f["x_prompt"][0], f["x_sample"][0]], 0)
    a = {"xT": x.T.reshape(KD, P, T).transpose(1, 0, 2)}
    a["cond"] = np.stack([f["c_ctx"], f["c"][0]], 1).reshape(KD, P, 2).transpose(1, 0, 2)
    a["w_ada"] = tiles(f["w_ada"][0], None, P)
    w = f["w_in"][0]
    at = {}
    n0 = 0
    for name, n in (("z", D), ("xbc", XBC), ("dt", 32), ("q", 512), ("k", 512), ("v", D), ("o", D), ("i", 16),
                    ("f", 16), ("g", 2 * D)):
        at[name] = w[:, n0:n0 + n]
        n0 += n
    zero = np.zeros((D, P), np.float32)
    ta = np.concatenate([at["dt"], at["f"], zero[:, 48:]], 1)
    tb = np.concatenate([zero[:, :32], at["i"], zero[:, 48:]], 1)
    a["w_in_ch"] = tiles(np.concatenate([ta, tb, at["xbc"], at["q"], at["k"], at["g"]], 1), None, P)
    a["w_in_tok"] = tiles(np.concatenate([at["z"], at["v"], at["o"]], 1), None, 512)
    a["w_o"] = np.concatenate([tiles(f[n][0], None, P) for n in ("w_o_ssd", "w_o_ml", "w_out")], 0)
    up = f["w_up"][0]
    a["w_up"] = np.stack([tiles(up[:, :FF], None, P), tiles(up[:, FF:], None, P)], 1).reshape(2 * FT, P, KD, P)
    a["w_down"] = f["w_down"][0].reshape(FT // 2, 2, P, D).transpose(0, 2, 1, 3)

    par = np.zeros((P, NPAR), np.float32)

    def put(name, v):
        v = v.reshape(-1, P).T
        par[:, PC[name]:PC[name] + v.shape[1]] = v

    for name in ("norm_mix", "b_ada", "norm_ffn", "ssd_norm", "ml_norm"):
        put(name, f[name][0])
    put("final_norm", f["final_norm"])
    put("conv_b", f["ssd_conv_b"][0])
    put("conv_w", f["ssd_conv_w"][0].reshape(3, XT, P).transpose(1, 0, 2))
    put("ffn_b", f["ffn_conv_b"][0])
    put("ffn_w", f["ffn_conv_w"][0].reshape(9, FT, P).transpose(1, 0, 2))
    par[0:32, PC["gate_bias"]] = f["ssd_dt_bias"][0].reshape(-1)
    par[32:48, PC["gate_bias"]] = f["ml_f_bias"][0].reshape(-1)
    par[32:48, PC["i_bias"]] = f["ml_i_bias"][0].reshape(-1)
    par[0:32, PC["a_log"]] = f["ssd_a_log"][0].reshape(-1)
    par[32:48, PC["m0"]] = f["state_mlstm_m"][0, 0].reshape(-1)
    a["params"] = par
    a["ssd_d"] = np.broadcast_to(np.repeat(f["ssd_d"][0], SP)[None], (P, D))
    s = f["state_ssd"][0, 0].reshape(2, 2, 2, HG, SP, SN).transpose(2, 5, 0, 1, 3, 4)
    a["s_ssd"] = s.reshape(P, 2, 512)
    cn = np.concatenate([f["state_mlstm_C"][0, 0], f["state_mlstm_n"][0, 0][:, :, None, :]], 2)
    a["s_ml"] = cn.reshape(2, 4, 2, DV1, DK).transpose(2, 4, 0, 1, 3).reshape(P, 2, 4, DV1)
    a["consts"], a["selm"], a["selq"] = constants()
    return {n: np.ascontiguousarray(v) for n, v in a.items()}


OUTS = {"y": (P, KD, T), "ssd": (P, 2, 512), "ml": (P, 2, 4, DV1), "m": (16, 1)}


def kernel(**inputs):
    import concourse.bacc as bacc
    from concourse.bass_utils import run_bass_kernel_spmd

    nc = bacc.Bacc("TRN2", target_bir_lowering=False, num_devices=1)
    arrays = {f"in_{n}": v for n, v in lay_out(inputs).items()}
    a = {n[3:]: nc.dram_tensor(n, v.shape, F32, kind="ExternalInput").ap() for n, v in arrays.items()}
    o = {n: nc.dram_tensor(f"out_{n}", s, F32, kind="ExternalOutput").ap() for n, s in OUTS.items()}
    build(nc, a, o)
    got = run_bass_kernel_spmd(nc, [arrays], core_ids=[0]).results[0]
    y = got["out_y"].transpose(2, 1, 0).reshape(T, D)
    s = got["out_ssd"].reshape(2, SN, 2, 2, HG, SP).transpose(2, 3, 0, 4, 5, 1).reshape(1, 1, 2, SH, SP, SN)
    cn = got["out_ml"].reshape(2, DK, 2, 4, DV1).transpose(2, 3, 0, 4, 1).reshape(1, 1, 2, MH, DV1, DK)
    c = np.ascontiguousarray
    return (c(y[None, :CTX]), c(y[None, CTX:]), c(s), c(cn[:, :, :, :, :DV]), c(cn[:, :, :, :, DV]),
            c(got["out_m"].reshape(1, 1, 2, MH)))
```

```python
from contextlib import ExitStack

import numpy as np

import concourse.bass as bass
from concourse import mybir

F32 = mybir.dt.float32
F32R = mybir.dt.float32r
BF16 = mybir.dt.bfloat16
ACT = mybir.ActivationFunctionType
ALU = mybir.AluOpType
AX = mybir.AxisListType

P = 128
D = 1024
KD = D // P
CTX = 128
LAT = 1024
T = CTX + LAT
C = 128
NC = T // C
EPS = 1e-6
SH, SP, SG, SN = 16, 64, 4, 64
HG = SH // SG
MH, DV, DK = 8, 128, 64
DV1 = DV + 1
XBC = 1536
XT = XBC // P
FF = 2816
FT = FF // P
GRID_W = 64
ROWS = LAT // GRID_W
NEG = -1.0e30
TB = 384
BLOCKS = tuple((b, b * TB, TB) for b in range(T // TB))
PARTS = ((0, slice(0, CTX), lambda x: x[:, 0, 0:CTX]),
         (1, slice(CTX, TB), lambda x: x[:, 0, CTX:TB]),
         (1, slice(TB, T), lambda x: x[:, 1:3, :]))

PC = {}
_at = 0
for _n, _w in (("norm_mix", KD), ("b_ada", 48), ("norm_ffn", KD), ("ssd_norm", KD), ("ml_norm", KD),
               ("conv_b", XT), ("conv_w", 3 * XT), ("ffn_b", FT), ("ffn_w", 9 * FT), ("final_norm", KD),
               ("gate_bias", 1), ("i_bias", 1), ("a_log", 1), ("m0", 1)):
    PC[_n] = _at
    _at += _w
NPAR = _at

CC = {}
_at = 0
for _n, _w in (("ident", P), ("le", P), ("gt", P), ("ge", P), ("lt", P), ("ones", P), ("row127", P),
               ("row0", P), ("sign", 1), ("fwd", 1), ("bwd", 1), ("eps", 1), ("half0", 1), ("half1", 1), ("i16", 16)):
    CC[_n] = _at
    _at += _w
NCON = _at

TA, TI, TX, TQ, TK, TG = 0, 1, 2, 14, 18, 22
NT = 38


def build(nc, a, o):
    scr = {
        "xbc": nc.dram_tensor("scr_xbc", [XT, P, T], F32).ap(),
        "qk": nc.dram_tensor("scr_qk", [8, P, T], F32).ap(),
        "gate": nc.dram_tensor("scr_gate", [16, P, T], F32).ap(),
        "zvo": nc.dram_tensor("scr_zvo", [3, NC, P, D], F32).ap(),
        "yn": nc.dram_tensor("scr_yn", [P, KD, T], F32).ap(),
        "hm": nc.dram_tensor("scr_hm", [P, KD, T], F32).ap(),
    }
    with ExitStack() as ctx:
        o = {**o, **{f"{n}_out": nc.alloc_semaphore(f"{n}_out") for n in ("ssd", "ml", "m", "y0", "y1")}}
        par = ctx.enter_context(nc.sbuf_tensor("par", [P, NPAR], F32))
        mod = ctx.enter_context(nc.sbuf_tensor("mod", [P, 48, 2], F32))
        k = {"par": par, "mod": mod}
        with ExitStack() as mix:
            k["con"] = mix.enter_context(nc.sbuf_tensor("con", [P, NCON], F32))
            g = {n: mix.enter_context(nc.sbuf_tensor(n, [P, NC, w], F32)) for n, w in
                 (("dt_ig", 48), ("dec", 48), ("ecum", 48), ("eend", 48), ("em", 16), ("dbc", 48))}
            g["negm"] = mix.enter_context(nc.sbuf_tensor("negm", [48, T], F32))
            with ExitStack() as proj:
                cond = proj.enter_context(nc.sbuf_tensor("cond", [P, KD, 2], F32))
                uh = proj.enter_context(nc.sbuf_tensor("uh", [P, KD, T], F32R))
                ul = proj.enter_context(nc.sbuf_tensor("ul", [P, KD, T], F32R))
                norm_mix(nc, a, k, cond, uh, ul)
                proj_ch(nc, a, k, g, cond, uh, ul, scr, o)
                proj_tok(nc, a, uh, ul, scr)
            ssd(nc, a, k, g, scr, o)
            mlstm(nc, a, k, g, scr, o)
        h = ctx.enter_context(nc.sbuf_tensor("h", [P, KD, T], F32))
        with ExitStack() as ff:
            uh = ff.enter_context(nc.sbuf_tensor("uh2", [P, KD, T], F32R))
            ul = ff.enter_context(nc.sbuf_tensor("ul2", [P, KD, T], F32R))
            out_proj(nc, a, k, h, uh, ul, scr)
            norm_ffn(nc, a, k, h, uh, ul)
            ffn(nc, a, k, h, uh, ul)
        final_norm(nc, a, k, h, o)


def col(k, name, i=0, n=1, rows=slice(0, P)):
    return k["par"][rows, PC[name] + i:PC[name] + i + n]


def const(k, name, rows=slice(0, P), n=None):
    n = n or (P if CC[name] < 8 * P else 1)
    return k["con"][rows, CC[name]:CC[name] + n]


class Chain:

    def __init__(self, eng, sem):
        self.eng, self.sem, self.n = eng, sem, 0

    def __call__(self, ins):
        self.n += 1
        ins.then_inc(self.sem, 1)
        self.eng.wait_ge(self.sem, self.n)


def open_sems(nc, ctx, *names):
    sems = [nc.alloc_semaphore(n) for n in names]
    ctx.callback(clear_sems, nc, sems)
    return sems


def clear_sems(nc, sems):
    nc.clear_and_free_semaphores(sems)
    nc.all_engine_barrier()


def spread(x, shape):
    return x.to_broadcast(shape)


def blocks(x):
    return x.rearrange("p (b n) -> p b n", n=TB)


def part(x, t):
    x = x[:, t]
    return blocks(x) if t.stop == T else x


def split_product(pe, acc, wh, wl, ah, al, kt, last_k, first=True):
    ins = None
    for w, act, s, e in ((wh, ah, True, False), (wh, al, False, False), (wl, ah, False, True)):
        for bank, t0, n in BLOCKS:
            ins = pe.matmul(acc[:, bank, 0:n], w, act[:, kt, t0:t0 + n],
                            start=(first and s), stop=(last_k and e))
    return ins


def norm_mix(nc, a, k, cond, uh, ul):
    with ExitStack() as ctx:
        RING = 9
        x = ctx.enter_context(nc.sbuf_tensor("x", [P, KD, T], F32))
        wa = ctx.enter_context(nc.sbuf_tensor("wa", [P, RING, KD, P], F32))
        sq = ctx.enter_context(nc.sbuf_tensor("sq", [P, 2, T], F32))
        u = ctx.enter_context(nc.sbuf_tensor("u", [P, 3, T], F32))
        rstd = ctx.enter_context(nc.sbuf_tensor("rstd", [P, T], F32))
        scl = ctx.enter_context(nc.sbuf_tensor("scl", [P, KD, 2], F32))
        craw = ctx.enter_context(nc.sbuf_tensor("craw", [P, KD, 2], F32))
        ss_bank = ctx.enter_context(nc.psum_tensor("ss", [P, 3, 512], F32))
        ss = ss_bank[:, :, 0:TB]
        pmod = ctx.enter_context(nc.psum_tensor("pmod", [P, 48, 2], F32))
        (par_in, con_in, cond_in, sq_ready, sq_used, ss_done, log, rstd_ready, mod_done, cond_ready,
         scl_ready, xn_ready, u_ready, hi_done, lo_v, lo_p, chain) = open_sems(
            nc, ctx, "par_in", "con_in", "cond_in", "sq_ready", "sq_used", "ss_done", "log", "rstd_ready",
            "mod_done", "cond_ready", "scl_ready", "xn_ready", "u_ready", "hi_done", "lo_v", "lo_p", "chain_nm")
        x_in = open_sems(nc, ctx, *[f"x_in{i}" for i in range(KD)])
        wa_in = open_sems(nc, ctx, *[f"wa_in{i}" for i in range(RING)])
        mod_used, = open_sems(nc, ctx, "mod_used")
        block = ctx.enter_context(nc.Block())
        NA = 16
        PART = ((0, slice(0, CTX)), (1, slice(CTX, T)))

        def low_part(eng, i):
            eng.wait_ge(hi_done, i + 1)
            return eng.tensor_tensor(ul[:, i, :], u[:, i % 3, :], uh[:, i, :].bitcast(F32), ALU.subtract)

        @block.sync
        def _(sp):
            sp.dma_start(craw[:, :, :], a["cond"]).then_inc(cond_in, 16)
            sp.dma_start(k["con"][:, :], a["consts"]).then_inc(con_in, 16)
            sp.dma_start(k["par"][:, :], a["params"]).then_inc(par_in, 16)
            for i in range(KD):
                sp.dma_start(x[:, i, :], a["xT"][:, i, :]).then_inc(x_in[i], 16)
            for j in range(NA):
                if j >= RING:
                    sp.wait_ge(mod_done, j - RING + 1)
                sp.dma_start(wa[:, j % RING, :, :], a["w_ada"][j]).then_inc(wa_in[j % RING], 16)

        @block.scalar
        def _(act):
            act.wait_ge(cond_in, 16)
            act.activation(cond[:, :, :], craw[:, :, :], ACT.Silu).then_inc(cond_ready, 1)
            for i in range(KD):
                act.wait_ge(x_in[i], 16)
                if i >= 2:
                    act.wait_ge(sq_used, i - 1)
                act.activation(sq[:, i % 2, :], x[:, i, :], ACT.Square).then_inc(sq_ready, 1)
            act.wait_ge(ss_done, 1)
            act.wait_ge(con_in, 16)
            act.activation(blocks(rstd[:, :]), ss, ACT.Ln, bias=const(k, "eps"), scale=1.0 / D).then_inc(log, 1)
            act.wait_ge(log, 1)
            act.activation(rstd[:, :], rstd[:, :], ACT.Exp, scale=-0.5).then_inc(rstd_ready, 1)
            act.wait_ge(scl_ready, 2)
            for i in range(KD):
                act.wait_ge(xn_ready, i + 1)
                for s, t in PART:
                    m = act.activation(uh[:, i, t], x[:, i, t], ACT.Identity, bias=k["mod"][:, i, s:s + 1],
                                       scale=scl[:, i, s:s + 1])
                m.then_inc(hi_done, 1)

        @block.tensor
        def _(pe):
            pe.wait_ge(con_in, 16)
            for i in range(KD):
                pe.wait_ge(sq_ready, i + 1)
                for bank, t0, n in BLOCKS:
                    m = pe.matmul(ss[:, bank, 0:n], const(k, "ones"), sq[:, i % 2, t0:t0 + n],
                                  start=(i == 0), stop=(i == KD - 1))
                m.then_inc(sq_used, 1)
                if i == KD - 1:
                    pe.wait_ge(sq_used, KD)
                    m = pe.matmul(pmod[:, 47, :], const(k, "ones"), k["con"][:, 0:2], start=True, stop=True)
                    m.then_inc(ss_done, 1)
            pe.wait_ge(cond_ready, 1)
            for j in range(NA):
                pe.wait_ge(wa_in[j % RING], 16 * (j // RING + 1))
                for i in range(KD):
                    m = pe.matmul(pmod[:, j, :], wa[:, j % RING, i, :], cond[:, i, :],
                                  start=(i == 0), stop=(i == KD - 1))
                m.then_inc(mod_done, 1)

        @block.vector
        def _(dve):
            link = Chain(dve, chain)
            dve.wait_ge(rstd_ready, 1)
            for i in range(KD):
                dve.tensor_tensor(x[:, i, :], x[:, i, :], rstd[:, :], ALU.mult).then_inc(xn_ready, 1)
            dve.wait_ge(par_in, 16)
            dve.wait_ge(mod_done, NA)
            link(dve.tensor_tensor(k["mod"][:, 0:NA, :], pmod[:, 0:NA, :],
                                   spread(col(k, "b_ada", 0, NA).unsqueeze(2), [P, NA, 2]), ALU.add))
            for s in range(2):
                dve.scalar_tensor_tensor(out=scl[:, :, s], in0=k["mod"][:, KD:2 * KD, s], scalar=1.0,
                                         in1=col(k, "norm_mix", 0, KD), op0=ALU.add,
                                         op1=ALU.mult).then_inc(scl_ready, 1)
            dve.wait_ge(scl_ready, 2)
            dve.wait_ge(xn_ready, KD)

            def modulated(i):
                if i >= 3:
                    dve.wait_ge(*((lo_p, (i - 3) // 2 + 1) if (i - 3) % 2 else (lo_v, (i - 3) // 2 + 1)))
                for s, t in PART:
                    m = dve.tensor_scalar(u[:, i % 3, t], x[:, i, t], scl[:, i, s:s + 1], k["mod"][:, i, s:s + 1],
                                          ALU.mult, ALU.add)
                m.then_inc(u_ready, 1)

            modulated(0)
            for i in range(KD):
                if i + 1 < KD:
                    modulated(i + 1)
                if i % 2 == 0:
                    dve.wait_ge(u_ready, i + 1)
                    low_part(dve, i).then_inc(lo_v, 1)
            dve.wait_ge(lo_v, KD // 2)

        @block.gpsimd
        def _(pool):
            for i in range(1, KD, 2):
                pool.wait_ge(u_ready, i + 1)
                low_part(pool, i).then_inc(lo_p, 1)
            pool.wait_ge(lo_p, KD // 2)


def proj_ch(nc, a, k, g, cond, uh, ul, scr, o):
    with ExitStack() as ctx:
        RING, ORING, PADT = 4, 3, T + 4
        raw = ctx.enter_context(nc.sbuf_tensor("raw", [P, RING, KD, P], F32))
        wh = ctx.enter_context(nc.sbuf_tensor("wh", [P, 2, KD, P], F32R))
        wl = ctx.enter_context(nc.sbuf_tensor("wl", [P, 2, KD, P], F32R))
        pad = ctx.enter_context(nc.sbuf_tensor("pad", [P, 2, PADT], F32))
        cv = ctx.enter_context(nc.sbuf_tensor("cv", [P, 2, PADT], F32))
        ob = ctx.enter_context(nc.sbuf_tensor("ob", [P, ORING, T], F32))
        acc = [ctx.enter_context(nc.psum_tensor(f"acc{i}", [P, 3, 512], F32))[:, :, 0:TB] for i in range(2)]
        pmod = ctx.enter_context(nc.psum_tensor("pmod2", [P, 48, 2], F32))
        ML = slice(32, 48)
        row = {n: ctx.enter_context(nc.sbuf_tensor("row_" + n, [48, T], F32)) for n in
               ("a", "b", "e", "u", "l", "sp", "w")}
        row["x"] = row["g2"] = row["a"]
        row["d"], row["mf"], row["mb"], row["mm"] = row["b"], row["e"], row["u"], row["l"]
        pm = ctx.enter_context(nc.sbuf_tensor("g_pm", [48, 2, NC], F32))
        pp = ctx.enter_context(nc.sbuf_tensor("g_pp", [48, NC], F32))
        mn = ctx.enter_context(nc.sbuf_tensor("g_mn", [48, NC], F32))
        ac = ctx.enter_context(nc.sbuf_tensor("g_ac", [48, 1], F32))
        end = ctx.enter_context(nc.sbuf_tensor("g_end", [P, NC, 48], F32))
        pg = ctx.enter_context(nc.psum_tensor("pg", [P, 512], F32))
        tok = pg[:, 0:NC * 48].rearrange("p (c r) -> p c r", c=NC)
        tok_m = pg[:, 0:NC * 16].rearrange("p (c r) -> p c r", c=NC)
        GATE_STEPS = {24 + n: name for n, name in enumerate(("dt_ig", "dec", "em", "ecum", "end", "dbc"))}
        (hi_done, lo_done, tile_done, evac_done, mod_done, pad_zero, pad_ready, conv_done, silu_done,
         ob_ready, chain) = open_sems(
            nc, ctx, "w_hi_done", "w_lo_done", "tile_done", "evac_done", "mod2_done", "pad_zero", "pad_ready",
            "conv_done", "silu_done", "ob_ready", "chain_pc")
        chain_rows, ex, u1, ln_in, ln_out, a_exp, rows_done, tok_done, tok_out, ends_done = open_sems(
            nc, ctx, "chain_rows", "g_exp", "g_u1", "g_ln_in", "g_ln_out", "g_aexp", "rows_done", "g_tok_done",
            "g_tok_out", "g_ends_done")
        raw_in = open_sems(nc, ctx, *[f"raw_in{i}" for i in range(RING)])
        stored = open_sems(nc, ctx, *[f"stored{i}" for i in range(ORING)])
        block = ctx.enter_context(nc.Block())

        jobs = []
        for i in range(NT):
            jobs.append(("w", i))
            if i < 32:
                jobs.append(("ada", 16 + i))
        slot = {job: n for n, job in enumerate(jobs)}
        outs = [i for i in range(NT) if i >= TX]

        def out_slot(i):
            return (i - TX) % ORING, (i - TX) // ORING

        @block.sync
        def _(sp):
            for n, (kind, i) in enumerate(jobs):
                if n >= RING:
                    was, j = jobs[n - RING]
                    if was == "w":
                        sp.wait_ge(hi_done, j + 1)
                        sp.wait_ge(lo_done, j + 1)
                    else:
                        sp.wait_ge(mod_done, j - 15)
                src = a["w_in_ch"][i] if kind == "w" else a["w_ada"][i]
                sp.dma_start(raw[:, n % RING, :, :], src).then_inc(raw_in[n % RING], 16)
            sp.wait_ge(rows_done, 1)
            with nc.allow_non_contiguous_dma(reason="eight single values"):
                sp.dma_start(o["m"][0:8, :], row["mf"][32:40, CTX - 1:CTX]).then_inc(o["m_out"], 16)
                sp.dma_start(o["m"][8:16, :], row["mb"][40:48, 0:1]).then_inc(o["m_out"], 16)
            sp.wait_ge(o["m_out"], 32)

        def arrived(eng, job):
            n = slot[job]
            eng.wait_ge(raw_in[n % RING], 16 * (n // RING + 1))
            return raw[:, n % RING, :, :]

        @block.tensor
        def _(pe):
            idn, i16 = const(k, "ident", slice(0, 48), 48), k["con"][ML, CC["i16"]:CC["i16"] + 16]
            quarters = (slice(0, 16), slice(16, 32), slice(32, 40), slice(40, 48))

            def gate_step(i):
                name, n = GATE_STEPS[i], i - min(GATE_STEPS)
                if n == 0:
                    pe.wait_ge(rows_done, 1)
                else:
                    pe.wait_ge(tok_out, n)
                for c in range(NC):
                    t = slice(c * C, (c + 1) * C)
                    if name in ("dt_ig", "dec"):
                        m = pe.transpose(tok[:, c, :], row["sp" if name == "dt_ig" else "g2"][:, t], idn)
                    elif name == "em":
                        m = pe.transpose(tok_m[:, c, :], g["negm"][ML, t], i16)
                if name in ("ecum", "end"):
                    masks, own = (("le", "ge"), "d") if name == "ecum" else (("gt", "lt"), "w")
                    for j, cols in enumerate(quarters):
                        pe.matmul(tok[:, :, cols], const(k, masks[j % 2]), g["dec"][:, :, cols], start=(j == 0),
                                  stop=False, skip_group_check=True)
                    for c in range(NC):
                        m = pe.matmul(tok[:, c, 32:48], row[own][ML, c * C:(c + 1) * C], i16, start=False,
                                      stop=(c == NC - 1), skip_group_check=True)
                if name == "dbc":
                    for j, cols in enumerate(quarters):
                        m = pe.matmul(tok[:, :, cols], const(k, ("row127", "row0")[j % 2]), g["ecum"][:, :, cols],
                                      start=(j == 0), stop=(j == 3), skip_group_check=True)
                m.then_inc(tok_done, 1)

            for kind, i in jobs:
                if kind == "w":
                    pe.wait_ge(hi_done, i + 1)
                    pe.wait_ge(lo_done, i + 1)
                    if i >= 2:
                        pe.wait_ge(evac_done, i - 1)
                    for kt in range(KD):
                        m = split_product(pe, acc[i % 2], wh[:, i % 2, kt, :], wl[:, i % 2, kt, :], uh, ul, kt,
                                          kt == KD - 1, kt == 0)
                    m.then_inc(tile_done, 1)
                    if i in GATE_STEPS:
                        gate_step(i)
                else:
                    w = arrived(pe, (kind, i))
                    for kt in range(KD):
                        m = pe.matmul(pmod[:, i, :], w[:, kt, :], cond[:, kt, :], start=(kt == 0),
                                      stop=(kt == KD - 1))
                    m.then_inc(mod_done, 1)

        @block.scalar
        def _(act):
            def high(i):
                w = arrived(act, ("w", i))
                if i >= 2:
                    act.wait_ge(tile_done, i - 1)
                act.activation(wh[:, i % 2, :, :], w, ACT.Copy).then_inc(hi_done, 1)

            def out_free(i):
                s, n = out_slot(i)
                if n:
                    act.wait_ge(stored[s], 16 * n)

            def silu(i):
                act.wait_ge(conv_done, i - TX + 1)
                out_free(i)
                s, _ = out_slot(i)
                b = col(k, "conv_b", i - TX)
                act.activation(ob[:, s, 0:CTX], cv[:, i % 2, 1:1 + CTX], ACT.Silu, bias=b)
                act.activation(ob[:, s, CTX:T], cv[:, i % 2, CTX + 3:T + 3], ACT.Silu,
                               bias=b).then_inc(ob_ready, 1)

            act.activation(ac[0:32, :], col(k, "a_log", rows=slice(0, 32)), ACT.Exp).then_inc(a_exp, 1)
            high(0)
            for i in range(NT):
                if i + 1 < NT:
                    high(i + 1)
                if i == TX + 1:
                    act.wait_ge(ex, 1)
                    act.activation(row["e"][:, :], row["e"][:, :], ACT.Exp, scale=-1.0).then_inc(u1, 1)
                if i == TX + 3:
                    act.wait_ge(ln_in, 1)
                    act.activation(row["l"][:, :], row["u"][:, :], ACT.Ln).then_inc(ln_out, 1)
                step = GATE_STEPS.get(i - 1)
                if step in ("em", "ecum", "end"):
                    act.wait_ge(tok_done, i - min(GATE_STEPS))
                    dst = end if step == "end" else g[step]
                    act.activation(dst[:, :, :], tok_m if step == "em" else tok, ACT.Exp).then_inc(tok_out, 1)
                act.wait_ge(tile_done, i + 1)
                if i < TX:
                    dst = row["a" if i == TA else "b"]
                    act.activation(blocks(dst[:, :]), acc[i % 2][0:48, :, :], ACT.Copy).then_inc(evac_done, 1)
                elif i < TQ:
                    if i == TX:
                        act.wait_ge(pad_zero, 1)
                    if i >= TX + 2:
                        act.wait_ge(conv_done, i - TX - 1)
                    for s, t, view in PARTS:
                        line = pad[:, i % 2, 1 + 2 * s:1 + 2 * s + T]
                        act.activation(part(line, t), view(acc[i % 2]), ACT.Copy).then_inc(pad_ready, 1)
                    act.wait_ge(pad_ready, 3 * (i - TX) + 3)
                    act.sem_inc(evac_done, 1)
                    if i > TX:
                        silu(i - 1)
                else:
                    if i == TQ:
                        silu(i - 1)
                    out_free(i)
                    s, _ = out_slot(i)
                    fn = ACT.Sigmoid if i >= TG else ACT.Copy
                    sc = DK ** -0.5 if i < TK else 1.0
                    act.activation(blocks(ob[:, s, :]), acc[i % 2], fn, scale=sc).then_inc(ob_ready, 1)
                    act.wait_ge(ob_ready, i - TX + 1)
                    act.sem_inc(evac_done, 1)

        @block.vector
        def _(dve):
            link = Chain(dve, chain)
            dve.memset(pad[:, :, :], 0.0).then_inc(pad_zero, 1)

            def low(i):
                w = arrived(dve, ("w", i))
                dve.wait_ge(hi_done, i + 1)
                dve.tensor_tensor(wl[:, i % 2, :, :], w, wh[:, i % 2, :, :].bitcast(F32),
                                  ALU.subtract).then_inc(lo_done, 1)

            def conv(i):
                dve.wait_ge(pad_ready, 3 * (i - TX) + 3)
                if i >= TX + 2:
                    dve.wait_ge(ob_ready, i - TX - 1)
                x, y = pad[:, i % 2, :], cv[:, i % 2, 1:PADT - 1]
                n = PADT - 2
                w = [col(k, "conv_w", 3 * (i - TX) + j) for j in range(3)]
                link(dve.tensor_scalar(y, x[:, 1:1 + n], w[1], None, ALU.mult))
                link(dve.scalar_tensor_tensor(out=y, in0=x[:, 0:n], scalar=w[0], in1=y, op0=ALU.mult, op1=ALU.add))
                dve.scalar_tensor_tensor(out=y, in0=x[:, 2:2 + n], scalar=w[2], in1=y, op0=ALU.mult,
                                         op1=ALU.add).then_inc(conv_done, 1)

            rlink = Chain(dve, chain_rows)

            def gate_rows():
                X, E, U, L, SPR, G2 = (row[n][:, :] for n in ("x", "e", "u", "l", "sp", "g2"))
                sgn = const(k, "sign", slice(0, 48))
                rlink(dve.memset(pm[:, :, :], 0.0))
                dve.wait_ge(evac_done, 2)
                rlink(dve.tensor_scalar(X, row["a"][:, :], col(k, "gate_bias", rows=slice(0, 48)), sgn,
                                        ALU.add, ALU.mult))
                dve.scalar_tensor_tensor(out=E, in0=X, scalar=-1.0, in1=X, op0=ALU.mult, op1=ALU.max).then_inc(ex, 1)
                yield
                yield
                dve.wait_ge(u1, 1)
                dve.tensor_scalar(U, E, 1.0, None, ALU.add).then_inc(ln_in, 1)
                yield
                yield
                dve.wait_ge(ln_out, 1)
                rlink(dve.scalar_tensor_tensor(out=SPR, in0=U, scalar=-1.0, in1=E, op0=ALU.add, op1=ALU.subtract))
                rlink(dve.reciprocal(U, U))
                yield
                rlink(dve.tensor_tensor(SPR, SPR, U, ALU.mult))
                rlink(dve.tensor_tensor(SPR, L, SPR, ALU.subtract))
                rlink(dve.scalar_tensor_tensor(out=SPR, in0=X, scalar=0.0, in1=SPR, op0=ALU.max, op1=ALU.add))
                yield
                dve.wait_ge(a_exp, 1)
                rlink(dve.tensor_scalar(G2[0:32, :], SPR[0:32, :], ac[0:32, :], -1.0, ALU.mult, ALU.mult))
                rlink(dve.tensor_scalar(G2[ML, :], SPR[ML, :], -1.0, None, ALU.mult))
                rlink(dve.tensor_scalar(SPR[ML, :], row["b"][ML, :], col(k, "i_bias", rows=ML), None, ALU.add))
                yield
                ig, lf = SPR[ML, :], G2[ML, :]
                MF, MB = row["mf"][ML, :], row["mb"][ML, :]
                m0 = col(k, "m0", rows=ML)
                for dst, st in ((MF, 1), (MB, -1)):
                    for t0, t1, init in ((0, CTX, 0.0), (CTX, T, m0)):
                        rlink(dve.tensor_tensor_scan(dst[:, t0:t1][:, ::st], lf[:, t0:t1][:, ::st],
                                                     ig[:, t0:t1][:, ::st], init, ALU.add, ALU.max))
                    yield
                fw, bw = const(k, "fwd", ML), const(k, "bwd", ML)
                rlink(dve.tensor_copy(pm[ML, 0, 1:2], m0))
                rlink(dve.tensor_copy(pm[ML, 1, NC - 1:NC], m0))
                rlink(dve.tensor_copy(pm[ML, 0, 2:NC], MF[:, 2 * C - 1:T - C:C]))
                rlink(dve.tensor_copy(pm[ML, 1, 1:NC - 1], MB[:, 2 * C:T:C]))

                def by_direction(dst, f, b):
                    rlink(dve.tensor_scalar(dst, f, fw, None, ALU.mult))
                    rlink(dve.scalar_tensor_tensor(out=dst, in0=b, scalar=bw, in1=dst, op0=ALU.mult, op1=ALU.add))

                MM = row["mm"][ML, :]
                by_direction(MM, MF, MB)
                yield
                by_direction(pp[ML, :], pm[ML, 0, :], pm[ML, 1, :])
                by_direction(mn[ML, :], MF[:, C - 1:T:C], MB[:, 0:T:C])
                cs = [16, NC, C]
                rlink(dve.tensor_tensor(row["d"][ML, :].rearrange("p (c t) -> p c t", c=NC),
                                        spread(pp[ML, :].unsqueeze(2), cs),
                                        MM.rearrange("p (c t) -> p c t", c=NC), ALU.subtract))
                yield
                rlink(dve.tensor_tensor(row["w"][ML, :].rearrange("p (c t) -> p c t", c=NC),
                                        ig.rearrange("p (c t) -> p c t", c=NC),
                                        spread(mn[ML, :].unsqueeze(2), cs), ALU.subtract))
                dve.tensor_scalar(g["negm"][ML, :], MM, -1.0, None, ALU.mult).then_inc(rows_done, 1)

            rows_work = gate_rows()
            low(0)
            for i in range(NT):
                if i + 1 < NT:
                    low(i + 1)
                if TX <= i < TQ:
                    conv(i)
                if i >= TX:
                    next(rows_work, None)
                step = GATE_STEPS.get(i - 1)
                if step in ("dt_ig", "dec", "dbc"):
                    dve.wait_ge(tok_done, i - min(GATE_STEPS))
                    dve.tensor_copy(g[step][:, :, :], tok).then_inc(tok_out, 1)
                if step == "dbc":
                    dve.wait_ge(tok_out, len(GATE_STEPS) - 1)
                    dve.tensor_copy(g["eend"][:, :, 32:48], end[:, :, 32:48]).then_inc(ends_done, 1)
                    dve.tensor_tensor(g["eend"][:, :, 0:32], end[:, :, 0:32], g["dt_ig"][:, :, 0:32],
                                      ALU.mult).then_inc(ends_done, 1)
            dve.wait_ge(ends_done, 2)
            dve.wait_ge(tok_out, len(GATE_STEPS))
            dve.wait_ge(mod_done, 32)
            dve.tensor_tensor(k["mod"][:, 16:48, :], pmod[:, 16:48, :],
                              spread(col(k, "b_ada", 16, 32).unsqueeze(2), [P, 32, 2]), ALU.add).then_inc(chain, 1)
            dve.wait_ge(chain, link.n + 1)

        @block.gpsimd
        def _(pool):
            for n, i in enumerate(outs):
                s, _ = out_slot(i)
                pool.wait_ge(ob_ready, n + 1)
                if i < TQ:
                    dst = scr["xbc"][i - TX]
                elif i < TG:
                    dst = scr["qk"][i - TQ]
                else:
                    dst = scr["gate"][i - TG]
                pool.dma_start(dst, ob[:, s, :]).then_inc(stored[s], 16)
            for s in range(ORING):
                pool.wait_ge(stored[s], 16 * len([i for i in outs if out_slot(i)[0] == s]))


def proj_tok(nc, a, uh, ul, scr):
    with ExitStack() as ctx:
        NB, W, OR = 6, 512, 4
        raw = ctx.enter_context(nc.sbuf_tensor("rawn", [P, 2, KD, W], F32))
        wh = ctx.enter_context(nc.sbuf_tensor("whn", [P, 2, KD, W], F32R))
        wl = ctx.enter_context(nc.sbuf_tensor("wln", [P, 2, KD, W], F32R))
        ob = ctx.enter_context(nc.sbuf_tensor("obn", [P, OR, W], F32))
        NP = 8
        acc = ctx.enter_context(nc.psum_tensor("accn", [P, NP, W], F32))
        hi_done, lo_done, blk_done, tok_done, ob_ready = open_sems(
            nc, ctx, "n_hi_done", "n_lo_done", "blk_done", "tok_done", "n_ob_ready")
        raw_in = open_sems(nc, ctx, *[f"n_raw_in{i}" for i in range(2)])
        stored = open_sems(nc, ctx, *[f"n_stored{i}" for i in range(OR)])
        block = ctx.enter_context(nc.Block())
        H = KD // 2

        @block.sync
        def _(sp):
            for b in range(NB):
                if b >= 2:
                    sp.wait_ge(hi_done, 2 * (b - 1))
                    sp.wait_ge(lo_done, 2 * (b - 1))
                sp.dma_start(raw[:, b % 2, :, :], a["w_in_tok"][b]).then_inc(raw_in[b % 2], 16)

        @block.tensor
        def _(pe):
            for b in range(NB):
                for c in range(NC):
                    n = b * NC + c
                    if n >= NP:
                        pe.wait_ge(ob_ready, n - NP + 1)
                    for kt in range(KD):
                        if c == 0 and kt % H == 0:
                            pe.wait_ge(hi_done, 2 * b + kt // H + 1)
                            pe.wait_ge(lo_done, 2 * b + kt // H + 1)
                        for q, (x, w) in enumerate(((uh, wh), (uh, wl), (ul, wh))):
                            m = pe.matmul(acc[:, n % NP, :], x[:, kt, c * C:(c + 1) * C], w[:, b % 2, kt, :],
                                          start=(kt == 0 and q == 0), stop=(kt == KD - 1 and q == 2))
                    m.then_inc(tok_done, 1)

        @block.scalar
        def _(act):
            def high(b):
                act.wait_ge(raw_in[b % 2], 16 * (b // 2 + 1))
                if b >= 2:
                    act.wait_ge(tok_done, NC * (b - 1))
                for j in range(2):
                    act.activation(wh[:, b % 2, j * H:(j + 1) * H, :], raw[:, b % 2, j * H:(j + 1) * H, :],
                                   ACT.Copy).then_inc(hi_done, 1)

            high(0)
            for b in range(NB):
                if b + 1 < NB:
                    high(b + 1)
                fn = (ACT.Silu, ACT.Copy, ACT.Sigmoid)[b // 2]
                for c in range(NC):
                    n = b * NC + c
                    act.wait_ge(tok_done, n + 1)
                    if n >= OR:
                        act.wait_ge(stored[n % OR], 16 * (n // OR))
                    act.activation(ob[:, n % OR, :], acc[:, n % NP, :], fn).then_inc(ob_ready, 1)

        @block.vector
        def _(dve):
            for b in range(NB):
                for j in range(2):
                    dve.wait_ge(hi_done, 2 * b + j + 1)
                    dve.tensor_tensor(wl[:, b % 2, j * H:(j + 1) * H, :], raw[:, b % 2, j * H:(j + 1) * H, :],
                                      wh[:, b % 2, j * H:(j + 1) * H, :].bitcast(F32),
                                      ALU.subtract).then_inc(lo_done, 1)

        @block.gpsimd
        def _(pool):
            for n in range(NB * NC):
                b, c = n // NC, n % NC
                pool.wait_ge(ob_ready, n + 1)
                dst = scr["zvo"][b // 2][c][:, (b % 2) * W:(b % 2 + 1) * W]
                pool.dma_start(dst, ob[:, n % OR, :]).then_inc(stored[n % OR], 16)
            for s in range(OR):
                pool.wait_ge(stored[s], 16 * len(range(s, NB * NC, OR)))


def head_decay(g, d, c, gp):
    r = slice(64 * gp, 64 * gp + 64)
    v = g["dbc"][r, c, d * SH:(d + 1) * SH].rearrange("p (a b h) -> p a b h", a=2, b=2)[:, :, gp, :]
    return spread(v.unsqueeze(3), [64, 2, HG, SP])


def state_view(s, gp):
    return s[64 * gp:64 * gp + 64, :].rearrange("p (a h x) -> p a h x", a=2, h=HG)


def ssd(nc, a, k, g, scr, o):
    with ExitStack() as ctx:
        x = ctx.enter_context(nc.sbuf_tensor("x_tok", [P, NC, D], F32))
        b = ctx.enter_context(nc.sbuf_tensor("b_tok", [P, NC, SG * SN], F32))
        snap = ctx.enter_context(nc.sbuf_tensor("snap", [P, NC - 1, 512], F32))
        ssd_backward(nc, a, k, g, scr, o, x, b, snap)
        ssd_forward(nc, a, k, g, scr, x, b, snap)


def ssd_backward(nc, a, k, g, scr, o, x, b, snap):
    with ExitStack() as ctx:
        xc = ctx.enter_context(nc.sbuf_tensor("xc", [P, 2, 10, C], F32))
        xw = ctx.enter_context(nc.sbuf_tensor("xw", [P, 2, D], F32))
        fin = ctx.enter_context(nc.sbuf_tensor("fin", [P, 2, 512], F32))
        tr = [ctx.enter_context(nc.psum_tensor(f"tr{i}", [P, 3, 512], F32)) for i in range(2)]
        st = ctx.enter_context(nc.psum_tensor("st", [P, 2, 512], F32))
        tr_done, x_tok, b_tok, xw_ready, st_done, st_used, s0_in, chain = open_sems(
            nc, ctx, "tr_done", "x_tokd", "b_tokd", "xw_ready", "st_done", "st_used", "s0_in", "chain_sb")
        xc_in = open_sems(nc, ctx, "xc_in0", "xc_in1")
        block = ctx.enter_context(nc.Block())
        order = [0] + list(range(NC - 1, 0, -1))
        jobs = [(0, 0), (0, 1)] + [(c, 1) for c in range(NC - 1, 1, -1)]
        at = {c: n for n, c in enumerate(order)}

        @block.sync
        def _(sp):
            sp.dma_start(snap[:, NC - 2, :], a["s_ssd"][:, 1, :]).then_inc(s0_in, 16)
            for n, c in enumerate(order):
                if n >= 2:
                    sp.wait_ge(tr_done, n - 1)
                sp.dma_start(xc[:, n % 2, :, :],
                             scr["xbc"][0:10, :, c * C:(c + 1) * C].rearrange("i p t -> p i t")
                             ).then_inc(xc_in[n % 2], 16)
            sp.wait_ge(st_used, 2)
            sp.dma_start(o["ssd"], fin[:, :, :]).then_inc(o["ssd_out"], 16)
            sp.wait_ge(o["ssd_out"], 16)

        @block.tensor
        def _(pe):
            def turn(n):
                pe.wait_ge(xc_in[n % 2], 16 * (n // 2 + 1))
                if n >= 2:
                    pe.wait_ge(x_tok, n - 1)
                    pe.wait_ge(b_tok, n - 1)
                for i in range(10):
                    m = pe.transpose(tr[n % 2][:, i // 4, (i % 4) * P:(i % 4 + 1) * P], xc[:, n % 2, i, :],
                                     const(k, "ident"))
                m.then_inc(tr_done, 1)

            def state(n):
                c, d = jobs[n]
                pe.wait_ge(xw_ready, n + 1)
                pe.wait_ge(b_tok, at[c] + 1)
                if n >= 2:
                    pe.wait_ge(st_used, n - 1)
                for q in range(SG):
                    m = pe.matmul(st[64 * (q % 2):64 * (q % 2) + 64, n % 2, 256 * (q // 2):256 * (q // 2) + 256],
                                  b[:, c, q * SN:(q + 1) * SN], xw[:, n % 2, q * 256:(q + 1) * 256],
                                  start=True, stop=True, skip_group_check=True)
                m.then_inc(st_done, 1)

            turn(0)
            turn(1)
            state(0)
            state(1)
            for n in range(2, NC):
                turn(n)
                state(n)

        @block.scalar
        def _(act):
            for n, c in enumerate(order):
                act.wait_ge(tr_done, n + 1)
                act.activation(x[:, c, :].rearrange("p (b n) -> p b n", b=2), tr[n % 2][:, 0:2, :],
                               ACT.Copy).then_inc(x_tok, 1)

        @block.gpsimd
        def _(pool):
            for n, (c, d) in enumerate(jobs):
                pool.wait_ge(x_tok, at[c] + 1)
                if n >= 2:
                    pool.wait_ge(st_done, n - 1)
                w = spread(g["eend"][:, c, d * SH:(d + 1) * SH].unsqueeze(2), [P, SH, SP])
                pool.tensor_tensor(xw[:, n % 2, :].rearrange("p (h x) -> p h x", h=SH),
                                   x[:, c, :].rearrange("p (h x) -> p h x", h=SH), w,
                                   ALU.mult).then_inc(xw_ready, 1)

        @block.vector
        def _(dve):
            link = Chain(dve, chain)
            dve.wait_ge(s0_in, 16)

            def b_copy(n):
                dve.wait_ge(tr_done, n + 1)
                dve.tensor_copy(b[:, order[n], :], tr[n % 2][:, 2, 0:256]).then_inc(b_tok, 1)

            b_copy(0)
            b_copy(1)
            for n, (c, d) in enumerate(jobs):
                if n + 2 < NC:
                    b_copy(n + 2)
                dve.wait_ge(st_done, n + 1)
                if c == 0:
                    dve.tensor_copy(fin[:, d, :], st[:, n % 2, :]).then_inc(st_used, 1)
                else:
                    for gp in range(2):
                        link(dve.tensor_tensor(state_view(snap[:, c - 2, :], gp), state_view(snap[:, c - 1, :], gp),
                                               head_decay(g, 1, c, gp), ALU.mult))
                    dve.tensor_tensor(snap[:, c - 2, :], snap[:, c - 2, :], st[:, n % 2, :],
                                      ALU.add).then_inc(st_used, 1)
                    dve.wait_ge(st_used, n + 1)


def ssd_forward(nc, a, k, g, scr, x, b, snap):
    with ExitStack() as ctx:
        U = NC * SG
        bc = ctx.enter_context(nc.sbuf_tensor("bc", [P, 2, 4, C], F32))
        cm = ctx.enter_context(nc.sbuf_tensor("cm", [P, 2, 2, 2, C], F32))
        z = ctx.enter_context(nc.sbuf_tensor("z", [P, 2, D], F32))
        rm = ctx.enter_context(nc.sbuf_tensor("rm", [P, 2, 2, HG, C], F32))
        s2 = ctx.enter_context(nc.sbuf_tensor("s2", [P, 2, SG, C], F32))
        xdt = ctx.enter_context(nc.sbuf_tensor("xdt", [P, 2, 2, D], F32))
        e = ctx.enter_context(nc.sbuf_tensor("e", [P, 2, HG, C], F32))
        wm = ctx.enter_context(nc.sbuf_tensor("wm", [P, 2, 2, HG, C], F32))
        dful = ctx.enter_context(nc.sbuf_tensor("dful", [P, D], F32))
        xd = ctx.enter_context(nc.sbuf_tensor("xd", [P, 2, 512], F32))
        xw = ctx.enter_context(nc.sbuf_tensor("xwf", [P, D], F32))
        t1 = ctx.enter_context(nc.sbuf_tensor("t1", [P, 2, 512], F32))
        t2 = ctx.enter_context(nc.sbuf_tensor("t2", [P, 512], F32))
        yz = ctx.enter_context(nc.sbuf_tensor("yz", [P, 2, D], F32))
        sqb = ctx.enter_context(nc.sbuf_tensor("sqb", [P, D], F32))
        ss = ctx.enter_context(nc.sbuf_tensor("ss_y", [P, NC], F32))
        rs = ctx.enter_context(nc.sbuf_tensor("rs_y", [P, NC], F32))
        sf = ctx.enter_context(nc.sbuf_tensor("sf", [P, 2, 512], F32))
        yo = ctx.enter_context(nc.sbuf_tensor("yo", [P, 2, KD, C], F32))
        arg = ctx.enter_context(nc.psum_tensor("arg", [P, 2, HG, C], F32))
        sc = ctx.enter_context(nc.psum_tensor("sc", [P, SG, C], F32))
        misc = ctx.enter_context(nc.psum_tensor("misc", [P, 512], F32))
        fb = ctx.enter_context(nc.psum_tensor("fb", [P, 2, 512], F32))
        yd = ctx.enter_context(nc.psum_tensor("yd", [P, 2, 512], F32))
        (rmf_ready, rmb_ready, s2_ready, xdt_ready, arg_done, exp_done, sc_done, wm_done, fb_done, fb_used, y_done, y_used, xd_ready,
         xw_ready, yz_done, ss_done, rs_done, yn_done, misc_done, misc_used, s0_in, d_in,
         chain, act_c) = open_sems(
            nc, ctx, *["f_" + n for n in (
                "rmf_ready", "rmb_ready", "s2_ready", "xdt_ready", "arg_done", "exp_done", "sc_done", "wm_done", "fb_done", "fb_used",
                "y_done", "y_used", "xd_ready", "xw_ready", "yz_done", "ss_done", "rs_done",
                "yn_done", "misc_done", "misc_used", "s0_in", "d_in", "chain", "act")])
        bc_in = open_sems(nc, ctx, "bc_in0", "bc_in1")
        cm_ready, = open_sems(nc, ctx, "cm_ready")
        z_in = open_sems(nc, ctx, "z_in0", "z_in1")
        yo_out = open_sems(nc, ctx, "yo_out0", "yo_out1")
        block = ctx.enter_context(nc.Block())

        uses = []
        for u in range(U + 6):
            c, r = u // SG, u % SG
            if r < 2 and 2 <= c <= NC + 1:
                uses.append((f"tr{r}", c - 2))
            if r == 2 and 1 <= c <= NC - 2:
                uses.append(("st", c))
        misc_at = {name: n for n, name in enumerate(uses)}

        def store(sp, c):
            sp.wait_ge(misc_used, misc_at["tr1", c] + 1)
            sp.dma_start(scr["yn"][:, :, c * C:(c + 1) * C], yo[:, c % 2, :, :]).then_inc(yo_out[c % 2], 16)

        @block.sync
        def _(sp):
            sp.dma_start(sf[:, 1, :], a["s_ssd"][:, 0, :]).then_inc(s0_in, 16)
            sp.dma_start(dful[:, :], a["ssd_d"]).then_inc(d_in, 16)
            for c in range(NC):
                if c >= 2:
                    sp.wait_ge(sc_done, c - 1)
                    sp.wait_ge(cm_ready, 2 * (c - 1))
                sp.dma_start(bc[:, c % 2, :, :],
                             scr["xbc"][8:12, :, c * C:(c + 1) * C].rearrange("i p t -> p i t")
                             ).then_inc(bc_in[c % 2], 16)
                if c >= 2:
                    sp.wait_ge(yz_done, 2 * (c - 1))
                sp.dma_start(z[:, c % 2, :], scr["zvo"][0][c]).then_inc(z_in[c % 2], 16)
                if c >= 3:
                    store(sp, c - 3)
            for c in range(NC - 3, NC):
                store(sp, c)
            for s in range(2):
                sp.wait_ge(yo_out[s], 16 * len(range(s, NC, 2)))

        @block.gpsimd
        def _(pool):
            def dt_x(c, d):
                if c >= 2:
                    pool.wait_ge(y_done, SG * (c - 1))
                pool.tensor_tensor(xdt[:, c % 2, d, :].rearrange("p (h x) -> p h x", h=SH),
                                   x[:, c, :].rearrange("p (h x) -> p h x", h=SH),
                                   spread(g["dt_ig"][:, c, d * SH:(d + 1) * SH].unsqueeze(2), [P, SH, SP]),
                                   ALU.mult).then_inc(xdt_ready, 1)

            for u in range(U):
                c, q = u // SG, u % SG
                if u >= 2:
                    pool.wait_ge(arg_done, u - 1)
                hs = [P, HG, C]
                pool.tensor_tensor(rm[:, u % 2, 0, :, :],
                                   spread(g["dec"][:, c, q * HG:(q + 1) * HG].unsqueeze(2), hs),
                                   spread(const(k, "le").unsqueeze(1), hs), ALU.mult).then_inc(rmf_ready, 1)
                if u == 0:
                    dt_x(0, 0)
                    dt_x(0, 1)
                if u % 2 == 1:
                    v = u // 2
                    if v == 0:
                        pool.wait_ge(d_in, 16)
                    if v >= 2:
                        pool.wait_ge(yz_done, v - 1)
                    hf = slice((v % 2) * 512, (v % 2) * 512 + 512)
                    pool.tensor_tensor(xd[:, v % 2, :], x[:, c, hf], dful[:, hf], ALU.mult).then_inc(xd_ready, 1)
                if q == 0 and 1 <= c <= NC - 2:
                    if c >= 2:
                        pool.wait_ge(misc_done, misc_at["st", c - 1] + 1)
                    w = spread(g["eend"][:, c, 0:SH].unsqueeze(2), [P, SH, SP])
                    pool.tensor_tensor(xw[:, :].rearrange("p (h x) -> p h x", h=SH),
                                       x[:, c, :].rearrange("p (h x) -> p h x", h=SH), w,
                                       ALU.mult).then_inc(xw_ready, 1)
                if q in (1, 2) and c + 1 < NC:
                    dt_x(c + 1, q - 1)

        @block.tensor
        def _(pe):
            def shared(name):
                n = misc_at[name]
                if n:
                    pe.wait_ge(misc_used, n)

            def scores(c):
                pe.wait_ge(bc_in[c % 2], 16 * (c // 2 + 1))
                pe.wait_ge(cm_ready, 2 * (c + 1))
                if c:
                    pe.wait_ge(s2_ready, c)
                for q in range(SG):
                    m = pe.matmul(sc[:, q, :], bc[:, c % 2, q // 2, :], cm[:, c % 2, q % 2, q // 2, :],
                                  start=True, stop=True)
                m.then_inc(sc_done, 1)

            scores(0)
            for u in range(U + 6):
                c, r = u // SG, u % SG
                if u < U:
                    if r % 2 == 0:
                        v = u // 2
                        if v >= 3:
                            pe.wait_ge(fb_used, v - 2)
                        if c == 0:
                            pe.sem_inc(fb_done, 1)
                        else:
                            if c == 1:
                                pe.wait_ge(s0_in, 16)
                            else:
                                pe.wait_ge(misc_used, misc_at["st", c - 1] + 1)
                            for d in range(2):
                                s = sf[:, c % 2, :] if d == 0 else snap[:, c - 1, :]
                                for gp in range(2):
                                    gh = v % 2
                                    m = pe.matmul(fb[:, d, gp * 256:gp * 256 + 256], cm[:, c % 2, gp, gh, :],
                                                  s[:, gh * 256:gh * 256 + 256], start=True, stop=True,
                                                  skip_group_check=True)
                            m.then_inc(fb_done, 1)
                    pe.wait_ge(rmf_ready, u + 1)
                    pe.wait_ge(rmb_ready, u + 1)
                    if u >= 2:
                        pe.wait_ge(exp_done, u - 1)
                    for d, mask in enumerate(("gt", "lt")):
                        m = pe.matmul(arg[:, u % 2, :, :], const(k, mask), rm[:, u % 2, d, :, :], start=(d == 0),
                                      stop=(d == 1))
                    m.then_inc(arg_done, 1)
                if 1 <= u <= U:
                    w = u - 1
                    cw, q, v = w // SG, w % SG, w // 2
                    pe.wait_ge(wm_done, w + 1)
                    if w % 2 == 0 and v >= 2:
                        pe.wait_ge(y_used, v - 1)
                    pe.wait_ge(xdt_ready, 2 * (cw + 1))
                    for i in range(HG):
                        hd = q * HG + i
                        for d in range(2):
                            m = pe.matmul(yd[:, v % 2, (hd % 8) * SP:(hd % 8 + 1) * SP], wm[:, w % 2, d, i, :],
                                          xdt[:, cw % 2, d, hd * SP:(hd + 1) * SP], start=(d == 0), stop=(d == 1),
                                          skip_group_check=True)
                    m.then_inc(y_done, 1)
                if r == 3 and c + 1 < NC:
                    scores(c + 1)
                if r == 2 and 1 <= c <= NC - 2:
                    pe.wait_ge(xw_ready, c)
                    shared(("st", c))
                    for q in range(SG):
                        m = pe.matmul(misc[64 * (q % 2):64 * (q % 2) + 64, 256 * (q // 2):256 * (q // 2) + 256],
                                      b[:, c, q * SN:(q + 1) * SN], xw[:, q * 256:(q + 1) * 256], start=True,
                                      stop=True, skip_group_check=True)
                    m.then_inc(misc_done, 1)
                for name, j, r0, back in (("tr0", 0, 0, 2), ("tr1", 1, 1, 2)):
                    if r == r0 and back <= c <= NC - 1 + back:
                        cc = c - back
                        pe.wait_ge(yn_done, cc + 1)
                        shared((name, cc))
                        for i in range(4):
                            m = pe.transpose(misc[:, i * P:(i + 1) * P],
                                             yz[:, cc % 2, (4 * j + i) * P:(4 * j + i + 1) * P], const(k, "ident"))
                        m.then_inc(misc_done, 1)

        @block.scalar
        def _(act):
            link = Chain(act, act_c)

            def one_group(c):
                act.wait_ge(bc_in[c % 2], 16 * (c // 2 + 1))
                if c >= 2:
                    act.wait_ge(sc_done, c - 1)
                    act.wait_ge(fb_done, 2 * (c - 1))
                for half in range(2):
                    act.activation(cm[:, c % 2, half, :, :], bc[:, c % 2, 2:4, :], ACT.Copy,
                                   scale=const(k, f"half{half}")).then_inc(cm_ready, 1)

            def backward_decay(u):
                if u >= 2:
                    act.wait_ge(arg_done, u - 1)
                for i in range(HG):
                    j = SH + (u % SG) * HG + i
                    m = act.activation(rm[:, u % 2, 1, i, :], const(k, "ge"), ACT.Copy,
                                       scale=g["dec"][:, u // SG, j:j + 1])
                m.then_inc(rmb_ready, 1)

            one_group(0)
            backward_decay(0)
            for u in range(U + 6):
                c, r = u // SG, u % SG
                if u + 1 < U:
                    backward_decay(u + 1)
                if r == 2 and c + 1 < NC:
                    one_group(c + 1)
                if u < U:
                    act.wait_ge(arg_done, u + 1)
                    if u >= 2:
                        act.wait_ge(wm_done, u - 1)
                    act.activation(e[:, u % 2, :, :], arg[:, u % 2, :, :], ACT.Exp).then_inc(exp_done, 1)
                if r == 1 and 1 <= c <= NC:
                    cc = c - 1
                    act.wait_ge(yz_done, 2 * cc + 2)
                    link(act.activation(sqb[:, :], yz[:, cc % 2, :], ACT.Square, accum_out=ss[:, cc:cc + 1]))
                    link(act.activation(rs[:, cc:cc + 1], ss[:, cc:cc + 1], ACT.Ln, bias=const(k, "eps"),
                                        scale=1.0 / D))
                    act.activation(rs[:, cc:cc + 1], rs[:, cc:cc + 1], ACT.Exp, scale=-0.5).then_inc(rs_done, 1)
                if r < 2 and 2 <= c <= NC + 1:
                    cc = c - 2
                    act.wait_ge(misc_done, misc_at[f"tr{r}", cc] + 1)
                    if cc >= 2:
                        act.wait_ge(yo_out[cc % 2], 16 * (cc // 2))
                    for i in range(4 * r, 4 * r + 4):
                        m = act.activation(yo[:, cc % 2, i, :], misc[:, (i % 4) * P:(i % 4 + 1) * P], ACT.Copy,
                                           scale=col(k, "ssd_norm", i))
                    m.then_inc(misc_used, 1)

        @block.vector
        def _(dve):
            link = Chain(dve, chain)

            def masked_scores(c):
                dve.wait_ge(sc_done, c + 1)
                if c:
                    dve.wait_ge(wm_done, SG * c)
                for d, mask in enumerate(("le", "ge")):
                    m = dve.tensor_tensor(s2[:, d, :, :], sc[:, :, :],
                                          spread(const(k, mask).unsqueeze(1), [P, SG, C]), ALU.mult)
                m.then_inc(s2_ready, 1)

            def move_state(c):
                if c == 1:
                    dve.wait_ge(s0_in, 16)
                else:
                    dve.wait_ge(fb_done, 2 * c)
                    dve.wait_ge(misc_used, misc_at["st", c - 1] + 1)
                for gp in range(2):
                    link(dve.tensor_tensor(state_view(sf[:, (c + 1) % 2, :], gp),
                                           state_view(sf[:, c % 2, :], gp), head_decay(g, 0, c, gp), ALU.mult))
                dve.wait_ge(misc_done, misc_at["st", c] + 1)
                dve.tensor_tensor(sf[:, (c + 1) % 2, :], sf[:, (c + 1) % 2, :], misc[:, :],
                                  ALU.add).then_inc(misc_used, 1)

            masked_scores(0)
            for u in range(U + 6):
                c, r = u // SG, u % SG
                if r == 3 and 1 <= c <= NC - 2:
                    move_state(c)
                if u < U:
                    if u % 2 == 0 and c >= 1:
                        v = u // 2
                        dve.wait_ge(fb_done, v + 1)
                        if v >= 2:
                            dve.wait_ge(yz_done, v - 1)
                        hs = [P, 8, SP]
                        for d, dst in ((0, t1[:, v % 2, :]), (1, t2[:, :])):
                            w = spread(g["ecum"][:, c, d * SH + 8 * (v % 2):d * SH + 8 * (v % 2) + 8].unsqueeze(2), hs)
                            ins = dve.tensor_tensor(dst.rearrange("p (h x) -> p h x", h=8),
                                                    fb[:, d, :].rearrange("p (h x) -> p h x", h=8), w, ALU.mult)
                            ins.then_inc(chain, 1)
                            link.n += 1
                        dve.wait_ge(chain, link.n)
                        link(dve.tensor_tensor(t1[:, v % 2, :], t1[:, v % 2, :], t2[:, :], ALU.add))
                        dve.sem_inc(fb_used, 1)
                    dve.wait_ge(exp_done, u + 1)
                    if u >= 2:
                        dve.wait_ge(y_done, u - 1)
                    if r == 0:
                        dve.wait_ge(s2_ready, c + 1)
                    for d in range(2):
                        m = dve.tensor_tensor(wm[:, u % 2, d, :, :], e[:, u % 2, :, :],
                                              spread(s2[:, d, r, :].unsqueeze(1), [P, HG, C]), ALU.mult)
                    m.then_inc(wm_done, 1)
                    if r == 3 and c + 1 < NC:
                        masked_scores(c + 1)
                if u % 2 == 0 and 2 <= u <= U:
                    v = u // 2 - 1
                    cc, half = v // 2, slice((v % 2) * 512, (v % 2) * 512 + 512)
                    dve.wait_ge(y_done, 2 * v + 2)
                    dve.wait_ge(xd_ready, v + 1)
                    if cc == 0:
                        link(dve.tensor_tensor(t1[:, v % 2, :], xd[:, v % 2, :], yd[:, v % 2, :], ALU.add))
                        dve.sem_inc(y_used, 1)
                    else:
                        link(dve.tensor_tensor(t1[:, v % 2, :], t1[:, v % 2, :], yd[:, v % 2, :], ALU.add))
                        dve.sem_inc(y_used, 1)
                        link(dve.tensor_tensor(t1[:, v % 2, :], t1[:, v % 2, :], xd[:, v % 2, :], ALU.add))
                    dve.wait_ge(z_in[cc % 2], 16 * (cc // 2 + 1))
                    if cc >= 2:
                        dve.wait_ge(misc_done, misc_at["tr1", cc - 2] + 1)
                    dve.tensor_tensor(yz[:, cc % 2, half], t1[:, v % 2, :], z[:, cc % 2, half],
                                      ALU.mult).then_inc(yz_done, 1)
                if r == 2 and 1 <= c <= NC:
                    cc = c - 1
                    dve.wait_ge(rs_done, cc + 1)
                    dve.tensor_scalar(yz[:, cc % 2, :], yz[:, cc % 2, :], rs[:, cc:cc + 1], None,
                                      ALU.mult).then_inc(yn_done, 1)


def ml_decay(g, d, c, hp, n, half):
    r = slice(64 * half, 64 * half + 64)
    v = g["dbc"][r, c, 32 + 8 * d:40 + 8 * d].rearrange("p (a b) -> p a b", b=2)[:, hp:hp + n, half]
    return spread(v.unsqueeze(2), [64, n, DV1])


def mlstm(nc, a, k, g, scr, o):
    with ExitStack() as ctx:
        v = ctx.enter_context(nc.sbuf_tensor("v_one", [P, NC, MH, DV1], F32))
        kt = ctx.enter_context(nc.sbuf_tensor("k_tok", [P, NC, MH * DK], F32))
        snap = ctx.enter_context(nc.sbuf_tensor("snap_c", [P, NC - 1, 4, DV1], F32))
        mlstm_backward(nc, a, k, g, scr, o, v, kt, snap)
        mlstm_forward(nc, a, k, g, scr, v, kt, snap)


def mlstm_backward(nc, a, k, g, scr, o, v, kt, snap):
    with ExitStack() as ctx:
        kc = ctx.enter_context(nc.sbuf_tensor("kc", [P, 2, 4, C], F32))
        vw = ctx.enter_context(nc.sbuf_tensor("vw", [P, 2, MH, DV1], F32))
        fin = ctx.enter_context(nc.sbuf_tensor("fin_c", [P, 2, 4, DV1], F32))
        tr = ctx.enter_context(nc.psum_tensor("trk", [P, 2, 512], F32))
        st = ctx.enter_context(nc.psum_tensor("stc", [P, 2, 2, 512], F32))
        tr_done, k_tok, one, vw_ready, st_done, st_used, c0_in, chain = open_sems(
            nc, ctx, *["mb_" + n for n in ("tr_done", "k_tok", "one", "vw_ready", "st_done", "st_used", "c0_in",
                                           "chain")])
        kc_in = open_sems(nc, ctx, "kc_in0", "kc_in1")
        v_in = open_sems(nc, ctx, *[f"v_in{i}" for i in range(NC)])
        block = ctx.enter_context(nc.Block())
        order = [0] + list(range(NC - 1, 0, -1))
        jobs = [(0, 0), (0, 1)] + [(c, 1) for c in range(NC - 1, 1, -1)]
        at = {c: n for n, c in enumerate(order)}

        @block.sync
        def _(sp):
            sp.dma_start(snap[:, NC - 2, :, :], a["s_ml"][:, 1, :, :]).then_inc(c0_in, 16)
            for n, c in enumerate(order):
                if n >= 2:
                    sp.wait_ge(tr_done, n - 1)
                sp.dma_start(kc[:, n % 2, :, :],
                             scr["qk"][4:8, :, c * C:(c + 1) * C].rearrange("i p t -> p i t")
                             ).then_inc(kc_in[n % 2], 16)
                sp.dma_start(v[:, c, :, 0:DV], scr["zvo"][1][c].rearrange("p (h x) -> p h x", h=MH)
                             ).then_inc(v_in[c], 16)
            sp.wait_ge(st_used, 2)
            sp.dma_start(o["ml"], fin[:, :, :, :]).then_inc(o["ml_out"], 16)
            sp.wait_ge(o["ml_out"], 16)

        @block.tensor
        def _(pe):
            def turn(n):
                pe.wait_ge(kc_in[n % 2], 16 * (n // 2 + 1))
                if n >= 2:
                    pe.wait_ge(k_tok, n - 1)
                for i in range(4):
                    m = pe.transpose(tr[:, n % 2, i * P:(i + 1) * P], kc[:, n % 2, i, :], const(k, "ident"))
                m.then_inc(tr_done, 1)

            def state(n):
                c, d = jobs[n]
                pe.wait_ge(vw_ready, n + 1)
                pe.wait_ge(k_tok, at[c] + 1)
                if n >= 2:
                    pe.wait_ge(st_used, n - 1)
                for h in range(MH):
                    hp, r = h // 2, slice(64 * (h % 2), 64 * (h % 2) + 64)
                    m = pe.matmul(st[r, n % 2, hp // 2, (hp % 2) * DV1:(hp % 2 + 1) * DV1],
                                  kt[:, c, h * DK:(h + 1) * DK], vw[:, n % 2, h, :], start=True, stop=True,
                                  skip_group_check=True)
                m.then_inc(st_done, 1)

            turn(0)
            turn(1)
            state(0)
            state(1)
            for n in range(2, NC):
                turn(n)
                state(n)

        @block.scalar
        def _(act):
            for n, c in enumerate(order):
                act.wait_ge(tr_done, n + 1)
                act.activation(kt[:, c, :], tr[:, n % 2, :], ACT.Copy).then_inc(k_tok, 1)

        @block.gpsimd
        def _(pool):
            pool.memset(v[:, :, :, DV:DV1], 1.0).then_inc(one, 1)
            pool.wait_ge(one, 1)
            for n, (c, d) in enumerate(jobs):
                pool.wait_ge(v_in[c], 16)
                if n >= 2:
                    pool.wait_ge(st_done, n - 1)
                w = spread(g["eend"][:, c, 32 + 8 * d:40 + 8 * d].unsqueeze(2), [P, MH, DV1])
                pool.tensor_tensor(vw[:, n % 2, :, :], v[:, c, :, :], w, ALU.mult).then_inc(vw_ready, 1)

        @block.vector
        def _(dve):
            link = Chain(dve, chain)
            dve.wait_ge(c0_in, 16)
            for n, (c, d) in enumerate(jobs):
                dve.wait_ge(st_done, n + 1)
                if c == 0:
                    for j in range(2):
                        link(dve.tensor_copy(fin[:, d, 2 * j:2 * j + 2, :],
                                             st[:, n % 2, j, 0:2 * DV1].rearrange("p (a x) -> p a x", a=2)))
                else:
                    for half in range(2):
                        r = slice(64 * half, 64 * half + 64)
                        link(dve.tensor_tensor(snap[r, c - 2, :, :], snap[r, c - 1, :, :],
                                               ml_decay(g, 1, c, 0, 4, half), ALU.mult))
                    for j in range(2):
                        link(dve.tensor_tensor(snap[:, c - 2, 2 * j:2 * j + 2, :], snap[:, c - 2, 2 * j:2 * j + 2, :],
                                               st[:, n % 2, j, 0:2 * DV1].rearrange("p (a x) -> p a x", a=2),
                                               ALU.add))
                dve.sem_inc(st_used, 1)


def mlstm_forward(nc, a, k, g, scr, v, kt, snap):
    with ExitStack() as ctx:
        U = NC * 4
        qk = ctx.enter_context(nc.sbuf_tensor("qk", [P, 2, 8, C], F32))
        qm = ctx.enter_context(nc.sbuf_tensor("qm", [P, 2, 2, 4, C], F32))
        og = ctx.enter_context(nc.sbuf_tensor("og", [P, 2, D], F32))
        lm = ctx.enter_context(nc.sbuf_tensor("lm", [P, 2, 4, C], F32))
        e = ctx.enter_context(nc.sbuf_tensor("e_m", [P, 2, 4, C], F32))
        wm = ctx.enter_context(nc.sbuf_tensor("wm_m", [P, 2, 4, C], F32))
        qw = ctx.enter_context(nc.sbuf_tensor("qw", [P, 2, 2, 4, C], F32))
        vw = ctx.enter_context(nc.sbuf_tensor("vwf", [P, MH, DV1], F32))
        hb = ctx.enter_context(nc.sbuf_tensor("hb", [P, 2, 2, MH, DV1], F32))
        hs = ctx.enter_context(nc.sbuf_tensor("hs", [P, 2, D], F32))
        sqb = ctx.enter_context(nc.sbuf_tensor("sqm", [P, D], F32))
        den = ctx.enter_context(nc.sbuf_tensor("den", [P, 2, MH], F32))
        ss = ctx.enter_context(nc.sbuf_tensor("ss_m", [P, 2, MH], F32))
        cf = ctx.enter_context(nc.sbuf_tensor("cf", [P, 2, 4, DV1], F32))
        ho = ctx.enter_context(nc.sbuf_tensor("ho", [P, 2, KD, C], F32))
        selm = ctx.enter_context(nc.sbuf_tensor("selm", [48, 16, P], F32))
        selq = ctx.enter_context(nc.sbuf_tensor("selq", [48, 8, P], F32))
        wir = ctx.enter_context(nc.sbuf_tensor("wir", [48, T], F32))
        negi = ctx.enter_context(nc.sbuf_tensor("negi", [P, P], BF16))
        mk = ctx.enter_context(nc.sbuf_tensor("mk", [P, 2, 4, C], BF16))
        arg = ctx.enter_context(nc.psum_tensor("arg_m", [P, 2, 4, C], F32))
        sc = ctx.enter_context(nc.psum_tensor("sc_m", [P, 2, 4, C], F32))
        qb = ctx.enter_context(nc.psum_tensor("qb", [P, 4, C], F32))
        misc = ctx.enter_context(nc.psum_tensor("misc_m", [P, 512], F32))
        num = ctx.enter_context(nc.psum_tensor("num", [P, 2, 512], F32))
        (lm_ready, arg_done, exp_done, sc_done, wm_done, qb_done, qw_done, num_done, h_copied, vw_ready,
         hm_done, ss_done, rs_done, hn_done, misc_done, misc_used, c0_in, sel_in, wi_done, wi_row, mk_ready,
         chain, act_c) = open_sems(
            nc, ctx, *["m_" + n for n in (
                "lm_ready", "arg_done", "exp_done", "sc_done", "wm_done", "qb_done", "qw_done", "num_done",
                "h_copied", "vw_ready", "hm_done", "ss_done", "rs_done", "hn_done", "misc_done",
                "misc_used", "c0_in", "sel_in", "wi_done", "wi_row", "mk_ready", "chain", "act")])
        qk_in = open_sems(nc, ctx, "qk_in0", "qk_in1")
        qm_ready, = open_sems(nc, ctx, "qm_ready")
        og_in = open_sems(nc, ctx, "og_in0", "og_in1")
        ho_out = open_sems(nc, ctx, "ho_out0", "ho_out1")
        block = ctx.enter_context(nc.Block())
        ML = slice(32, 48)

        uses = []
        for w in range(U + 7):
            c, r = w // 4, w % 4
            if r == 0 and 2 <= c <= NC - 1:
                uses.append(("st1", c - 1))
            if r in (1, 2) and 2 <= c <= NC + 1:
                uses.append((f"tr{r - 1}", c - 2))
            if r == 3 and 1 <= c <= NC - 2:
                uses.append(("st0", c))
        misc_at = {name: n for n, name in enumerate(uses)}

        def store(sp, c):
            sp.wait_ge(misc_used, misc_at["tr1", c] + 1)
            sp.dma_start(scr["hm"][:, :, c * C:(c + 1) * C], ho[:, c % 2, :, :]).then_inc(ho_out[c % 2], 16)

        @block.sync
        def _(sp):
            sp.dma_start(selm[:, :, :], a["selm"]).then_inc(sel_in, 16)
            sp.dma_start(selq[:, :, :], a["selq"]).then_inc(sel_in, 16)
            sp.dma_start(cf[:, 1, :, :], a["s_ml"][:, 0, :, :]).then_inc(c0_in, 16)
            for c in range(NC):
                if c >= 2:
                    sp.wait_ge(sc_done, 2 * (c - 1))
                    sp.wait_ge(qm_ready, 2 * (c - 1))
                sp.dma_start(qk[:, c % 2, :, :],
                             scr["qk"][:, :, c * C:(c + 1) * C].rearrange("i p t -> p i t")
                             ).then_inc(qk_in[c % 2], 16)
                if c >= 2:
                    sp.wait_ge(hn_done, c - 1)
                sp.dma_start(og[:, c % 2, :], scr["zvo"][2][c]).then_inc(og_in[c % 2], 16)
                if c >= 3:
                    store(sp, c - 3)
            for c in range(NC - 3, NC):
                store(sp, c)
            for s in range(2):
                sp.wait_ge(ho_out[s], 16 * len(range(s, NC, 2)))

        @block.gpsimd
        def _(pool):
            for w in range(U + 7):
                c, r = w // 4, w % 4
                if w < U:
                    hg, d = r // 2, r % 2
                    if w >= 2:
                        pool.wait_ge(arg_done, w - 1)
                    f = g["dec"][:, c, 32 + 8 * d + 4 * hg:36 + 8 * d + 4 * hg]
                    pool.tensor_tensor(lm[:, w % 2, :, :], spread(f.unsqueeze(2), [P, 4, C]),
                                       spread(const(k, "le" if d == 0 else "ge").unsqueeze(1), [P, 4, C]),
                                       ALU.mult).then_inc(lm_ready, 1)
                if r == 0 and 1 <= c <= NC - 2:
                    if c >= 2:
                        pool.wait_ge(misc_done, misc_at["st1", c - 1] + 1)
                    pool.tensor_tensor(vw[:, :, :], v[:, c, :, :],
                                       spread(g["eend"][:, c, 32:40].unsqueeze(2), [P, MH, DV1]),
                                       ALU.mult).then_inc(vw_ready, 1)

        @block.tensor
        def _(pe):
            for n, c0 in enumerate(range(0, NC, 3)):
                if n:
                    pe.wait_ge(wi_row, n)
                for c in range(c0, c0 + 3):
                    m = pe.transpose(misc[0:48, (c - c0) * C:(c - c0 + 1) * C], g["ecum"][:, c, :],
                                     const(k, "ident"))
                m.then_inc(wi_done, 1)
            pe.wait_ge(wi_row, NC // 3)

            def shared(name):
                n = misc_at[name]
                if n:
                    pe.wait_ge(misc_used, n)

            pe.wait_ge(mk_ready, 3)
            pe.wait_ge(sel_in, 32)
            for w in range(U + 7):
                c, r = w // 4, w % 4
                if w < U:
                    hg, d, s = r // 2, r % 2, c % 2
                    if d == 0:
                        x = w // 2
                        if r == 0:
                            pe.wait_ge(qk_in[s], 16 * (c // 2 + 1))
                            pe.wait_ge(qm_ready, 2 * (c + 1))
                        if x >= 2:
                            pe.wait_ge(wm_done, 2 * (x - 1))
                        for i in range(4):
                            h = 4 * hg + i
                            m = pe.matmul(sc[:, x % 2, i, :], qk[:, s, 4 + h // 2, :], qm[:, s, h % 2, h // 2, :],
                                          start=True, stop=True)
                        m.then_inc(sc_done, 1)
                    if r < 2 and c >= 1:
                        n = 2 * (c - 1) + r
                        if n:
                            pe.wait_ge(qw_done, n + 2)
                        for hp in range(4):
                            m = pe.matmul(qb[:, hp, :], selq[ML, 4 * r + hp, :], wir[ML, c * C:(c + 1) * C],
                                          start=True, stop=True, skip_group_check=True)
                        m.then_inc(qb_done, 1)
                    pe.wait_ge(lm_ready, w + 1)
                    if w >= 2:
                        pe.wait_ge(exp_done, w - 1)
                    pe.matmul(arg[:, w % 2, :, :], const(k, "gt" if d == 0 else "lt"), lm[:, w % 2, :, :],
                              start=True, stop=False, skip_group_check=True)
                    for i in range(4):
                        pe.matmul(arg[:, w % 2, i, :], selm[ML, 8 * d + 4 * hg + i, :],
                                  g["negm"][ML, c * C:(c + 1) * C], start=False, stop=False, skip_group_check=True)
                    pe.matmul(arg[:, w % 2, :, :], negi[:, :], mk[:, d, :, :], start=False, stop=True,
                              skip_group_check=True).then_inc(arg_done, 1)
                if 1 <= w <= U:
                    wn = w - 1
                    cn, hg, d = wn // 4, (wn % 4) // 2, wn % 2
                    pe.wait_ge(wm_done, wn + 1)
                    if cn >= 1:
                        pe.wait_ge(qw_done, 2 * cn + d + 1)
                        if cn == 1:
                            pe.wait_ge(c0_in, 16)
                        else:
                            pe.wait_ge(misc_used, misc_at[f"st{hg}", cn - 1] + 1)
                    for j in range(2):
                        n = 2 * wn + j
                        if n >= 2:
                            pe.wait_ge(h_copied, n - 1)
                        for i in range(2):
                            h = 4 * hg + 2 * j + i
                            dst = num[:, n % 2, i * DV1:(i + 1) * DV1]
                            m = pe.matmul(dst, wm[:, wn % 2, 2 * j + i, :], v[:, cn, h, :], start=True,
                                          stop=(cn == 0), skip_group_check=True)
                            if cn >= 1:
                                st = cf[:, cn % 2, h // 2, :] if d == 0 else snap[:, cn - 1, h // 2, :]
                                m = pe.matmul(dst, qw[:, d, h % 2, h // 2, :], st, start=False, stop=True,
                                              skip_group_check=True)
                        m.then_inc(num_done, 1)
                if (r == 3 and 1 <= c <= NC - 2) or (r == 0 and 2 <= c <= NC - 1):
                    j = 0 if r == 3 else 1
                    cs = c - j
                    pe.wait_ge(vw_ready, cs)
                    shared((f"st{j}", cs))
                    for h in range(4 * j, 4 * j + 4):
                        p0 = slice(64 * (h % 2), 64 * (h % 2) + 64)
                        i = (h // 2) % 2
                        m = pe.matmul(misc[p0, i * DV1:(i + 1) * DV1], kt[:, cs, h * DK:(h + 1) * DK], vw[:, h, :],
                                      start=True, stop=True, skip_group_check=True)
                    m.then_inc(misc_done, 1)
                for name, j, r0, back in (("tr0", 0, 1, 2), ("tr1", 1, 2, 2)):
                    if r == r0 and back <= c <= NC - 1 + back:
                        cc = c - back
                        pe.wait_ge(hn_done, cc + 1)
                        shared((name, cc))
                        for i in range(4):
                            m = pe.transpose(misc[:, i * P:(i + 1) * P],
                                             hs[:, cc % 2, (4 * j + i) * P:(4 * j + i + 1) * P], const(k, "ident"))
                        m.then_inc(misc_done, 1)

        @block.scalar
        def _(act):
            link = Chain(act, act_c)
            for n in range(NC // 3):
                act.wait_ge(wi_done, n + 1)
                act.activation(wir[ML, 3 * n * C:3 * (n + 1) * C], misc[ML, 0:3 * C], ACT.Copy).then_inc(wi_row, 1)

            def one_head(c):
                act.wait_ge(qk_in[c % 2], 16 * (c // 2 + 1))
                if c >= 2:
                    act.wait_ge(sc_done, 2 * (c - 1))
                    act.wait_ge(qw_done, 2 * (c - 1))
                for half in range(2):
                    act.activation(qm[:, c % 2, half, :, :], qk[:, c % 2, 0:4, :], ACT.Copy,
                                   scale=const(k, f"half{half}")).then_inc(qm_ready, 1)

            one_head(0)
            for w in range(U + 7):
                c, r = w // 4, w % 4
                if r == 2 and c + 1 < NC:
                    one_head(c + 1)
                if w < U:
                    hg, d = r // 2, r % 2
                    act.wait_ge(arg_done, w + 1)
                    if w >= 2:
                        act.wait_ge(wm_done, w - 1)
                    for i in range(4):
                        j = 32 + 8 * d + 4 * hg + i
                        m = act.activation(e[:, w % 2, i, :], arg[:, w % 2, i, :], ACT.Exp,
                                           bias=g["dt_ig"][:, c, j:j + 1])
                    m.then_inc(exp_done, 1)
                if 1 <= w <= U:
                    wn = w - 1
                    cn, hg, d = wn // 4, (wn % 4) // 2, wn % 2
                    if cn >= 2 and wn % 4 == 0:
                        act.wait_ge(hm_done, cn - 1)
                    for j in range(2):
                        n = 2 * wn + j
                        act.wait_ge(num_done, n + 1)
                        act.activation(hb[:, cn % 2, d, 4 * hg + 2 * j:4 * hg + 2 * j + 2, :],
                                       num[:, n % 2, 0:2 * DV1].rearrange("p (a x) -> p a x", a=2),
                                       ACT.Copy).then_inc(h_copied, 1)
                if r in (1, 2) and 2 <= c <= NC + 1:
                    j, cc = r - 1, c - 2
                    act.wait_ge(misc_done, misc_at[f"tr{j}", cc] + 1)
                    if cc >= 2:
                        act.wait_ge(ho_out[cc % 2], 16 * (cc // 2))
                    for i in range(4 * j, 4 * j + 4):
                        m = act.activation(ho[:, cc % 2, i, :], misc[:, (i % 4) * P:(i % 4 + 1) * P], ACT.Copy,
                                           scale=col(k, "ml_norm", i))
                    m.then_inc(misc_used, 1)
                if r == 3 and 1 <= c <= NC:
                    cc = c - 1
                    act.wait_ge(ss_done, cc + 1)
                    link(act.activation(ss[:, cc % 2, :], ss[:, cc % 2, :], ACT.Ln, bias=const(k, "eps"),
                                        scale=1.0 / DV))
                    act.activation(ss[:, cc % 2, :], ss[:, cc % 2, :], ACT.Exp, scale=-0.5).then_inc(rs_done, 1)

        @block.vector
        def _(dve):
            link = Chain(dve, chain)
            dve.tensor_scalar(negi[:, :], const(k, "ident"), NEG, None, ALU.mult).then_inc(mk_ready, 1)
            for d, mask in enumerate(("gt", "lt")):
                dve.tensor_copy(mk[:, d, :, :], spread(const(k, mask).unsqueeze(1), [P, 4, C])).then_inc(mk_ready, 1)

            def cf_view(c, j):
                return cf[:, (c + 1) % 2, 2 * j:2 * j + 2, :]

            def decay_state(c, j):
                if c == 1:
                    dve.wait_ge(c0_in, 16)
                else:
                    dve.wait_ge(num_done, 8 * c)
                    dve.wait_ge(misc_used, misc_at[f"st{j}", c - 1] + 1)
                for half in range(2):
                    p0 = slice(64 * half, 64 * half + 64)
                    link(dve.tensor_tensor(cf_view(c, j)[p0], cf_view(c - 1, j)[p0], ml_decay(g, 0, c, 2 * j, 2, half),
                                           ALU.mult))

            def add_state(c, j):
                dve.wait_ge(misc_done, misc_at[f"st{j}", c] + 1)
                dve.tensor_tensor(cf_view(c, j), cf_view(c, j),
                                  misc[:, 0:2 * DV1].rearrange("p (a x) -> p a x", a=2),
                                  ALU.add).then_inc(misc_used, 1)

            for w in range(U + 7):
                c, r = w // 4, w % 4
                if r < 2 and 2 <= c <= NC - 1:
                    add_state(c - 1, r)
                if w < U:
                    hg, d, s = r // 2, r % 2, c % 2
                    if r < 2:
                        if c >= 1:
                            dve.wait_ge(qb_done, 2 * (c - 1) + r + 1)
                            if c >= 2:
                                dve.wait_ge(num_done, 2 * (4 * (c - 1) + 2 + r) + 2)
                            for half in range(2):
                                m = dve.tensor_tensor(qw[:, r, half, :, :], qm[:, s, half, :, :], qb[:, :, :],
                                                      ALU.mult)
                            m.then_inc(qw_done, 1)
                        else:
                            dve.sem_inc(qw_done, 1)
                    dve.wait_ge(exp_done, w + 1)
                    if w >= 2:
                        dve.wait_ge(num_done, 2 * (w - 1))
                    dve.wait_ge(sc_done, w // 2 + 1)
                    dve.tensor_tensor(wm[:, w % 2, :, :], e[:, w % 2, :, :], sc[:, (w // 2) % 2, :, :],
                                      ALU.mult).then_inc(wm_done, 1)
                if r == 1 and 1 <= c <= NC:
                    cc = c - 1
                    q = cc % 2
                    dve.wait_ge(h_copied, 8 * (cc + 1))
                    dn = hb[:, q, :, :, DV]
                    link(dve.scalar_tensor_tensor(out=den[:, :, :], in0=dn, scalar=-1.0, in1=dn, op0=ALU.mult,
                                                  op1=ALU.max))
                    link(dve.tensor_tensor(den[:, :, :], den[:, :, :],
                                           g["em"][:, cc, :].rearrange("p (d h) -> p d h", d=2), ALU.max))
                    link(dve.reciprocal(den[:, :, :], den[:, :, :]))
                    h3 = hs[:, q, :].rearrange("p (h x) -> p h x", h=MH)
                    s3 = sqb[:, :].rearrange("p (h x) -> p h x", h=MH)
                    if cc >= 2:
                        dve.wait_ge(misc_done, misc_at["tr1", cc - 2] + 1)
                    link(dve.tensor_tensor(h3, hb[:, q, 0, :, 0:DV], spread(den[:, 0, :].unsqueeze(2), [P, MH, DV]),
                                           ALU.mult))
                    link(dve.tensor_tensor(s3, hb[:, q, 1, :, 0:DV], spread(den[:, 1, :].unsqueeze(2), [P, MH, DV]),
                                           ALU.mult))
                    dve.sem_inc(hm_done, 1)
                if r == 2 and 1 <= c <= NC:
                    cc = c - 1
                    q = cc % 2
                    s3 = sqb[:, :].rearrange("p (h x) -> p h x", h=MH)
                    link(dve.tensor_tensor(hs[:, q, :], hs[:, q, :], sqb[:, :], ALU.add))
                    link(dve.tensor_tensor(sqb[:, :], hs[:, q, :], hs[:, q, :], ALU.mult))
                    dve.tensor_reduce(ss[:, q, :], s3, AX.X, ALU.add).then_inc(ss_done, 1)
                    dve.wait_ge(ss_done, cc + 1)
                if r == 0 and 2 <= c <= NC + 1:
                    cc = c - 2
                    q = cc % 2
                    h3 = hs[:, q, :].rearrange("p (h x) -> p h x", h=MH)
                    dve.wait_ge(rs_done, cc + 1)
                    link(dve.tensor_tensor(h3, h3, spread(ss[:, q, :].unsqueeze(2), [P, MH, DV]), ALU.mult))
                    dve.wait_ge(og_in[q], 16 * (cc // 2 + 1))
                    dve.tensor_tensor(hs[:, q, :], hs[:, q, :], og[:, q, :], ALU.mult).then_inc(hn_done, 1)
                if (r == 3 and 1 <= c <= NC - 2) or (r == 0 and 2 <= c <= NC - 1):
                    decay_state(c if r == 3 else c - 1, 0 if r == 3 else 1)


def out_proj(nc, a, k, h, ah, al, scr):
    with ExitStack() as ctx:
        NT3 = 3 * KD
        raw = ctx.enter_context(nc.sbuf_tensor("raw_o", [P, 4, KD, P], F32))
        wh = ctx.enter_context(nc.sbuf_tensor("wh_o", [P, 2, KD, P], F32R))
        wl = ctx.enter_context(nc.sbuf_tensor("wl_o", [P, 2, KD, P], F32R))
        xr = ctx.enter_context(nc.sbuf_tensor("xr", [P, 2, T], F32))
        gt = ctx.enter_context(nc.sbuf_tensor("gt", [P, 2, T], F32))
        tm = ctx.enter_context(nc.sbuf_tensor("tm", [P, T], F32))
        acc = [ctx.enter_context(nc.psum_tensor(f"acc_o{i}", [P, 3, 512], F32))[:, :, 0:TB] for i in range(2)]
        w_hi, w_lo, a_hi, a_lo, tile_done, out_done, chain = open_sems(
            nc, ctx, "o_w_hi", "o_w_lo", "o_a_hi", "o_a_lo", "o_tile", "o_out", "chain_o")
        raw_in = open_sems(nc, ctx, *[f"o_raw{i}" for i in range(4)])
        xr_in = open_sems(nc, ctx, "o_xr0", "o_xr1")
        gt_in = open_sems(nc, ctx, "o_gt0", "o_gt1")
        block = ctx.enter_context(nc.Block())

        @block.sync
        def _(sp):
            def weight(i):
                if i >= 4:
                    sp.wait_ge(w_lo, i - 3)
                sp.dma_start(raw[:, i % 4, :, :], a["w_o"][i]).then_inc(raw_in[i % 4], 16)

            def operand(i):
                if i >= 2:
                    sp.wait_ge(a_lo, i - 1)
                src = scr["yn" if i < KD else "hm"][:, i % KD, :]
                sp.dma_start(xr[:, i % 2, :], src).then_inc(xr_in[i % 2], 16)

            for load, i0, i1 in ((weight, 0, 4), (operand, 0, KD), (weight, 4, 10), (operand, KD, KD + 2),
                                 (weight, 10, 12), (operand, KD + 2, 2 * KD), (weight, 12, NT3)):
                for i in range(i0, i1):
                    load(i)

        @block.gpsimd
        def _(pool):
            for i in range(NT3):
                if i >= 2:
                    pool.wait_ge(out_done, i - 1)
                src = scr["gate"][i] if i < 2 * KD else a["xT"][:, i - 2 * KD, :]
                pool.dma_start(gt[:, i % 2, :], src).then_inc(gt_in[i % 2], 16)

        @block.scalar
        def _(act):
            def weight(i):
                act.wait_ge(raw_in[i % 4], 16 * (i // 4 + 1))
                if i >= 2:
                    act.wait_ge(tile_done, i - 1)
                act.activation(wh[:, i % 2, :, :], raw[:, i % 4, :, :], ACT.Copy).then_inc(w_hi, 1)

            weight(0)
            for i in range(NT3):
                if i % KD == 0:
                    gi = i // KD
                    if gi:
                        act.wait_ge(tile_done, i)
                    if gi == 2:
                        act.wait_ge(out_done, i)
                    for q in range(KD):
                        n = i + q
                        if gi < 2:
                            act.wait_ge(xr_in[n % 2], 16 * (n // 2 + 1))
                        act.activation(ah[:, q, :], xr[:, n % 2, :] if gi < 2 else h[:, q, :],
                                       ACT.Copy).then_inc(a_hi, 1)
                if i + 1 < NT3:
                    weight(i + 1)

        @block.tensor
        def _(pe):
            for i in range(NT3):
                pe.wait_ge(w_hi, i + 1)
                pe.wait_ge(w_lo, i + 1)
                if i >= 2:
                    pe.wait_ge(out_done, i - 1)
                for kt in range(KD):
                    if i % KD == 0:
                        pe.wait_ge(a_lo, i + kt + 1)
                    m = split_product(pe, acc[i % 2], wh[:, i % 2, kt, :], wl[:, i % 2, kt, :], ah, al, kt,
                                      kt == KD - 1, kt == 0)
                m.then_inc(tile_done, 1)

        @block.vector
        def _(dve):
            link = Chain(dve, chain)

            def weight(i):
                dve.wait_ge(w_hi, i + 1)
                dve.tensor_tensor(wl[:, i % 2, :, :], raw[:, i % 4, :, :], wh[:, i % 2, :, :].bitcast(F32),
                                  ALU.subtract).then_inc(w_lo, 1)

            weight(0)
            for i in range(NT3):
                gi, q = i // KD, i % KD
                if q == 0:
                    for j in range(KD):
                        n = i + j
                        dve.wait_ge(a_hi, n + 1)
                        dve.tensor_tensor(al[:, j, :], xr[:, n % 2, :] if gi < 2 else h[:, j, :],
                                          ah[:, j, :].bitcast(F32), ALU.subtract).then_inc(a_lo, 1)
                    if gi == 2:
                        dve.wait_ge(a_lo, NT3)
                if i + 1 < NT3:
                    weight(i + 1)
                dve.wait_ge(tile_done, i + 1)
                dve.wait_ge(gt_in[i % 2], 16 * (i // 2 + 1))
                gate, dst = blocks(gt[:, i % 2, :]), blocks(h[:, q, :])
                if gi == 0:
                    link(dve.tensor_tensor(dst, acc[i % 2], gate, ALU.mult))
                elif gi == 1:
                    link(dve.tensor_tensor(blocks(tm[:, :]), acc[i % 2], gate, ALU.mult))
                    link(dve.tensor_tensor(h[:, q, :], h[:, q, :], tm[:, :], ALU.add))
                else:
                    for s, t, view in PARTS:
                        link(dve.scalar_tensor_tensor(out=part(h[:, q, :], t), in0=view(acc[i % 2]),
                                                      scalar=k["mod"][:, 16 + q, s:s + 1],
                                                      in1=part(gt[:, i % 2, :], t), op0=ALU.mult, op1=ALU.add))
                dve.sem_inc(out_done, 1)


def norm_ffn(nc, a, k, h, uh, ul):
    with ExitStack() as ctx:
        sq = ctx.enter_context(nc.sbuf_tensor("sq2", [P, 2, T], F32))
        xs = ctx.enter_context(nc.sbuf_tensor("xs2", [P, 3, T], F32))
        rstd = ctx.enter_context(nc.sbuf_tensor("rstd2", [P, T], F32))
        scl = ctx.enter_context(nc.sbuf_tensor("scl2", [P, KD, 2], F32))
        one = ctx.enter_context(nc.sbuf_tensor("one2", [P, P + 1], F32))
        ss_bank = ctx.enter_context(nc.psum_tensor("ss2", [P, 3, 512], F32))
        ss = ss_bank[:, :, 0:TB]
        one_set, sq_ready, sq_used, log, rstd_ready, scl_ready, xs_ready, u_ready, hi_done, lo_v, lo_p = open_sems(
            nc, ctx, *["n2_" + n for n in ("one", "sq_ready", "sq_used", "log", "rstd", "scl", "xs", "u", "hi",
                                           "lo_v", "lo_p")])
        block = ctx.enter_context(nc.Block())
        PART = ((0, slice(0, CTX)), (1, slice(CTX, T)))


        @block.scalar
        def _(act):
            for i in range(KD):
                if i >= 2:
                    act.wait_ge(sq_used, i - 1)
                act.activation(sq[:, i % 2, :], h[:, i, :], ACT.Square).then_inc(sq_ready, 1)
            act.wait_ge(sq_used, KD)
            act.wait_ge(one_set, 2)
            act.activation(blocks(rstd[:, :]), ss, ACT.Ln, bias=one[:, P:P + 1], scale=1.0 / D).then_inc(log, 1)
            act.wait_ge(log, 1)
            act.activation(rstd[:, :], rstd[:, :], ACT.Exp, scale=-0.5).then_inc(rstd_ready, 1)
            for i in range(KD):
                act.wait_ge(xs_ready, i + 1)
                for s, t in PART:
                    dst = xs[:, i % 3, t] if i % 2 else uh[:, i, t]
                    m = act.activation(dst, xs[:, i % 3, t], ACT.Identity, bias=k["mod"][:, 24 + i, s:s + 1])
                if i % 2:
                    m.then_inc(u_ready, 1)
                    act.wait_ge(u_ready, i // 2 + 1)
                    m = act.activation(uh[:, i, :], xs[:, i % 3, :], ACT.Copy)
                m.then_inc(hi_done, 1)

        @block.tensor
        def _(pe):
            pe.wait_ge(one_set, 1)
            for i in range(KD):
                pe.wait_ge(sq_ready, i + 1)
                for bank, t0, n in BLOCKS:
                    m = pe.matmul(ss[:, bank, 0:n], one[:, 0:P], sq[:, i % 2, t0:t0 + n], start=(i == 0),
                                  stop=(i == KD - 1))
                m.then_inc(sq_used, 1)

        @block.vector
        def _(dve):
            dve.memset(one[:, 0:P], 1.0).then_inc(one_set, 1)
            dve.memset(one[:, P:P + 1], EPS).then_inc(one_set, 1)
            for s in range(2):
                dve.scalar_tensor_tensor(out=scl[:, :, s], in0=k["mod"][:, 32:40, s], scalar=1.0,
                                         in1=col(k, "norm_ffn", 0, KD), op0=ALU.add,
                                         op1=ALU.mult).then_inc(scl_ready, 1)
            dve.wait_ge(scl_ready, 2)
            dve.wait_ge(rstd_ready, 1)

            def scaled(i):
                if i >= 3:
                    dve.wait_ge(*((lo_p, (i - 3) // 2 + 1) if (i - 3) % 2 else (lo_v, (i - 3) // 2 + 1)))
                for s, t in PART:
                    m = dve.scalar_tensor_tensor(out=xs[:, i % 3, t], in0=h[:, i, t], scalar=scl[:, i, s:s + 1],
                                                 in1=rstd[:, t], op0=ALU.mult, op1=ALU.mult)
                m.then_inc(xs_ready, 1)

            scaled(0)
            for i in range(KD):
                if i + 1 < KD:
                    scaled(i + 1)
                if i % 2 == 0:
                    dve.wait_ge(hi_done, i + 1)
                    for s, t in PART:
                        m = dve.scalar_tensor_tensor(out=ul[:, i, t], in0=xs[:, i % 3, t],
                                                     scalar=k["mod"][:, 24 + i, s:s + 1],
                                                     in1=uh[:, i, t].bitcast(F32), op0=ALU.add, op1=ALU.subtract)
                    m.then_inc(lo_v, 1)
            dve.wait_ge(lo_v, KD // 2)

        @block.gpsimd
        def _(pool):
            for i in range(1, KD, 2):
                pool.wait_ge(hi_done, i + 1)
                pool.tensor_tensor(ul[:, i, :], xs[:, i % 3, :], uh[:, i, :].bitcast(F32),
                                   ALU.subtract).then_inc(lo_p, 1)
            pool.wait_ge(lo_p, KD // 2)


def ffn(nc, a, k, h, uh, ul):
    with ExitStack() as ctx:
        NG, NU, RING, AR = FT // 2, 2 * FT, 2, 3
        PR, PW = ROWS + 2, GRID_W + 2
        PIECES = 3 * KD
        HALF = PIECES // 2
        raw = ctx.enter_context(nc.sbuf_tensor("raw_u", [P, RING, KD, P], F32))
        wh = ctx.enter_context(nc.sbuf_tensor("wh_u", [P, 2, KD, P], F32R))
        wl = ctx.enter_context(nc.sbuf_tensor("wl_u", [P, 2, KD, P], F32R))
        dr = ctx.enter_context(nc.sbuf_tensor("raw_d", [P, 2, D], F32))
        dh = ctx.enter_context(nc.sbuf_tensor("wh_d", [P, 2, D], F32R))
        dl = ctx.enter_context(nc.sbuf_tensor("wl_d", [P, 2, D], F32R))
        fh = ctx.enter_context(nc.sbuf_tensor("fh", [P, AR, T], F32R))
        fl = ctx.enter_context(nc.sbuf_tensor("fl", [P, AR, T], F32R))
        gp = ctx.enter_context(nc.sbuf_tensor("gp", [P, PR, PW], F32))
        gc = ctx.enter_context(nc.sbuf_tensor("gc", [P, CTX + 2], F32))
        y = ctx.enter_context(nc.sbuf_tensor("y", [P, 2, T], F32))
        acc = [ctx.enter_context(nc.psum_tensor(f"acc_u{i}", [P, 3, 512], F32))[:, :, 0:TB] for i in range(2)]
        dacc = ctx.enter_context(nc.psum_tensor("dacc", [P, 2, 512], F32))
        (w_hi, w_lo, d_in, d_hi, d_lo, up_done, g_evac, pad_zero, conv_done, silu_done, act_done, f_hi, f_lo,
         piece_done, piece_used, down_done, chain) = open_sems(
            nc, ctx, *["u_" + n for n in (
                "w_hi", "w_lo", "d_in", "d_hi", "d_lo", "up_done", "g_evac", "pad_zero", "conv_done", "silu_done",
                "act_done", "f_hi", "f_lo", "piece_done", "piece_used", "down_done", "chain")])
        raw_in = open_sems(nc, ctx, *[f"u_raw{i}" for i in range(RING)])
        block = ctx.enter_context(nc.Block())

        @block.sync
        def _(sp):
            for i in range(NU):
                if i >= RING:
                    sp.wait_ge(w_lo, i - RING + 1)
                sp.dma_start(raw[:, i % RING, :, :], a["w_up"][i]).then_inc(raw_in[i % RING], 16)
                if i % 4 == 1:
                    if i // 4:
                        sp.wait_ge(d_lo, i // 4)
                    sp.dma_start(dr[:, :, :], a["w_down"][i // 4]).then_inc(d_in, 16)

        @block.tensor
        def _(pe):
            def up(i):
                pe.wait_ge(w_hi, i + 1)
                pe.wait_ge(w_lo, i + 1)
                f = i // 2
                if f >= 1:
                    if i % 2 == 0:
                        pe.wait_ge(g_evac, f)
                    else:
                        pe.wait_ge(act_done, f)
                for kt in range(KD):
                    m = split_product(pe, acc[i % 2], wh[:, i % 2, kt, :], wl[:, i % 2, kt, :], uh, ul, kt,
                                      kt == KD - 1, kt == 0)
                m.then_inc(up_done, 1)

            def down(q0, q1):
                j = q0 // PIECES
                pe.wait_ge(d_hi, j + 1)
                pe.wait_ge(d_lo, j + 1)
                pe.wait_ge(f_hi, 2 * j + 2)
                pe.wait_ge(f_lo, 2 * j + 2)
                for q in range(q0, q1):
                    m_, (bank, t0, n) = q % PIECES // 3, BLOCKS[q % 3]
                    if q >= 2:
                        pe.wait_ge(piece_used, q - 1)
                    cols = slice(m_ * P, m_ * P + P)
                    for r in range(2):
                        s = (2 * j + r) % AR
                        for p_, (w, x) in enumerate(((dh, fh), (dh, fl), (dl, fh))):
                            m = pe.matmul(dacc[:, q % 2, 0:n], w[:, r, cols], x[:, s, t0:t0 + n],
                                          start=(r == 0 and p_ == 0), stop=(r == 1 and p_ == 2))
                    m.then_inc(piece_done, 1)

            for f in range(FT):
                up(2 * f)
                if f >= 2:
                    down(HALF * (f - 2), HALF * (f - 1))
                up(2 * f + 1)
            down(HALF * (FT - 2), HALF * FT)

        @block.scalar
        def _(act):
            def high(i):
                act.wait_ge(raw_in[i % RING], 16 * (i // RING + 1))
                if i >= 2:
                    act.wait_ge(up_done, i - 1)
                act.activation(wh[:, i % 2, :, :], raw[:, i % RING, :, :], ACT.Copy).then_inc(w_hi, 1)

            def high_down(j):
                act.wait_ge(d_in, 16 * (j + 1))
                if j:
                    act.wait_ge(piece_done, 3 * KD * j)
                act.activation(dh[:, :, :], dr[:, :, :], ACT.Copy).then_inc(d_hi, 1)

            def evac(f):
                act.wait_ge(up_done, 2 * f + 1)
                if f == 0:
                    act.wait_ge(pad_zero, 2)
                else:
                    act.wait_ge(conv_done, f)
                act.activation(gc[:, 1:1 + CTX], PARTS[0][2](acc[0]), ACT.Copy)
                r = (TB - CTX) // GRID_W
                act.activation(gp[:, 1:1 + r, 1:1 + GRID_W],
                               PARTS[1][2](acc[0]).rearrange("p (r w) -> p r w", w=GRID_W), ACT.Copy)
                for b in (1, 2):
                    r0 = 1 + (b * TB - CTX) // GRID_W
                    m = act.activation(gp[:, r0:r0 + TB // GRID_W, 1:1 + GRID_W],
                                       acc[0][:, b, :].rearrange("p (r w) -> p r w", w=GRID_W), ACT.Copy)
                m.then_inc(g_evac, 1)

            def silu(f):
                act.wait_ge(conv_done, f + 1)
                act.activation(y[:, f % 2, :], y[:, f % 2, :], ACT.Silu,
                               bias=col(k, "ffn_b", f)).then_inc(silu_done, 1)

            def act_high(f):
                act.wait_ge(act_done, f + 1)
                if f >= AR:
                    act.wait_ge(piece_done, 3 * KD * ((f - AR) // 2 + 1))
                act.activation(fh[:, f % AR, :], y[:, f % 2, :], ACT.Copy).then_inc(f_hi, 1)

            high(0)
            high(1)
            for f in range(FT):
                evac(f)
                if 2 * f + 2 < NU:
                    high(2 * f + 2)
                silu(f)
                if 2 * f + 3 < NU:
                    high(2 * f + 3)
                act_high(f)
                if f % 2 == 1:
                    high_down(f // 2)

        @block.vector
        def _(dve):
            link = Chain(dve, chain)
            dve.memset(gp[:, :, :], 0.0).then_inc(pad_zero, 1)
            dve.memset(gc[:, :], 0.0).then_inc(pad_zero, 1)

            def conv(f):
                q = HALF * (f - 2)

                def pieces(n):
                    if f >= 2:
                        add_down(q + 3 * n, q + 3 * n + 3)

                pieces(0)
                dve.wait_ge(g_evac, f + 1)
                if f >= 2:
                    dve.wait_ge(f_lo, f - 1)
                yc = y[:, f % 2, 0:CTX]
                yl = y[:, f % 2, CTX:T].rearrange("p (r w) -> p r w", w=GRID_W)
                for n, (dx, tap) in enumerate(((0, 3), (1, 4), (2, 5))):
                    w = col(k, "ffn_w", 9 * f + tap)
                    x = gc[:, dx:dx + CTX]
                    link(dve.tensor_scalar(yc, x, w, None, ALU.mult) if n == 0 else
                         dve.scalar_tensor_tensor(out=yc, in0=x, scalar=w, in1=yc, op0=ALU.mult, op1=ALU.add))
                for tap in range(9):
                    if tap in (1, 2, 3):
                        pieces(tap)
                    if tap == 5 and 2 * f + 2 < NU:
                        low(2 * f + 2)
                    w = col(k, "ffn_w", 9 * f + tap)
                    x = gp[:, tap // 3:tap // 3 + ROWS, tap % 3:tap % 3 + GRID_W]
                    if tap == 0:
                        link(dve.tensor_scalar(yl, x, w, None, ALU.mult))
                    else:
                        ins = dve.scalar_tensor_tensor(out=yl, in0=x, scalar=w, in1=yl, op0=ALU.mult, op1=ALU.add)
                        if tap < 8:
                            link(ins)
                ins.then_inc(conv_done, 1)

            def low(i):
                dve.wait_ge(w_hi, i + 1)
                dve.tensor_tensor(wl[:, i % 2, :, :], raw[:, i % RING, :, :], wh[:, i % 2, :, :].bitcast(F32),
                                  ALU.subtract).then_inc(w_lo, 1)

            def times_value(f):
                dve.wait_ge(silu_done, f + 1)
                dve.wait_ge(up_done, 2 * f + 2)
                yb = blocks(y[:, f % 2, :])
                dve.tensor_tensor(yb, yb, acc[1], ALU.mult).then_inc(act_done, 1)

            def low_down(j):
                dve.wait_ge(d_hi, j + 1)
                dve.tensor_tensor(dl[:, :, :], dr[:, :, :], dh[:, :, :].bitcast(F32),
                                  ALU.subtract).then_inc(d_lo, 1)

            def add_down(q0, q1):
                for q in range(q0, q1):
                    m_, (bank, t0, n) = q % PIECES // 3, BLOCKS[q % 3]
                    dve.wait_ge(piece_done, q + 1)
                    for s_, p0, p1 in (((0, 0, CTX), (1, CTX, TB)) if bank == 0 else ((1, 0, TB),)):
                        x = h[:, m_, t0 + p0:t0 + p1]
                        ins = dve.scalar_tensor_tensor(out=x, in0=dacc[:, q % 2, p0:p1],
                                                       scalar=k["mod"][:, 40 + m_, s_:s_ + 1], in1=x,
                                                       op0=ALU.mult, op1=ALU.add)
                    ins.then_inc(piece_used, 1)

            low(0)
            low(1)
            for f in range(FT):
                conv(f)
                times_value(f)
                if 2 * f + 3 < NU:
                    low(2 * f + 3)
                if f % 2 == 1:
                    low_down(f // 2)
            add_down(HALF * (FT - 2), HALF * FT)

        @block.gpsimd
        def _(pool):
            for f in range(FT):
                pool.wait_ge(f_hi, f + 1)
                if f >= AR:
                    pool.wait_ge(piece_done, 3 * KD * ((f - AR) // 2 + 1))
                pool.tensor_tensor(fl[:, f % AR, :], y[:, f % 2, :], fh[:, f % AR, :].bitcast(F32),
                                   ALU.subtract).then_inc(f_lo, 1)
            pool.wait_ge(f_lo, FT)


def final_norm(nc, a, k, h, o):
    with ExitStack() as ctx:
        sq = ctx.enter_context(nc.sbuf_tensor("sq3", [P, 2, T], F32))
        out = ctx.enter_context(nc.sbuf_tensor("out3", [P, 2, T], F32))
        rstd = ctx.enter_context(nc.sbuf_tensor("rstd3", [P, T], F32))
        one = ctx.enter_context(nc.sbuf_tensor("one3", [P, P + 1], F32))
        ss_bank = ctx.enter_context(nc.psum_tensor("ss3", [P, 3, 512], F32))
        ss = ss_bank[:, :, 0:TB]
        one_set, sq_ready, sq_used, root, rstd_ready, y_ready = open_sems(
            nc, ctx, *["n3_" + n for n in ("one", "sq_ready", "sq_used", "root", "rstd", "y")])
        y_out = o["y0_out"], o["y1_out"]
        block = ctx.enter_context(nc.Block())

        @block.scalar
        def _(act):
            for i in range(KD):
                if i >= 2:
                    act.wait_ge(sq_used, i - 1)
                act.activation(sq[:, i % 2, :], h[:, i, :], ACT.Square).then_inc(sq_ready, 1)
            act.wait_ge(sq_used, KD)
            act.wait_ge(one_set, 2)
            act.activation(blocks(rstd[:, :]), ss, ACT.Sqrt, bias=one[:, P:P + 1], scale=1.0 / D).then_inc(root, 1)

        @block.tensor
        def _(pe):
            pe.wait_ge(one_set, 1)
            for i in range(KD):
                pe.wait_ge(sq_ready, i + 1)
                for bank, t0, n in BLOCKS:
                    m = pe.matmul(ss[:, bank, 0:n], one[:, 0:P], sq[:, i % 2, t0:t0 + n], start=(i == 0),
                                  stop=(i == KD - 1))
                m.then_inc(sq_used, 1)

        @block.vector
        def _(dve):
            dve.memset(one[:, 0:P], 1.0).then_inc(one_set, 1)
            dve.memset(one[:, P:P + 1], EPS).then_inc(one_set, 1)
            dve.wait_ge(root, 1)
            dve.reciprocal(rstd[:, :], rstd[:, :]).then_inc(rstd_ready, 1)
            dve.wait_ge(rstd_ready, 1)
            for i in range(KD):
                if i >= 2:
                    dve.wait_ge(y_out[i % 2], 16 * (i // 2))
                dve.scalar_tensor_tensor(out=out[:, i % 2, :], in0=h[:, i, :], scalar=col(k, "final_norm", i),
                                         in1=rstd[:, :], op0=ALU.mult, op1=ALU.mult).then_inc(y_ready, 1)

        @block.sync
        def _(sp):
            for i in range(KD):
                sp.wait_ge(y_ready, i + 1)
                sp.dma_start(o["y"][:, i, :], out[:, i % 2, :]).then_inc(y_out[i % 2], 16)
            for s in range(2):
                sp.wait_ge(y_out[s], 16 * (KD // 2))


def constants():
    i, j = np.arange(P)[:, None], np.arange(P)[None, :]
    con = np.zeros((P, NCON), np.float32)
    for name, m in (("ident", i == j), ("le", i <= j), ("gt", i > j), ("ge", i >= j), ("lt", i < j),
                    ("ones", i >= 0), ("row127", i == P - 1), ("row0", i == 0)):
        con[:, CC[name]:CC[name] + P] = np.broadcast_to(m, (P, P))
    r = np.arange(P)
    con[:, CC["sign"]] = np.where(r < 32, 1.0, -1.0)
    con[:, CC["fwd"]] = (r >= 32) & (r < 40)
    con[:, CC["bwd"]] = (r >= 40) & (r < 48)
    con[:, CC["eps"]] = EPS
    con[:, CC["half0"]] = r < 64
    con[:, CC["half1"]] = r >= 64
    for q in range(16):
        con[32 + q, CC["i16"] + q] = 1.0
    selm = np.zeros((48, 16, P), np.float32)
    selq = np.zeros((48, 8, P), np.float32)
    for q in range(16):
        selm[32 + q, q, :] = 1.0
        selq[32 + q, q // 2, 64 * (q % 2):64 * (q % 2) + 64] = 1.0
    return con, selm, selq


def tiles(w, cols, width):
    w = np.ascontiguousarray(w[:, cols] if cols is not None else w)
    return w.reshape(-1, P, w.shape[1] // width, width).transpose(2, 1, 0, 3)


def lay_out(i):
    f = {n: np.asarray(v) for n, v in i.items()}
    x = np.concatenate([f["x_prompt"][0], f["x_sample"][0]], 0)
    a = {"xT": x.T.reshape(KD, P, T).transpose(1, 0, 2)}
    a["cond"] = np.stack([f["c_ctx"], f["c"][0]], 1).reshape(KD, P, 2).transpose(1, 0, 2)
    a["w_ada"] = tiles(f["w_ada"][0], None, P)
    w = f["w_in"][0]
    at = {}
    n0 = 0
    for name, n in (("z", D), ("xbc", XBC), ("dt", 32), ("q", 512), ("k", 512), ("v", D), ("o", D), ("i", 16),
                    ("f", 16), ("g", 2 * D)):
        at[name] = w[:, n0:n0 + n]
        n0 += n
    zero = np.zeros((D, P), np.float32)
    ta = np.concatenate([at["dt"], at["f"], zero[:, 48:]], 1)
    tb = np.concatenate([zero[:, :32], at["i"], zero[:, 48:]], 1)
    a["w_in_ch"] = tiles(np.concatenate([ta, tb, at["xbc"], at["q"], at["k"], at["g"]], 1), None, P)
    a["w_in_tok"] = tiles(np.concatenate([at["z"], at["v"], at["o"]], 1), None, 512)
    a["w_o"] = np.concatenate([tiles(f[n][0], None, P) for n in ("w_o_ssd", "w_o_ml", "w_out")], 0)
    up = f["w_up"][0]
    a["w_up"] = np.stack([tiles(up[:, :FF], None, P), tiles(up[:, FF:], None, P)], 1).reshape(2 * FT, P, KD, P)
    a["w_down"] = f["w_down"][0].reshape(FT // 2, 2, P, D).transpose(0, 2, 1, 3)

    par = np.zeros((P, NPAR), np.float32)

    def put(name, v):
        v = v.reshape(-1, P).T
        par[:, PC[name]:PC[name] + v.shape[1]] = v

    for name in ("norm_mix", "b_ada", "norm_ffn", "ssd_norm", "ml_norm"):
        put(name, f[name][0])
    put("final_norm", f["final_norm"])
    put("conv_b", f["ssd_conv_b"][0])
    put("conv_w", f["ssd_conv_w"][0].reshape(3, XT, P).transpose(1, 0, 2))
    put("ffn_b", f["ffn_conv_b"][0])
    put("ffn_w", f["ffn_conv_w"][0].reshape(9, FT, P).transpose(1, 0, 2))
    par[0:32, PC["gate_bias"]] = f["ssd_dt_bias"][0].reshape(-1)
    par[32:48, PC["gate_bias"]] = f["ml_f_bias"][0].reshape(-1)
    par[32:48, PC["i_bias"]] = f["ml_i_bias"][0].reshape(-1)
    par[0:32, PC["a_log"]] = f["ssd_a_log"][0].reshape(-1)
    par[32:48, PC["m0"]] = f["state_mlstm_m"][0, 0].reshape(-1)
    a["params"] = par
    a["ssd_d"] = np.broadcast_to(np.repeat(f["ssd_d"][0], SP)[None], (P, D))
    s = f["state_ssd"][0, 0].reshape(2, 2, 2, HG, SP, SN).transpose(2, 5, 0, 1, 3, 4)
    a["s_ssd"] = s.reshape(P, 2, 512)
    cn = np.concatenate([f["state_mlstm_C"][0, 0], f["state_mlstm_n"][0, 0][:, :, None, :]], 2)
    a["s_ml"] = cn.reshape(2, 4, 2, DV1, DK).transpose(2, 4, 0, 1, 3).reshape(P, 2, 4, DV1)
    a["consts"], a["selm"], a["selq"] = constants()
    return {n: np.ascontiguousarray(v) for n, v in a.items()}


OUTS = {"y": (P, KD, T), "ssd": (P, 2, 512), "ml": (P, 2, 4, DV1), "m": (16, 1)}


def kernel(**inputs):
    import concourse.bacc as bacc
    from concourse.bass_utils import run_bass_kernel_spmd

    nc = bacc.Bacc("TRN2", target_bir_lowering=False, num_devices=1)
    arrays = {f"in_{n}": v for n, v in lay_out(inputs).items()}
    a = {n[3:]: nc.dram_tensor(n, v.shape, F32, kind="ExternalInput").ap() for n, v in arrays.items()}
    o = {n: nc.dram_tensor(f"out_{n}", s, F32, kind="ExternalOutput").ap() for n, s in OUTS.items()}
    build(nc, a, o)
    got = run_bass_kernel_spmd(nc, [arrays], core_ids=[0]).results[0]
    y = got["out_y"].transpose(2, 1, 0).reshape(T, D)
    s = got["out_ssd"].reshape(2, SN, 2, 2, HG, SP).transpose(2, 3, 0, 4, 5, 1).reshape(1, 1, 2, SH, SP, SN)
    cn = got["out_ml"].reshape(2, DK, 2, 4, DV1).transpose(2, 3, 0, 4, 1).reshape(1, 1, 2, MH, DV1, DK)
    c = np.ascontiguousarray
    return (c(y[None, :CTX]), c(y[None, CTX:]), c(s), c(cn[:, :, :, :, :DV]), c(cn[:, :, :, :, DV]),
            c(got["out_m"].reshape(1, 1, 2, MH)))
```

```python
from contextlib import ExitStack

import numpy as np

import concourse.bass as bass
from concourse import mybir

F32 = mybir.dt.float32
F32R = mybir.dt.float32r
BF16 = mybir.dt.bfloat16
ACT = mybir.ActivationFunctionType
ALU = mybir.AluOpType
AX = mybir.AxisListType

P = 128
D = 1024
KD = D // P
CTX = 128
LAT = 1024
T = CTX + LAT
C = 128
NC = T // C
EPS = 1e-6
SH, SP, SG, SN = 16, 64, 4, 64
HG = SH // SG
MH, DV, DK = 8, 128, 64
DV1 = DV + 1
XBC = 1536
XT = XBC // P
FF = 2816
FT = FF // P
GRID_W = 64
ROWS = LAT // GRID_W
NEG = -1.0e30
TB = 384
BLOCKS = tuple((b, b * TB, TB) for b in range(T // TB))
PARTS = ((0, slice(0, CTX), lambda x: x[:, 0, 0:CTX]),
         (1, slice(CTX, TB), lambda x: x[:, 0, CTX:TB]),
         (1, slice(TB, T), lambda x: x[:, 1:3, :]))

PC = {}
_at = 0
for _n, _w in (("norm_mix", KD), ("b_ada", 48), ("norm_ffn", KD), ("ssd_norm", KD), ("ml_norm", KD),
               ("conv_b", XT), ("conv_w", 3 * XT), ("ffn_b", FT), ("ffn_w", 9 * FT), ("final_norm", KD),
               ("gate_bias", 1), ("i_bias", 1), ("a_log", 1), ("m0", 1)):
    PC[_n] = _at
    _at += _w
NPAR = _at

CC = {}
_at = 0
for _n, _w in (("ident", P), ("le", P), ("gt", P), ("ge", P), ("lt", P), ("ones", P), ("row127", P),
               ("row0", P), ("sign", 1), ("fwd", 1), ("bwd", 1), ("eps", 1), ("half0", 1), ("half1", 1), ("i16", 16), ("s4", 2)):
    CC[_n] = _at
    _at += _w
NCON = _at

TX, TQ, TK, TG = 1, 13, 17, 21
NT = 37


def build(nc, a, o):
    scr = {
        "xbc": nc.dram_tensor("scr_xbc", [XT, P, T], F32).ap(),
        "qk": nc.dram_tensor("scr_qk", [8, P, T], F32).ap(),
        "gate": nc.dram_tensor("scr_gate", [16, P, T], F32).ap(),
        "zvo": nc.dram_tensor("scr_zvo", [3, NC, P, D], F32).ap(),
        "yn": nc.dram_tensor("scr_yn", [P, KD, T], F32).ap(),
        "hm": nc.dram_tensor("scr_hm", [P, KD, T], F32).ap(),
    }
    with ExitStack() as ctx:
        o = {**o, **{f"{n}_out": nc.alloc_semaphore(f"{n}_out") for n in ("ssd", "ml", "m", "y0", "y1")}}
        par = ctx.enter_context(nc.sbuf_tensor("par", [P, NPAR], F32))
        mod = ctx.enter_context(nc.sbuf_tensor("mod", [P, 48, 2], F32))
        k = {"par": par, "mod": mod}
        with ExitStack() as mix:
            k["con"] = mix.enter_context(nc.sbuf_tensor("con", [P, NCON], F32))
            g = {n: mix.enter_context(nc.sbuf_tensor(n, [P, NC, w], F32)) for n, w in
                 (("dt_ig", 48), ("dec", 48), ("ecum", 48), ("eend", 48), ("em", 16), ("dbc", 48))}
            g["negm"] = mix.enter_context(nc.sbuf_tensor("negm", [48, T], F32))
            with ExitStack() as proj:
                cond = proj.enter_context(nc.sbuf_tensor("cond", [P, KD, 4], F32R))
                uh = proj.enter_context(nc.sbuf_tensor("uh", [P, KD, T], F32R))
                ul = proj.enter_context(nc.sbuf_tensor("ul", [P, KD, T], F32R))
                with ExitStack() as ring:
                    raw = ring.enter_context(nc.sbuf_tensor("raw", [P, 4, KD, P], F32))
                    raw_in = open_sems(nc, ring, *[f"raw_in{i}" for i in range(4)])
                    norm_mix(nc, a, k, cond, uh, ul, raw, raw_in)
                    proj_ch(nc, a, k, g, cond, uh, ul, raw, raw_in, scr, o)
                proj_tok(nc, a, uh, ul, scr)
            ssd(nc, a, k, g, scr, o)
            mlstm(nc, a, k, g, scr, o)
        h = ctx.enter_context(nc.sbuf_tensor("h", [P, KD, T], F32))
        with ExitStack() as ff:
            uh = ff.enter_context(nc.sbuf_tensor("uh2", [P, KD, T], F32R))
            ul = ff.enter_context(nc.sbuf_tensor("ul2", [P, KD, T], F32R))
            up = {"raw": ff.enter_context(nc.sbuf_tensor("raw_u", [P, 2, KD, P], F32)),
                  "wh": ff.enter_context(nc.sbuf_tensor("wh_u", [P, 2, KD, P], F32R)),
                  "wl": ff.enter_context(nc.sbuf_tensor("wl_u", [P, 2, KD, P], F32R)),
                  "raw_in": open_sems(nc, ff, "u_raw0", "u_raw1")}
            up["w_hi"], up["w_lo"] = open_sems(nc, ff, "u_w_hi", "u_w_lo")
            out_proj(nc, a, k, h, uh, ul, up, scr)
            ffn(nc, a, k, h, uh, ul, up, o)


def col(k, name, i=0, n=1, rows=slice(0, P)):
    return k["par"][rows, PC[name] + i:PC[name] + i + n]


def const(k, name, rows=slice(0, P), n=None):
    n = n or (P if CC[name] < 8 * P else 1)
    return k["con"][rows, CC[name]:CC[name] + n]


class Chain:

    def __init__(self, eng, sem):
        self.eng, self.sem, self.n = eng, sem, 0

    def __call__(self, ins):
        self.n += 1
        ins.then_inc(self.sem, 1)
        self.eng.wait_ge(self.sem, self.n)


def open_sems(nc, ctx, *names):
    sems = [nc.alloc_semaphore(n) for n in names]
    ctx.callback(clear_sems, nc, sems)
    return sems


def clear_sems(nc, sems):
    nc.clear_and_free_semaphores(sems)
    nc.all_engine_barrier()


def spread(x, shape):
    return x.to_broadcast(shape)


def blocks(x):
    return x.rearrange("p (b n) -> p b n", n=TB)


def part(x, t):
    x = x[:, t]
    return blocks(x) if t.stop == T else x


def split_product(pe, acc, wh, wl, ah, al, kt, last_k, first=True):
    ins = None
    for w, act, s, e in ((wh, ah, True, False), (wh, al, False, False), (wl, ah, False, True)):
        for bank, t0, n in BLOCKS:
            ins = pe.matmul(acc[:, bank, 0:n], w, act[:, kt, t0:t0 + n],
                            start=(first and s), stop=(last_k and e))
    return ins


def ada_unit(pe, acc, cond, wh, wl, n):
    for kk in range(2):
        kt = 2 * (n % 4) + kk
        for w in (wh, wl):
            ins = pe.matmul(acc[0:4, :], cond[:, kt, :], w[:, 4 * kk:4 * kk + 4, :],
                            start=(kt == 0 and w is wh), stop=(kt == KD - 1 and w is wl))
    return ins


def ada_sum(pe, k, pmod, line, b):
    for j in range(4):
        ins = pe.matmul(pmod[:, 4 * b + j, :], line[0:4, j * P:(j + 1) * P], const(k, "s4", slice(0, 4), 2),
                        start=True, stop=True)
    return ins


def norm_mix(nc, a, k, cond, uh, ul, raw, raw_in):
    with ExitStack() as ctx:
        RING, WS = 6, 3
        x = ctx.enter_context(nc.sbuf_tensor("x", [P, KD, T], F32))
        own = ctx.enter_context(nc.sbuf_tensor("wa", [P, RING - 4, KD, P], F32))
        wa = [raw[:, n, :, :] for n in range(4)] + [own[:, n, :, :] for n in range(RING - 4)]
        wh = ctx.enter_context(nc.sbuf_tensor("wa_h", [P, WS, KD, P], F32R))
        wl = ctx.enter_context(nc.sbuf_tensor("wa_l", [P, WS, KD, P], F32R))
        line = ctx.enter_context(nc.sbuf_tensor("mod_line", [4, 2, 512], F32))
        ssq = ctx.enter_context(nc.sbuf_tensor("ssq", [P, T], F32))
        u = ctx.enter_context(nc.sbuf_tensor("u", [P, 3, T], F32))
        sq = u[:, 0:2, :]
        rstd = ctx.enter_context(nc.sbuf_tensor("rstd", [P, T], F32))
        scl = ctx.enter_context(nc.sbuf_tensor("scl", [P, KD, 2], F32))
        craw = ctx.enter_context(nc.sbuf_tensor("craw", [P, KD, 2], F32))
        acc = ctx.enter_context(nc.psum_tensor("ada", [4, 2, 512], F32))
        ss_bank = ctx.enter_context(nc.psum_tensor("ss", [P, 3, 512], F32))
        ss = ss_bank[:, :, 0:TB]
        pmod = ctx.enter_context(nc.psum_tensor("pmod", [P, 48, 2], F32))
        (par_in, con_in, cond_in, sq_ready, sq_used, ss_done, log, rstd_ready, mod_done, cond_ready,
         scl_ready, xn_ready, u_ready, hi_done, lo_v, lo_p, chain) = open_sems(
            nc, ctx, "par_in", "con_in", "cond_in", "sq_ready", "sq_used", "ss_done", "log", "rstd_ready",
            "mod_done", "cond_ready", "scl_ready", "xn_ready", "u_ready", "hi_done", "lo_v", "lo_p", "chain_nm")
        x_in = open_sems(nc, ctx, *[f"x_in{i}" for i in range(KD)])
        wa_in = open_sems(nc, ctx, *[f"wa_in{i}" for i in range(RING)])
        wa_hi, wa_lo, unit_done, line_ready, cond_lo, xn_pool = open_sems(nc, ctx, "wa_hi", "wa_lo", "unit_done",
                                                                 "line_ready", "cond_lo", "xn_pool")
        block = ctx.enter_context(nc.Block())
        NA = 16
        PART = ((0, slice(0, CTX)), (1, slice(CTX, T)))

        def low_part(eng, i):
            eng.wait_ge(hi_done, i + 1)
            return eng.tensor_tensor(ul[:, i, :], u[:, i % 3, :], uh[:, i, :].bitcast(F32), ALU.subtract)

        @block.sync
        def _(sp):
            sp.dma_start(craw[:, :, :], a["cond"]).then_inc(cond_in, 16)
            for i in range(KD):
                sp.dma_start(x[:, i, :], a["xT"][:, i, :]).then_inc(x_in[i], 16)
            sp.dma_start(k["con"][:, :], a["consts"]).then_inc(con_in, 16)
            sp.dma_start(k["par"][:, :], a["params"]).then_inc(par_in, 16)
            for j in range(NA):
                if j >= RING:
                    sp.wait_ge(wa_lo, j - RING + 1)
                sp.dma_start(wa[j % RING], a["w_ada"][j]).then_inc(wa_in[j % RING], 16)
            for n in range(4):
                sp.wait_ge(wa_lo, NA - 4 + n + 1)
                sp.dma_start(raw[:, n, :, :], first_load(a, n)).then_inc(raw_in[n], 16)

        @block.scalar
        def _(act):
            act.wait_ge(cond_in, 16)
            def high(j):
                act.wait_ge(wa_in[j % RING], 16 * (j // RING + 1))
                if j >= WS:
                    act.wait_ge(unit_done, j - WS + 1)
                act.activation(wh[:, j % WS, :, :], wa[j % RING], ACT.Copy).then_inc(wa_hi, 1)

            act.activation(craw[:, :, :], craw[:, :, :], ACT.Silu).then_inc(cond_ready, 1)
            act.wait_ge(cond_ready, 1)
            act.activation(cond[:, :, 0:2], craw[:, :, :], ACT.Copy).then_inc(cond_ready, 1)
            for i in range(KD):
                act.wait_ge(x_in[i], 16)
                if i >= 2:
                    act.wait_ge(sq_used, i - 1)
                act.activation(sq[:, i % 2, :], x[:, i, :], ACT.Square).then_inc(sq_ready, 1)
            high(0)
            high(1)
            high(2)
            act.wait_ge(ss_done, 1)
            act.wait_ge(con_in, 16)
            act.activation(blocks(rstd[:, :]), ss, ACT.Ln, bias=const(k, "eps"), scale=1.0 / D).then_inc(log, 1)
            act.wait_ge(log, 1)
            act.activation(rstd[:, :], rstd[:, :], ACT.Exp, scale=-0.5).then_inc(rstd_ready, 1)
            def line_out(b):
                if b >= 2:
                    act.wait_ge(mod_done, b - 1)
                act.wait_ge(unit_done, 4 * b + 4)
                act.activation(line[:, b % 2, :], acc[:, b % 2, :], ACT.Copy).then_inc(line_ready, 1)

            for j in range(3, NA):
                high(j)
                if j % 4 == 0 and j:
                    line_out(j // 4 - 1)
            line_out(NA // 4 - 1)
            act.wait_ge(scl_ready, 2)
            act.wait_ge(xn_ready, KD // 2)
            act.wait_ge(xn_pool, KD // 2)
            for i in range(KD):
                for s, t in PART:
                    m = act.activation(uh[:, i, t], x[:, i, t], ACT.Identity, bias=k["mod"][:, i, s:s + 1],
                                       scale=scl[:, i, s:s + 1])
                m.then_inc(hi_done, 1)

        @block.tensor
        def _(pe):
            pe.wait_ge(con_in, 16)
            pe.wait_ge(sq_used, KD)
            for bank, t0, n in BLOCKS:
                m = pe.matmul(ss[:, bank, 0:n], const(k, "ones"), ssq[:, t0:t0 + n], start=True, stop=True)
            m.then_inc(ss_done, 1)
            pe.wait_ge(cond_ready, 2)
            pe.wait_ge(cond_lo, 1)
            for j in range(NA):
                pe.wait_ge(wa_hi, j + 1)
                pe.wait_ge(wa_lo, j + 1)
                b = j // 4
                if j % 4 == 0 and b >= 2:
                    pe.wait_ge(line_ready, b - 1)
                ada_unit(pe, acc[:, b % 2, :], cond, wh[:, j % WS], wl[:, j % WS], j).then_inc(unit_done, 1)
                if j % 4 == 1 and b or j == NA - 1:
                    bs = b if j == NA - 1 else b - 1
                    pe.wait_ge(line_ready, bs + 1)
                    ada_sum(pe, k, pmod, line[:, bs % 2, :], bs).then_inc(mod_done, 1)

        @block.vector
        def _(dve):
            link = Chain(dve, chain)
            dve.wait_ge(cond_ready, 2)
            dve.tensor_tensor(cond[:, :, 2:4], craw[:, :, :], cond[:, :, 0:2].bitcast(F32),
                              ALU.subtract).then_inc(cond_lo, 1)
            for i in range(KD):
                dve.wait_ge(sq_ready, i + 1)
                if i == 0:
                    dve.tensor_copy(ssq[:, :], sq[:, 0, :]).then_inc(sq_used, 1)
                else:
                    dve.tensor_tensor(ssq[:, :], ssq[:, :], sq[:, i % 2, :], ALU.add).then_inc(sq_used, 1)
                dve.wait_ge(sq_used, i + 1)
            dve.wait_ge(par_in, 16)
            for j in range(NA):
                dve.wait_ge(wa_hi, j + 1)
                if j >= WS:
                    dve.wait_ge(unit_done, j - WS + 1)
                dve.tensor_tensor(wl[:, j % WS, :, :], wa[j % RING], wh[:, j % WS, :, :].bitcast(F32),
                                  ALU.subtract).then_inc(wa_lo, 1)
                if j % 4 == 3:
                    i = 2 * (j // 4)
                    dve.wait_ge(rstd_ready, 1)
                    dve.tensor_tensor(x[:, i, :], x[:, i, :], rstd[:, :], ALU.mult).then_inc(xn_ready, 1)
            dve.wait_ge(mod_done, NA // 4)
            link(dve.tensor_tensor(k["mod"][:, 0:NA, :], pmod[:, 0:NA, :],
                                   spread(col(k, "b_ada", 0, NA).unsqueeze(2), [P, NA, 2]), ALU.add))
            for s in range(2):
                dve.scalar_tensor_tensor(out=scl[:, :, s], in0=k["mod"][:, KD:2 * KD, s], scalar=1.0,
                                         in1=col(k, "norm_mix", 0, KD), op0=ALU.add,
                                         op1=ALU.mult).then_inc(scl_ready, 1)
            dve.wait_ge(scl_ready, 2)
            dve.wait_ge(xn_ready, KD // 2)
            dve.wait_ge(xn_pool, KD // 2)

            def modulated(i):
                if i >= 3:
                    dve.wait_ge(*((lo_p, (i - 3) // 2 + 1) if (i - 3) % 2 else (lo_v, (i - 3) // 2 + 1)))
                for s, t in PART:
                    m = dve.tensor_scalar(u[:, i % 3, t], x[:, i, t], scl[:, i, s:s + 1], k["mod"][:, i, s:s + 1],
                                          ALU.mult, ALU.add)
                m.then_inc(u_ready, 1)

            modulated(0)
            for i in range(KD):
                if i + 1 < KD:
                    modulated(i + 1)
                if i % 2 == 0:
                    dve.wait_ge(u_ready, i + 1)
                    low_part(dve, i).then_inc(lo_v, 1)
            dve.wait_ge(lo_v, KD // 2)

        @block.gpsimd
        def _(pool):
            pool.wait_ge(rstd_ready, 1)
            for i in range(1, KD, 2):
                pool.tensor_tensor(x[:, i, :], x[:, i, :], rstd[:, :], ALU.mult).then_inc(xn_pool, 1)
            for i in range(1, KD, 2):
                pool.wait_ge(u_ready, i + 1)
                low_part(pool, i).then_inc(lo_p, 1)
            pool.wait_ge(lo_p, KD // 2)


def schedule():
    jobs, units, n = [], {i: [] for i in range(NT)}, 16
    for i in range(NT):
        jobs.append(("w", i))
        for _ in range(2 if i == 22 else 1):
            if n < 48:
                units[i].append(n)
                jobs.append(("ada", n))
                n += 1
    return jobs, units


def first_load(a, n):
    kind, i = schedule()[0][n]
    return a["w_in_ch" if kind == "w" else "w_ada"][i]


def proj_ch(nc, a, k, g, cond, uh, ul, raw, raw_in, scr, o):
    with ExitStack() as ctx:
        RING, ORING, PADT = 4, 3, T + 4
        wh = ctx.enter_context(nc.sbuf_tensor("wh", [P, 2, KD, P], F32R))
        wl = ctx.enter_context(nc.sbuf_tensor("wl", [P, 2, KD, P], F32R))
        pad = ctx.enter_context(nc.sbuf_tensor("pad", [P, 2, PADT], F32))
        cv = ctx.enter_context(nc.sbuf_tensor("cv", [P, 2, PADT], F32))
        ob = ctx.enter_context(nc.sbuf_tensor("ob", [P, ORING, T], F32))
        acc = [ctx.enter_context(nc.psum_tensor(f"acc{i}", [P, 3, 512], F32))[:, :, 0:TB] for i in range(2)]
        ah = ctx.enter_context(nc.sbuf_tensor("ada_h", [P, KD, P], F32R))
        al = ctx.enter_context(nc.sbuf_tensor("ada_l", [P, KD, P], F32R))
        line = ctx.enter_context(nc.sbuf_tensor("mod_line2", [4, 512], F32))
        modbank = ctx.enter_context(nc.psum_tensor("pmod2", [P, 512], F32))
        pmod = modbank[:, 0:96].rearrange("p (i s) -> p i s", s=2)
        ML = slice(32, 48)
        row = {n: ctx.enter_context(nc.sbuf_tensor("row_" + n, [48, T], F32)) for n in
               ("a", "b", "e", "u", "l", "sp", "w")}
        row["x"] = row["g2"] = row["a"]
        row["d"], row["mf"], row["mb"], row["mm"] = row["b"], row["e"], row["u"], row["l"]
        pm = ctx.enter_context(nc.sbuf_tensor("g_pm", [48, 2, NC], F32))
        pp = ctx.enter_context(nc.sbuf_tensor("g_pp", [48, NC], F32))
        mn = ctx.enter_context(nc.sbuf_tensor("g_mn", [48, NC], F32))
        ac = ctx.enter_context(nc.sbuf_tensor("g_ac", [48, 1], F32))
        end = ctx.enter_context(nc.sbuf_tensor("g_end", [P, NC, 48], F32))
        pg = ctx.enter_context(nc.psum_tensor("pg", [P, 512], F32))
        tok = pg[:, 0:NC * 48].rearrange("p (c r) -> p c r", c=NC)
        tok_m = modbank[:, 96:96 + NC * 16].rearrange("p (c r) -> p c r", c=NC)
        ada = pg[0:4, :]
        GATE_STEPS = {31 + n: name for n, name in enumerate(("dt_ig", "dec", "ecum", "end", "dbc"))}
        (hi_done, lo_done, tile_done, evac_done, mod_done, pad_zero, pad_ready, conv_done,
         ob_ready, chain) = open_sems(
            nc, ctx, "w_hi_done", "w_lo_done", "tile_done", "evac_done", "mod2_done", "pad_zero", "pad_ready",
            "conv_done", "ob_ready", "chain_pc")
        ada_hi, ada_lo, unit_done, line_ready = open_sems(nc, ctx, "ada_hi", "ada_lo", "ada_unit", "ada_line")
        chain_rows, ex, u1, ln_in, ln_out, a_exp, rows_done, tok_done, tok_out, ends_done, em_out = open_sems(
            nc, ctx, "chain_rows", "g_exp", "g_u1", "g_ln_in", "g_ln_out", "g_aexp", "rows_done", "g_tok_done",
            "g_tok_out", "g_ends_done", "g_em_out")
        stored = open_sems(nc, ctx, *[f"stored{i}" for i in range(ORING)])
        block = ctx.enter_context(nc.Block())

        jobs, units = schedule()
        ada_ends = {i: n // 4 for i in range(NT) for n in units[i] if n % 4 == 3}
        slot = {job: n for n, job in enumerate(jobs)}
        outs = [i for i in range(NT) if i >= TX]

        def out_slot(i):
            return (i - TX) % ORING, (i - TX) // ORING

        @block.sync
        def _(sp):
            for n, (kind, i) in enumerate(jobs):
                if n < RING:
                    continue
                was, j = jobs[n - RING]
                if was == "w":
                    sp.wait_ge(hi_done, j + 1)
                    sp.wait_ge(lo_done, j + 1)
                else:
                    sp.wait_ge(ada_lo, j - 15)
                src = a["w_in_ch"][i] if kind == "w" else a["w_ada"][i]
                sp.dma_start(raw[:, n % RING, :, :], src).then_inc(raw_in[n % RING], 16)
            sp.wait_ge(rows_done, 1)
            with nc.allow_non_contiguous_dma(reason="eight single values"):
                sp.dma_start(o["m"][0:8, :], row["mf"][32:40, CTX - 1:CTX]).then_inc(o["m_out"], 16)
                sp.dma_start(o["m"][8:16, :], row["mb"][40:48, 0:1]).then_inc(o["m_out"], 16)
            sp.wait_ge(o["m_out"], 32)

        def arrived(eng, job):
            n = slot[job]
            eng.wait_ge(raw_in[n % RING], 16 * (n // RING + 1))
            return raw[:, n % RING, :, :]

        @block.tensor
        def _(pe):
            idn, i16 = const(k, "ident", slice(0, 48), 48), k["con"][ML, CC["i16"]:CC["i16"] + 16]
            quarters = (slice(0, 16), slice(16, 32), slice(32, 40), slice(40, 48))

            def gate_step(i):
                name, n = GATE_STEPS[i], i - min(GATE_STEPS)
                if n == 0:
                    pe.wait_ge(rows_done, 1)
                    pe.wait_ge(line_ready, 8)
                else:
                    pe.wait_ge(tok_out, n)
                for c in range(NC):
                    t = slice(c * C, (c + 1) * C)
                    if name in ("dt_ig", "dec"):
                        m = pe.transpose(tok[:, c, :], row["sp" if name == "dt_ig" else "g2"][:, t], idn)
                    if name == "dec":
                        m = pe.transpose(tok_m[:, c, :], g["negm"][ML, t], i16)
                if name in ("ecum", "end"):
                    masks, own = (("le", "ge"), "d") if name == "ecum" else (("gt", "lt"), "w")
                    for j, cols in enumerate(quarters):
                        pe.matmul(tok[:, :, cols], const(k, masks[j % 2]), g["dec"][:, :, cols], start=(j == 0),
                                  stop=False, skip_group_check=True)
                    for c in range(NC):
                        m = pe.matmul(tok[:, c, 32:48], row[own][ML, c * C:(c + 1) * C], i16, start=False,
                                      stop=(c == NC - 1), skip_group_check=True)
                if name == "dbc":
                    for j, cols in enumerate(quarters):
                        m = pe.matmul(tok[:, :, cols], const(k, ("row127", "row0")[j % 2]), g["ecum"][:, :, cols],
                                      start=(j == 0), stop=(j == 3), skip_group_check=True)
                m.then_inc(tok_done, 1)

            for kind, i in jobs:
                if kind == "w":
                    pe.wait_ge(hi_done, i + 1)
                    pe.wait_ge(lo_done, i + 1)
                    if i >= 2:
                        pe.wait_ge(evac_done, i - 1)
                    for kt in range(KD):
                        m = split_product(pe, acc[i % 2], wh[:, i % 2, kt, :], wl[:, i % 2, kt, :], uh, ul, kt,
                                          kt == KD - 1, kt == 0)
                    m.then_inc(tile_done, 1)
                    if i - 1 in ada_ends:
                        b = ada_ends[i - 1]
                        pe.wait_ge(line_ready, b - 3)
                        ada_sum(pe, k, pmod, line, b).then_inc(mod_done, 1)
                    if i in GATE_STEPS:
                        gate_step(i)
                else:
                    pe.wait_ge(ada_hi, i - 15)
                    pe.wait_ge(ada_lo, i - 15)
                    if i % 4 == 0 and i > 16:
                        pe.wait_ge(line_ready, i // 4 - 4)
                    ada_unit(pe, ada, cond, ah, al, i).then_inc(unit_done, 1)

        @block.scalar
        def _(act):
            def high(i):
                w = arrived(act, ("w", i))
                if i >= 2:
                    act.wait_ge(tile_done, i - 1)
                act.activation(wh[:, i % 2, :, :], w, ACT.Copy).then_inc(hi_done, 1)

            def out_free(i):
                s, n = out_slot(i)
                if n:
                    act.wait_ge(stored[s], 16 * n)

            def silu(i):
                act.wait_ge(conv_done, i - TX + 1)
                out_free(i)
                s, _ = out_slot(i)
                b = col(k, "conv_b", i - TX)
                act.activation(ob[:, s, 0:CTX], cv[:, i % 2, 1:1 + CTX], ACT.Silu, bias=b)
                act.activation(ob[:, s, CTX:T], cv[:, i % 2, CTX + 3:T + 3], ACT.Silu,
                               bias=b).then_inc(ob_ready, 1)

            def ada_high(n):
                w = arrived(act, ("ada", n))
                if n > 16:
                    act.wait_ge(unit_done, n - 16)
                act.activation(ah[:, :, :], w, ACT.Copy).then_inc(ada_hi, 1)

            act.activation(ac[0:32, :], col(k, "a_log", rows=slice(0, 32)), ACT.Exp).then_inc(a_exp, 1)
            high(0)
            for i in range(NT):
                if i + 1 < NT:
                    high(i + 1)
                if i - 1 in ada_ends:
                    b = ada_ends[i - 1]
                    act.wait_ge(unit_done, 4 * b - 12)
                    if b > 4:
                        act.wait_ge(mod_done, b - 4)
                    act.activation(line[:, :], ada, ACT.Copy).then_inc(line_ready, 1)
                for n in units[i][:1]:
                    ada_high(n)
                if i == TX + 1:
                    act.wait_ge(ex, 1)
                    act.activation(row["e"][:, :], row["e"][:, :], ACT.Exp, scale=-1.0).then_inc(u1, 1)
                if i == TX + 3:
                    act.wait_ge(ln_in, 1)
                    act.activation(row["l"][:, :], row["u"][:, :], ACT.Ln).then_inc(ln_out, 1)
                step = GATE_STEPS.get(i - 1)
                if step == "dec":
                    act.wait_ge(tok_done, i - min(GATE_STEPS))
                    act.activation(g["em"][:, :, :], tok_m, ACT.Exp).then_inc(em_out, 1)
                if step in ("ecum", "end"):
                    act.wait_ge(tok_done, i - min(GATE_STEPS))
                    dst = end if step == "end" else g[step]
                    act.activation(dst[:, :, :], tok, ACT.Exp).then_inc(tok_out, 1)
                act.wait_ge(tile_done, i + 1)
                if i < TX:
                    act.activation(blocks(row["a"][:, :]), acc[i % 2][0:48, :, :], ACT.Copy)
                    act.activation(blocks(row["b"][ML, :]), acc[i % 2][64:80, :, :], ACT.Copy).then_inc(evac_done, 1)
                elif i < TQ:
                    if i == TX:
                        act.wait_ge(pad_zero, 1)
                    if i >= TX + 2:
                        act.wait_ge(conv_done, i - TX - 1)
                    for s, t, view in PARTS:
                        padded = pad[:, i % 2, 1 + 2 * s:1 + 2 * s + T]
                        act.activation(part(padded, t), view(acc[i % 2]), ACT.Copy).then_inc(pad_ready, 1)
                    act.wait_ge(pad_ready, 3 * (i - TX) + 3)
                    act.sem_inc(evac_done, 1)
                    if i > TX:
                        silu(i - 1)
                else:
                    if i == TQ:
                        silu(i - 1)
                    out_free(i)
                    s, _ = out_slot(i)
                    fn = ACT.Sigmoid if i >= TG else ACT.Copy
                    sc = DK ** -0.5 if i < TK else 1.0
                    act.activation(blocks(ob[:, s, :]), acc[i % 2], fn, scale=sc).then_inc(ob_ready, 1)
                    act.wait_ge(ob_ready, i - TX + 1)
                    act.sem_inc(evac_done, 1)
                for n in units[i][1:]:
                    ada_high(n)

        @block.vector
        def _(dve):
            link = Chain(dve, chain)
            dve.memset(pad[:, :, :], 0.0).then_inc(pad_zero, 1)

            def low(i):
                w = arrived(dve, ("w", i))
                dve.wait_ge(hi_done, i + 1)
                dve.tensor_tensor(wl[:, i % 2, :, :], w, wh[:, i % 2, :, :].bitcast(F32),
                                  ALU.subtract).then_inc(lo_done, 1)

            def conv(i):
                dve.wait_ge(pad_ready, 3 * (i - TX) + 3)
                if i >= TX + 2:
                    dve.wait_ge(ob_ready, i - TX - 1)
                x, y = pad[:, i % 2, :], cv[:, i % 2, 1:PADT - 1]
                n = PADT - 2
                w = [col(k, "conv_w", 3 * (i - TX) + j) for j in range(3)]
                link(dve.tensor_scalar(y, x[:, 1:1 + n], w[1], None, ALU.mult))
                link(dve.scalar_tensor_tensor(out=y, in0=x[:, 0:n], scalar=w[0], in1=y, op0=ALU.mult, op1=ALU.add))
                dve.scalar_tensor_tensor(out=y, in0=x[:, 2:2 + n], scalar=w[2], in1=y, op0=ALU.mult,
                                         op1=ALU.add).then_inc(conv_done, 1)

            def ada_low(n):
                dve.wait_ge(ada_hi, n - 15)
                if n > 16:
                    dve.wait_ge(unit_done, n - 16)
                dve.tensor_tensor(al[:, :, :], arrived(dve, ("ada", n)), ah[:, :, :].bitcast(F32),
                                  ALU.subtract).then_inc(ada_lo, 1)

            rlink = Chain(dve, chain_rows)

            def gate_rows():
                X, E, U, L, SPR, G2 = (row[n][:, :] for n in ("x", "e", "u", "l", "sp", "g2"))
                sgn = const(k, "sign", slice(0, 48))
                rlink(dve.memset(pm[:, :, :], 0.0))
                dve.wait_ge(evac_done, 1)
                rlink(dve.tensor_scalar(X, row["a"][:, :], col(k, "gate_bias", rows=slice(0, 48)), sgn,
                                        ALU.add, ALU.mult))
                dve.scalar_tensor_tensor(out=E, in0=X, scalar=-1.0, in1=X, op0=ALU.mult, op1=ALU.max).then_inc(ex, 1)
                yield
                yield
                dve.wait_ge(u1, 1)
                dve.tensor_scalar(U, E, 1.0, None, ALU.add).then_inc(ln_in, 1)
                yield
                yield
                dve.wait_ge(ln_out, 1)
                rlink(dve.scalar_tensor_tensor(out=SPR, in0=U, scalar=-1.0, in1=E, op0=ALU.add, op1=ALU.subtract))
                rlink(dve.reciprocal(U, U))
                yield
                rlink(dve.tensor_tensor(SPR, SPR, U, ALU.mult))
                rlink(dve.tensor_tensor(SPR, L, SPR, ALU.subtract))
                rlink(dve.scalar_tensor_tensor(out=SPR, in0=X, scalar=0.0, in1=SPR, op0=ALU.max, op1=ALU.add))
                yield
                dve.wait_ge(a_exp, 1)
                rlink(dve.tensor_scalar(G2[0:32, :], SPR[0:32, :], ac[0:32, :], -1.0, ALU.mult, ALU.mult))
                rlink(dve.tensor_scalar(G2[ML, :], SPR[ML, :], -1.0, None, ALU.mult))
                rlink(dve.tensor_scalar(SPR[ML, :], row["b"][ML, :], col(k, "i_bias", rows=ML), None, ALU.add))
                yield
                ig, lf = SPR[ML, :], G2[ML, :]
                MF, MB = row["mf"][ML, :], row["mb"][ML, :]
                m0 = col(k, "m0", rows=ML)
                for dst, st in ((MF, 1), (MB, -1)):
                    for t0, t1, init in ((0, CTX, 0.0), (CTX, T, m0)):
                        rlink(dve.tensor_tensor_scan(dst[:, t0:t1][:, ::st], lf[:, t0:t1][:, ::st],
                                                     ig[:, t0:t1][:, ::st], init, ALU.add, ALU.max))
                    yield
                fw, bw = const(k, "fwd", ML), const(k, "bwd", ML)
                rlink(dve.tensor_copy(pm[ML, 0, 1:2], m0))
                rlink(dve.tensor_copy(pm[ML, 1, NC - 1:NC], m0))
                rlink(dve.tensor_copy(pm[ML, 0, 2:NC], MF[:, 2 * C - 1:T - C:C]))
                rlink(dve.tensor_copy(pm[ML, 1, 1:NC - 1], MB[:, 2 * C:T:C]))

                def by_direction(dst, f, b):
                    rlink(dve.tensor_scalar(dst, f, fw, None, ALU.mult))
                    rlink(dve.scalar_tensor_tensor(out=dst, in0=b, scalar=bw, in1=dst, op0=ALU.mult, op1=ALU.add))

                MM = row["mm"][ML, :]
                by_direction(MM, MF, MB)
                yield
                by_direction(pp[ML, :], pm[ML, 0, :], pm[ML, 1, :])
                by_direction(mn[ML, :], MF[:, C - 1:T:C], MB[:, 0:T:C])
                cs = [16, NC, C]
                rlink(dve.tensor_tensor(row["d"][ML, :].rearrange("p (c t) -> p c t", c=NC),
                                        spread(pp[ML, :].unsqueeze(2), cs),
                                        MM.rearrange("p (c t) -> p c t", c=NC), ALU.subtract))
                yield
                rlink(dve.tensor_tensor(row["w"][ML, :].rearrange("p (c t) -> p c t", c=NC),
                                        ig.rearrange("p (c t) -> p c t", c=NC),
                                        spread(mn[ML, :].unsqueeze(2), cs), ALU.subtract))
                dve.tensor_scalar(g["negm"][ML, :], MM, -1.0, None, ALU.mult).then_inc(rows_done, 1)

            rows_work = gate_rows()
            low(0)
            for i in range(NT):
                if i + 1 < NT:
                    low(i + 1)
                for n in units[i][:1]:
                    ada_low(n)
                if TX <= i < TQ:
                    conv(i)
                for n in units[i][1:]:
                    ada_low(n)
                if i >= TX:
                    next(rows_work, None)
                step = GATE_STEPS.get(i - 1)
                if step in ("dt_ig", "dec", "dbc"):
                    dve.wait_ge(tok_done, i - min(GATE_STEPS))
                    dve.tensor_copy(g[step][:, :, :], tok).then_inc(tok_out, 1)
                if step == "dbc":
                    dve.wait_ge(tok_out, len(GATE_STEPS) - 1)
                    dve.tensor_copy(g["eend"][:, :, 32:48], end[:, :, 32:48]).then_inc(ends_done, 1)
                    dve.tensor_tensor(g["eend"][:, :, 0:32], end[:, :, 0:32], g["dt_ig"][:, :, 0:32],
                                      ALU.mult).then_inc(ends_done, 1)
            dve.wait_ge(ends_done, 2)
            dve.wait_ge(tok_out, len(GATE_STEPS))
            dve.wait_ge(em_out, 1)
            dve.wait_ge(mod_done, 8)
            dve.tensor_tensor(k["mod"][:, 16:48, :], pmod[:, 16:48, :],
                              spread(col(k, "b_ada", 16, 32).unsqueeze(2), [P, 32, 2]), ALU.add).then_inc(chain, 1)
            dve.wait_ge(chain, link.n + 1)

        @block.gpsimd
        def _(pool):
            for n, i in enumerate(outs):
                s, _ = out_slot(i)
                pool.wait_ge(ob_ready, n + 1)
                if i < TQ:
                    dst = scr["xbc"][i - TX]
                elif i < TG:
                    dst = scr["qk"][i - TQ]
                else:
                    dst = scr["gate"][i - TG]
                pool.dma_start(dst, ob[:, s, :]).then_inc(stored[s], 16)
            for s in range(ORING):
                pool.wait_ge(stored[s], 16 * len([i for i in outs if out_slot(i)[0] == s]))


def proj_tok(nc, a, uh, ul, scr):
    with ExitStack() as ctx:
        NB, W, OR = 6, 512, 4
        raw = ctx.enter_context(nc.sbuf_tensor("rawn", [P, 2, KD, W], F32))
        wh = ctx.enter_context(nc.sbuf_tensor("whn", [P, 2, KD, W], F32R))
        wl = ctx.enter_context(nc.sbuf_tensor("wln", [P, 2, KD, W], F32R))
        ob = ctx.enter_context(nc.sbuf_tensor("obn", [P, OR, W], F32))
        NP = 8
        acc = ctx.enter_context(nc.psum_tensor("accn", [P, NP, W], F32))
        hi_done, lo_done, tok_done, ob_ready = open_sems(
            nc, ctx, "n_hi_done", "n_lo_done", "tok_done", "n_ob_ready")
        Q = 4
        H = KD // Q
        raw_in = open_sems(nc, ctx, *[f"n_raw_in{i}" for i in range(2 * Q)])
        stored = open_sems(nc, ctx, *[f"n_stored{i}" for i in range(OR)])
        block = ctx.enter_context(nc.Block())

        @block.sync
        def _(sp):
            for b in range(NB):
                if b >= 2:
                    sp.wait_ge(hi_done, Q * (b - 1))
                    sp.wait_ge(lo_done, Q * (b - 1))
                for j in range(Q):
                    sp.dma_start(raw[:, b % 2, j * H:(j + 1) * H, :],
                                 a["w_in_tok"][b][:, j * H:(j + 1) * H, :]).then_inc(raw_in[Q * (b % 2) + j], 16)

        @block.tensor
        def _(pe):
            for b in range(NB):
                for c in range(NC):
                    n = b * NC + c
                    if n >= NP:
                        pe.wait_ge(ob_ready, n - NP + 1)
                    for kt in range(KD):
                        if c == 0 and kt % H == 0:
                            pe.wait_ge(hi_done, Q * b + kt // H + 1)
                            pe.wait_ge(lo_done, Q * b + kt // H + 1)
                        for q, (x, w) in enumerate(((uh, wh), (uh, wl), (ul, wh))):
                            m = pe.matmul(acc[:, n % NP, :], x[:, kt, c * C:(c + 1) * C], w[:, b % 2, kt, :],
                                          start=(kt == 0 and q == 0), stop=(kt == KD - 1 and q == 2))
                    m.then_inc(tok_done, 1)

        @block.scalar
        def _(act):
            def high(b):
                if b >= 2:
                    act.wait_ge(tok_done, NC * (b - 1))
                for j in range(Q):
                    act.wait_ge(raw_in[Q * (b % 2) + j], 16 * (b // 2 + 1))
                    act.activation(wh[:, b % 2, j * H:(j + 1) * H, :], raw[:, b % 2, j * H:(j + 1) * H, :],
                                   ACT.Copy).then_inc(hi_done, 1)

            high(0)
            for b in range(NB):
                if b + 1 < NB:
                    high(b + 1)
                fn = (ACT.Silu, ACT.Copy, ACT.Sigmoid)[b // 2]
                for c in range(NC):
                    n = b * NC + c
                    act.wait_ge(tok_done, n + 1)
                    if n >= OR:
                        act.wait_ge(stored[n % OR], 16 * (n // OR))
                    act.activation(ob[:, n % OR, :], acc[:, n % NP, :], fn).then_inc(ob_ready, 1)

        @block.vector
        def _(dve):
            for b in range(NB):
                for j in range(Q):
                    dve.wait_ge(hi_done, Q * b + j + 1)
                    dve.tensor_tensor(wl[:, b % 2, j * H:(j + 1) * H, :], raw[:, b % 2, j * H:(j + 1) * H, :],
                                      wh[:, b % 2, j * H:(j + 1) * H, :].bitcast(F32),
                                      ALU.subtract).then_inc(lo_done, 1)

        @block.gpsimd
        def _(pool):
            for n in range(NB * NC):
                b, c = n // NC, n % NC
                pool.wait_ge(ob_ready, n + 1)
                dst = scr["zvo"][b // 2][c][:, (b % 2) * W:(b % 2 + 1) * W]
                pool.dma_start(dst, ob[:, n % OR, :]).then_inc(stored[n % OR], 16)
            for s in range(OR):
                pool.wait_ge(stored[s], 16 * len(range(s, NB * NC, OR)))


def head_decay(g, d, c, gp):
    r = slice(64 * gp, 64 * gp + 64)
    v = g["dbc"][r, c, d * SH:(d + 1) * SH].rearrange("p (a b h) -> p a b h", a=2, b=2)[:, :, gp, :]
    return spread(v.unsqueeze(3), [64, 2, HG, SP])


def state_view(s, gp):
    return s[64 * gp:64 * gp + 64, :].rearrange("p (a h x) -> p a h x", a=2, h=HG)


def ssd(nc, a, k, g, scr, o):
    with ExitStack() as ctx:
        x = ctx.enter_context(nc.sbuf_tensor("x_tok", [P, NC, D], F32))
        b = ctx.enter_context(nc.sbuf_tensor("b_tok", [P, NC, SG * SN], F32))
        snap = ctx.enter_context(nc.sbuf_tensor("snap", [P, NC - 1, 512], F32))
        ssd_backward(nc, a, k, g, scr, o, x, b, snap)
        ssd_forward(nc, a, k, g, scr, x, b, snap)


def ssd_backward(nc, a, k, g, scr, o, x, b, snap):
    with ExitStack() as ctx:
        xc = ctx.enter_context(nc.sbuf_tensor("xc", [P, 2, 10, C], F32))
        xw = ctx.enter_context(nc.sbuf_tensor("xw", [P, 2, D], F32))
        fin = ctx.enter_context(nc.sbuf_tensor("fin", [P, 2, 512], F32))
        tr = [ctx.enter_context(nc.psum_tensor(f"tr{i}", [P, 3, 512], F32)) for i in range(2)]
        st = ctx.enter_context(nc.psum_tensor("st", [P, 2, 512], F32))
        tr_done, x_tok, b_tok, xw_ready, st_done, st_used, s0_in, chain = open_sems(
            nc, ctx, "tr_done", "x_tokd", "b_tokd", "xw_ready", "st_done", "st_used", "s0_in", "chain_sb")
        xc_in = open_sems(nc, ctx, "xc_in0", "xc_in1")
        block = ctx.enter_context(nc.Block())
        order = [0] + list(range(NC - 1, 0, -1))
        jobs = [(0, 0), (0, 1)] + [(c, 1) for c in range(NC - 1, 1, -1)]
        at = {c: n for n, c in enumerate(order)}

        @block.sync
        def _(sp):
            sp.dma_start(snap[:, NC - 2, :], a["s_ssd"][:, 1, :]).then_inc(s0_in, 16)
            for n, c in enumerate(order):
                if n >= 2:
                    sp.wait_ge(tr_done, n - 1)
                sp.dma_start(xc[:, n % 2, :, :],
                             scr["xbc"][0:10, :, c * C:(c + 1) * C].rearrange("i p t -> p i t")
                             ).then_inc(xc_in[n % 2], 16)
            sp.wait_ge(st_used, 2)
            sp.dma_start(o["ssd"], fin[:, :, :]).then_inc(o["ssd_out"], 16)
            sp.wait_ge(o["ssd_out"], 16)

        @block.tensor
        def _(pe):
            def turn(n):
                pe.wait_ge(xc_in[n % 2], 16 * (n // 2 + 1))
                if n >= 2:
                    pe.wait_ge(x_tok, n - 1)
                    pe.wait_ge(b_tok, n - 1)
                for i in range(10):
                    m = pe.transpose(tr[n % 2][:, i // 4, (i % 4) * P:(i % 4 + 1) * P], xc[:, n % 2, i, :],
                                     const(k, "ident"))
                m.then_inc(tr_done, 1)

            def state(n):
                c, d = jobs[n]
                pe.wait_ge(xw_ready, n + 1)
                pe.wait_ge(b_tok, at[c] + 1)
                if n >= 2:
                    pe.wait_ge(st_used, n - 1)
                for q in range(SG):
                    m = pe.matmul(st[64 * (q % 2):64 * (q % 2) + 64, n % 2, 256 * (q // 2):256 * (q // 2) + 256],
                                  b[:, c, q * SN:(q + 1) * SN], xw[:, n % 2, q * 256:(q + 1) * 256],
                                  start=True, stop=True, skip_group_check=True)
                m.then_inc(st_done, 1)

            turn(0)
            turn(1)
            state(0)
            state(1)
            for n in range(2, NC):
                turn(n)
                state(n)

        @block.scalar
        def _(act):
            for n, c in enumerate(order):
                act.wait_ge(tr_done, n + 1)
                act.activation(x[:, c, :].rearrange("p (b n) -> p b n", b=2), tr[n % 2][:, 0:2, :],
                               ACT.Copy).then_inc(x_tok, 1)

        @block.gpsimd
        def _(pool):
            for n, (c, d) in enumerate(jobs):
                pool.wait_ge(x_tok, at[c] + 1)
                if n >= 2:
                    pool.wait_ge(st_done, n - 1)
                w = spread(g["eend"][:, c, d * SH:(d + 1) * SH].unsqueeze(2), [P, SH, SP])
                pool.tensor_tensor(xw[:, n % 2, :].rearrange("p (h x) -> p h x", h=SH),
                                   x[:, c, :].rearrange("p (h x) -> p h x", h=SH), w,
                                   ALU.mult).then_inc(xw_ready, 1)

        @block.vector
        def _(dve):
            link = Chain(dve, chain)
            dve.wait_ge(s0_in, 16)

            def b_copy(n):
                dve.wait_ge(tr_done, n + 1)
                dve.tensor_copy(b[:, order[n], :], tr[n % 2][:, 2, 0:256]).then_inc(b_tok, 1)

            b_copy(0)
            b_copy(1)
            for n, (c, d) in enumerate(jobs):
                dve.wait_ge(st_done, n + 1)
                if c == 0:
                    dve.tensor_copy(fin[:, d, :], st[:, n % 2, :]).then_inc(st_used, 1)
                else:
                    for gp in range(2):
                        link(dve.tensor_tensor(state_view(snap[:, c - 2, :], gp), state_view(snap[:, c - 1, :], gp),
                                               head_decay(g, 1, c, gp), ALU.mult))
                    dve.tensor_tensor(snap[:, c - 2, :], snap[:, c - 2, :], st[:, n % 2, :],
                                      ALU.add).then_inc(st_used, 1)
                    dve.wait_ge(st_used, n + 1)
                if 1 <= n < NC - 1:
                    b_copy(n + 1)


def ssd_forward(nc, a, k, g, scr, x, b, snap):
    with ExitStack() as ctx:
        U = NC * SG
        bc = ctx.enter_context(nc.sbuf_tensor("bc", [P, 2, 4, C], F32))
        cm = ctx.enter_context(nc.sbuf_tensor("cm", [P, 2, 2, 2, C], F32))
        z = ctx.enter_context(nc.sbuf_tensor("z", [P, 2, D], F32))
        rmf = ctx.enter_context(nc.sbuf_tensor("rmf", [P, 2, 2, HG, C], F32R))
        rmb = ctx.enter_context(nc.sbuf_tensor("rmb", [P, 2, HG, C], F32))
        dh = ctx.enter_context(nc.sbuf_tensor("dta_hi", [P, NC, SH], F32R))
        dl = ctx.enter_context(nc.sbuf_tensor("dta_lo", [P, NC, SH], F32))
        after = ctx.enter_context(nc.sbuf_tensor("after_s", [P, P], F32R))
        s2 = ctx.enter_context(nc.sbuf_tensor("s2", [P, 2, SG, C], F32))
        xdt = ctx.enter_context(nc.sbuf_tensor("xdt", [P, 2, 2, D], F32))
        e = ctx.enter_context(nc.sbuf_tensor("e", [P, 2, HG, C], F32))
        wm = ctx.enter_context(nc.sbuf_tensor("wm", [P, 2, 2, HG, C], F32))
        dful = ctx.enter_context(nc.sbuf_tensor("dful", [P, D], F32))
        xd = ctx.enter_context(nc.sbuf_tensor("xd", [P, 2, 512], F32))
        xw = ctx.enter_context(nc.sbuf_tensor("xwf", [P, D], F32))
        t1 = ctx.enter_context(nc.sbuf_tensor("t1", [P, 2, 512], F32))
        t2 = ctx.enter_context(nc.sbuf_tensor("t2", [P, 512], F32))
        yz = ctx.enter_context(nc.sbuf_tensor("yz", [P, 2, D], F32))
        sqb = ctx.enter_context(nc.sbuf_tensor("sqb", [P, D], F32))
        ss = ctx.enter_context(nc.sbuf_tensor("ss_y", [P, NC], F32))
        rs = ctx.enter_context(nc.sbuf_tensor("rs_y", [P, NC], F32))
        sf = ctx.enter_context(nc.sbuf_tensor("sf", [P, 2, 512], F32))
        yo = ctx.enter_context(nc.sbuf_tensor("yo", [P, 2, KD, C], F32))
        arg = ctx.enter_context(nc.psum_tensor("arg", [P, 2, HG, C], F32))
        sc = ctx.enter_context(nc.psum_tensor("sc", [P, SG, C], F32))
        misc = ctx.enter_context(nc.psum_tensor("misc", [P, 512], F32))
        fb = ctx.enter_context(nc.psum_tensor("fb", [P, 2, 512], F32))
        yd = ctx.enter_context(nc.psum_tensor("yd", [P, 2, 512], F32))
        (rmf_ready, rmb_ready, s2_ready, xdt_ready, arg_done, exp_done, sc_done, wm_done, fb_done, fb_used, y_done, y_used, xd_ready,
         xw_ready, yz_done, rs_done, yn_done, misc_done, misc_used, s0_in, d_in,
         chain, act_c, split_hi, split_lo, after_ready) = open_sems(
            nc, ctx, *["f_" + n for n in (
                "rmf_ready", "rmb_ready", "s2_ready", "xdt_ready", "arg_done", "exp_done", "sc_done", "wm_done", "fb_done", "fb_used",
                "y_done", "y_used", "xd_ready", "xw_ready", "yz_done", "rs_done",
                "yn_done", "misc_done", "misc_used", "s0_in", "d_in", "chain", "act", "split_hi", "split_lo",
                "after_ready")])
        bc_in = open_sems(nc, ctx, "bc_in0", "bc_in1")
        cm_ready, = open_sems(nc, ctx, "cm_ready")
        z_in = open_sems(nc, ctx, "z_in0", "z_in1")
        yo_out = open_sems(nc, ctx, "yo_out0", "yo_out1")
        block = ctx.enter_context(nc.Block())

        uses = []
        for u in range(U + 6):
            c, r = u // SG, u % SG
            if r < 2 and 2 <= c <= NC + 1:
                uses.append((f"tr{r}", c - 2))
            if r == 2 and 1 <= c <= NC - 2:
                uses.append(("st", c))
        misc_at = {name: n for n, name in enumerate(uses)}

        def store(sp, c):
            sp.wait_ge(misc_used, misc_at["tr1", c] + 1)
            sp.dma_start(scr["yn"][:, :, c * C:(c + 1) * C], yo[:, c % 2, :, :]).then_inc(yo_out[c % 2], 16)

        @block.sync
        def _(sp):
            sp.dma_start(sf[:, 1, :], a["s_ssd"][:, 0, :]).then_inc(s0_in, 16)
            sp.dma_start(dful[:, :], a["ssd_d"]).then_inc(d_in, 16)
            for c in range(NC):
                if c >= 2:
                    sp.wait_ge(sc_done, c - 1)
                    sp.wait_ge(cm_ready, 2 * (c - 1))
                sp.dma_start(bc[:, c % 2, :, :],
                             scr["xbc"][8:12, :, c * C:(c + 1) * C].rearrange("i p t -> p i t")
                             ).then_inc(bc_in[c % 2], 16)
                if c >= 2:
                    sp.wait_ge(yz_done, 2 * (c - 1))
                sp.dma_start(z[:, c % 2, :], scr["zvo"][0][c]).then_inc(z_in[c % 2], 16)
                if c >= 3:
                    store(sp, c - 3)
            for c in range(NC - 3, NC):
                store(sp, c)
            for s in range(2):
                sp.wait_ge(yo_out[s], 16 * len(range(s, NC, 2)))

        @block.gpsimd
        def _(pool):
            def dt_x(c, d):
                if c >= 2:
                    pool.wait_ge(y_done, SG * (c - 1))
                pool.tensor_tensor(xdt[:, c % 2, d, :].rearrange("p (h x) -> p h x", h=SH),
                                   x[:, c, :].rearrange("p (h x) -> p h x", h=SH),
                                   spread(g["dt_ig"][:, c, d * SH:(d + 1) * SH].unsqueeze(2), [P, SH, SP]),
                                   ALU.mult).then_inc(xdt_ready, 1)

            for u in range(U):
                c, q = u // SG, u % SG
                if u >= 2:
                    pool.wait_ge(arg_done, u - 1)
                hs = [P, HG, C]
                if u == 0:
                    pool.wait_ge(split_lo, 1)
                for part_, f in enumerate((dh[:, c, q * HG:(q + 1) * HG].bitcast(F32), dl[:, c, q * HG:(q + 1) * HG])):
                    m = pool.tensor_tensor(rmf[:, u % 2, part_, :, :], spread(f.unsqueeze(2), hs),
                                           spread(const(k, "le").unsqueeze(1), hs), ALU.mult)
                m.then_inc(rmf_ready, 1)
                if u == 0:
                    dt_x(0, 0)
                    dt_x(0, 1)
                if u % 2 == 1:
                    v = u // 2
                    if v == 0:
                        pool.wait_ge(d_in, 16)
                    if v >= 2:
                        pool.wait_ge(yz_done, v - 1)
                    hf = slice((v % 2) * 512, (v % 2) * 512 + 512)
                    pool.tensor_tensor(xd[:, v % 2, :], x[:, c, hf], dful[:, hf], ALU.mult).then_inc(xd_ready, 1)
                if q == 0 and 1 <= c <= NC - 2:
                    if c >= 2:
                        pool.wait_ge(misc_done, misc_at["st", c - 1] + 1)
                    w = spread(g["eend"][:, c, 0:SH].unsqueeze(2), [P, SH, SP])
                    pool.tensor_tensor(xw[:, :].rearrange("p (h x) -> p h x", h=SH),
                                       x[:, c, :].rearrange("p (h x) -> p h x", h=SH), w,
                                       ALU.mult).then_inc(xw_ready, 1)
                if q in (1, 2) and c + 1 < NC:
                    dt_x(c + 1, q - 1)

        @block.tensor
        def _(pe):
            def shared(name):
                n = misc_at[name]
                if n:
                    pe.wait_ge(misc_used, n)

            def scores(c):
                pe.wait_ge(bc_in[c % 2], 16 * (c // 2 + 1))
                pe.wait_ge(cm_ready, 2 * (c + 1))
                if c:
                    pe.wait_ge(s2_ready, c)
                for q in range(SG):
                    m = pe.matmul(sc[:, q, :], bc[:, c % 2, q // 2, :], cm[:, c % 2, q % 2, q // 2, :],
                                  start=True, stop=True)
                m.then_inc(sc_done, 1)

            scores(0)
            pe.wait_ge(after_ready, 1)
            for u in range(U + 6):
                c, r = u // SG, u % SG
                if u < U:
                    if r % 2 == 0:
                        v = u // 2
                        if v >= 3:
                            pe.wait_ge(fb_used, v - 2)
                        if c == 0:
                            pe.sem_inc(fb_done, 1)
                        else:
                            if c == 1:
                                pe.wait_ge(s0_in, 16)
                            else:
                                pe.wait_ge(misc_used, misc_at["st", c - 1] + 1)
                            for d in range(2):
                                s = sf[:, c % 2, :] if d == 0 else snap[:, c - 1, :]
                                for gp in range(2):
                                    gh = v % 2
                                    m = pe.matmul(fb[:, d, gp * 256:gp * 256 + 256], cm[:, c % 2, gp, gh, :],
                                                  s[:, gh * 256:gh * 256 + 256], start=True, stop=True,
                                                  skip_group_check=True)
                            m.then_inc(fb_done, 1)
                    pe.wait_ge(rmf_ready, u + 1)
                    pe.wait_ge(rmb_ready, u + 1)
                    if u >= 2:
                        pe.wait_ge(exp_done, u - 1)
                    for part_ in range(2):
                        pe.matmul(arg[:, u % 2, :, :], after[:, :], rmf[:, u % 2, part_, :, :], start=(part_ == 0),
                                  stop=False)
                    m = pe.matmul(arg[:, u % 2, :, :], const(k, "lt"), rmb[:, u % 2, :, :], start=False, stop=True)
                    m.then_inc(arg_done, 1)
                if 1 <= u <= U:
                    w = u - 1
                    cw, q, v = w // SG, w % SG, w // 2
                    pe.wait_ge(wm_done, w + 1)
                    if w % 2 == 0 and v >= 2:
                        pe.wait_ge(y_used, v - 1)
                    pe.wait_ge(xdt_ready, 2 * (cw + 1))
                    for i in range(HG):
                        hd = q * HG + i
                        for d in range(2):
                            m = pe.matmul(yd[:, v % 2, (hd % 8) * SP:(hd % 8 + 1) * SP], wm[:, w % 2, d, i, :],
                                          xdt[:, cw % 2, d, hd * SP:(hd + 1) * SP], start=(d == 0), stop=(d == 1),
                                          skip_group_check=True)
                    m.then_inc(y_done, 1)
                if r == 3 and c + 1 < NC:
                    scores(c + 1)
                if r == 2 and 1 <= c <= NC - 2:
                    pe.wait_ge(xw_ready, c)
                    shared(("st", c))
                    for q in range(SG):
                        m = pe.matmul(misc[64 * (q % 2):64 * (q % 2) + 64, 256 * (q // 2):256 * (q // 2) + 256],
                                      b[:, c, q * SN:(q + 1) * SN], xw[:, q * 256:(q + 1) * 256], start=True,
                                      stop=True, skip_group_check=True)
                    m.then_inc(misc_done, 1)
                for name, j, r0, back in (("tr0", 0, 0, 2), ("tr1", 1, 1, 2)):
                    if r == r0 and back <= c <= NC - 1 + back:
                        cc = c - back
                        pe.wait_ge(yn_done, cc + 1)
                        shared((name, cc))
                        for i in range(4):
                            m = pe.transpose(misc[:, i * P:(i + 1) * P],
                                             yz[:, cc % 2, (4 * j + i) * P:(4 * j + i + 1) * P], const(k, "ident"))
                        m.then_inc(misc_done, 1)

        @block.scalar
        def _(act):
            link = Chain(act, act_c)

            def one_group(c):
                act.wait_ge(bc_in[c % 2], 16 * (c // 2 + 1))
                if c >= 2:
                    act.wait_ge(sc_done, c - 1)
                    act.wait_ge(fb_done, 2 * (c - 1))
                for half in range(2):
                    act.activation(cm[:, c % 2, half, :, :], bc[:, c % 2, 2:4, :], ACT.Copy,
                                   scale=const(k, f"half{half}")).then_inc(cm_ready, 1)

            def backward_decay(u):
                if u >= 2:
                    act.wait_ge(arg_done, u - 1)
                for i in range(HG):
                    j = SH + (u % SG) * HG + i
                    m = act.activation(rmb[:, u % 2, i, :], const(k, "ge"), ACT.Copy,
                                       scale=g["dec"][:, u // SG, j:j + 1])
                m.then_inc(rmb_ready, 1)

            act.activation(dh[:, :, :], g["dec"][:, :, 0:SH], ACT.Copy).then_inc(split_hi, 1)
            act.activation(after[:, :], const(k, "gt"), ACT.Copy).then_inc(after_ready, 1)
            one_group(0)
            backward_decay(0)
            for u in range(U + 6):
                c, r = u // SG, u % SG
                if u + 1 < U:
                    backward_decay(u + 1)
                if u < U:
                    act.wait_ge(arg_done, u + 1)
                    if u >= 2:
                        act.wait_ge(wm_done, u - 1)
                    act.activation(e[:, u % 2, :, :], arg[:, u % 2, :, :], ACT.Exp).then_inc(exp_done, 1)
                if r == 2 and c + 1 < NC:
                    one_group(c + 1)
                if r == 1 and 1 <= c <= NC:
                    cc = c - 1
                    act.wait_ge(yz_done, 2 * cc + 2)
                    link(act.activation(sqb[:, :], yz[:, cc % 2, :], ACT.Square, accum_out=ss[:, cc:cc + 1]))
                    link(act.activation(rs[:, cc:cc + 1], ss[:, cc:cc + 1], ACT.Ln, bias=const(k, "eps"),
                                        scale=1.0 / D))
                    act.activation(rs[:, cc:cc + 1], rs[:, cc:cc + 1], ACT.Exp, scale=-0.5).then_inc(rs_done, 1)
                if r < 2 and 2 <= c <= NC + 1:
                    cc = c - 2
                    act.wait_ge(misc_done, misc_at[f"tr{r}", cc] + 1)
                    if cc >= 2:
                        act.wait_ge(yo_out[cc % 2], 16 * (cc // 2))
                    for i in range(4 * r, 4 * r + 4):
                        m = act.activation(yo[:, cc % 2, i, :], misc[:, (i % 4) * P:(i % 4 + 1) * P], ACT.Copy,
                                           scale=col(k, "ssd_norm", i))
                    m.then_inc(misc_used, 1)

        @block.vector
        def _(dve):
            link = Chain(dve, chain)
            dve.wait_ge(split_hi, 1)
            dve.tensor_tensor(dl[:, :, :], g["dec"][:, :, 0:SH], dh[:, :, :].bitcast(F32),
                              ALU.subtract).then_inc(split_lo, 1)

            def masked_scores(c):
                dve.wait_ge(sc_done, c + 1)
                if c:
                    dve.wait_ge(wm_done, SG * c)
                for d, mask in enumerate(("le", "ge")):
                    m = dve.tensor_tensor(s2[:, d, :, :], sc[:, :, :],
                                          spread(const(k, mask).unsqueeze(1), [P, SG, C]), ALU.mult)
                m.then_inc(s2_ready, 1)

            def decay_state(c):
                if c == 1:
                    dve.wait_ge(s0_in, 16)
                else:
                    dve.wait_ge(fb_done, 2 * c)
                    dve.wait_ge(misc_used, misc_at["st", c - 1] + 1)
                for gp in range(2):
                    link(dve.tensor_tensor(state_view(sf[:, (c + 1) % 2, :], gp),
                                           state_view(sf[:, c % 2, :], gp), head_decay(g, 0, c, gp), ALU.mult))

            def add_state(c):
                dve.wait_ge(misc_done, misc_at["st", c] + 1)
                dve.tensor_tensor(sf[:, (c + 1) % 2, :], sf[:, (c + 1) % 2, :], misc[:, :],
                                  ALU.add).then_inc(misc_used, 1)

            masked_scores(0)
            for u in range(U + 6):
                c, r = u // SG, u % SG
                if r == 3 and 1 <= c <= NC - 2:
                    add_state(c)
                if u < U:
                    if u % 2 == 0 and c >= 1:
                        v = u // 2
                        dve.wait_ge(fb_done, v + 1)
                        if v >= 2:
                            dve.wait_ge(yz_done, v - 1)
                        hs = [P, 8, SP]
                        for d, dst in ((0, t1[:, v % 2, :]), (1, t2[:, :])):
                            w = spread(g["ecum"][:, c, d * SH + 8 * (v % 2):d * SH + 8 * (v % 2) + 8].unsqueeze(2), hs)
                            ins = dve.tensor_tensor(dst.rearrange("p (h x) -> p h x", h=8),
                                                    fb[:, d, :].rearrange("p (h x) -> p h x", h=8), w, ALU.mult)
                            ins.then_inc(chain, 1)
                            link.n += 1
                        dve.wait_ge(chain, link.n)
                        link(dve.tensor_tensor(t1[:, v % 2, :], t1[:, v % 2, :], t2[:, :], ALU.add))
                        dve.sem_inc(fb_used, 1)
                    dve.wait_ge(exp_done, u + 1)
                    if u >= 2:
                        dve.wait_ge(y_done, u - 1)
                    if r == 0:
                        dve.wait_ge(s2_ready, c + 1)
                    for d in range(2):
                        m = dve.tensor_tensor(wm[:, u % 2, d, :, :], e[:, u % 2, :, :],
                                              spread(s2[:, d, r, :].unsqueeze(1), [P, HG, C]), ALU.mult)
                    m.then_inc(wm_done, 1)
                    if r == 3 and c + 1 < NC:
                        masked_scores(c + 1)
                if u % 2 == 0 and 2 <= u <= U:
                    v = u // 2 - 1
                    cc, half = v // 2, slice((v % 2) * 512, (v % 2) * 512 + 512)
                    dve.wait_ge(y_done, 2 * v + 2)
                    dve.wait_ge(xd_ready, v + 1)
                    if cc == 0:
                        link(dve.tensor_tensor(t1[:, v % 2, :], xd[:, v % 2, :], yd[:, v % 2, :], ALU.add))
                        dve.sem_inc(y_used, 1)
                    else:
                        link(dve.tensor_tensor(t1[:, v % 2, :], t1[:, v % 2, :], yd[:, v % 2, :], ALU.add))
                        dve.sem_inc(y_used, 1)
                        link(dve.tensor_tensor(t1[:, v % 2, :], t1[:, v % 2, :], xd[:, v % 2, :], ALU.add))
                    dve.wait_ge(z_in[cc % 2], 16 * (cc // 2 + 1))
                    if cc >= 2:
                        dve.wait_ge(misc_done, misc_at["tr1", cc - 2] + 1)
                    dve.tensor_tensor(yz[:, cc % 2, half], t1[:, v % 2, :], z[:, cc % 2, half],
                                      ALU.mult).then_inc(yz_done, 1)
                if r == 1 and 1 <= c <= NC - 2:
                    decay_state(c)
                if r == 3 and 1 <= c <= NC:
                    cc = c - 1
                    dve.wait_ge(rs_done, cc + 1)
                    dve.tensor_scalar(yz[:, cc % 2, :], yz[:, cc % 2, :], rs[:, cc:cc + 1], None,
                                      ALU.mult).then_inc(yn_done, 1)


def ml_decay(g, d, c, hp, n, half):
    r = slice(64 * half, 64 * half + 64)
    v = g["dbc"][r, c, 32 + 8 * d:40 + 8 * d].rearrange("p (a b) -> p a b", b=2)[:, hp:hp + n, half]
    return spread(v.unsqueeze(2), [64, n, DV1])


def mlstm(nc, a, k, g, scr, o):
    with ExitStack() as ctx:
        v = ctx.enter_context(nc.sbuf_tensor("v_one", [P, NC, MH, DV1], F32))
        kt = ctx.enter_context(nc.sbuf_tensor("k_tok", [P, NC, MH * DK], F32))
        snap = ctx.enter_context(nc.sbuf_tensor("snap_c", [P, NC - 1, 4, DV1], F32))
        mlstm_backward(nc, a, k, g, scr, o, v, kt, snap)
        mlstm_forward(nc, a, k, g, scr, v, kt, snap)


def mlstm_backward(nc, a, k, g, scr, o, v, kt, snap):
    with ExitStack() as ctx:
        kc = ctx.enter_context(nc.sbuf_tensor("kc", [P, 2, 4, C], F32))
        vw = ctx.enter_context(nc.sbuf_tensor("vw", [P, 2, MH, DV1], F32))
        fin = ctx.enter_context(nc.sbuf_tensor("fin_c", [P, 2, 4, DV1], F32))
        tr = ctx.enter_context(nc.psum_tensor("trk", [P, 2, 512], F32))
        st = ctx.enter_context(nc.psum_tensor("stc", [P, 2, 2, 512], F32))
        tr_done, k_tok, one, vw_ready, st_done, st_used, c0_in, chain = open_sems(
            nc, ctx, *["mb_" + n for n in ("tr_done", "k_tok", "one", "vw_ready", "st_done", "st_used", "c0_in",
                                           "chain")])
        kc_in = open_sems(nc, ctx, "kc_in0", "kc_in1")
        v_in = open_sems(nc, ctx, *[f"v_in{i}" for i in range(NC)])
        block = ctx.enter_context(nc.Block())
        order = [0] + list(range(NC - 1, 0, -1))
        jobs = [(0, 0), (0, 1)] + [(c, 1) for c in range(NC - 1, 1, -1)]
        at = {c: n for n, c in enumerate(order)}

        @block.sync
        def _(sp):
            sp.dma_start(snap[:, NC - 2, :, :], a["s_ml"][:, 1, :, :]).then_inc(c0_in, 16)
            for n, c in enumerate(order):
                if n >= 2:
                    sp.wait_ge(tr_done, n - 1)
                sp.dma_start(kc[:, n % 2, :, :],
                             scr["qk"][4:8, :, c * C:(c + 1) * C].rearrange("i p t -> p i t")
                             ).then_inc(kc_in[n % 2], 16)
                sp.dma_start(v[:, c, :, 0:DV], scr["zvo"][1][c].rearrange("p (h x) -> p h x", h=MH)
                             ).then_inc(v_in[c], 16)
            sp.wait_ge(st_used, 2)
            sp.dma_start(o["ml"], fin[:, :, :, :]).then_inc(o["ml_out"], 16)
            sp.wait_ge(o["ml_out"], 16)

        @block.tensor
        def _(pe):
            def turn(n):
                pe.wait_ge(kc_in[n % 2], 16 * (n // 2 + 1))
                if n >= 2:
                    pe.wait_ge(k_tok, n - 1)
                for i in range(4):
                    m = pe.transpose(tr[:, n % 2, i * P:(i + 1) * P], kc[:, n % 2, i, :], const(k, "ident"))
                m.then_inc(tr_done, 1)

            def state(n):
                c, d = jobs[n]
                pe.wait_ge(vw_ready, n + 1)
                pe.wait_ge(k_tok, at[c] + 1)
                if n >= 2:
                    pe.wait_ge(st_used, n - 1)
                for h in range(MH):
                    hp, r = h // 2, slice(64 * (h % 2), 64 * (h % 2) + 64)
                    m = pe.matmul(st[r, n % 2, hp // 2, (hp % 2) * DV1:(hp % 2 + 1) * DV1],
                                  kt[:, c, h * DK:(h + 1) * DK], vw[:, n % 2, h, :], start=True, stop=True,
                                  skip_group_check=True)
                m.then_inc(st_done, 1)

            turn(0)
            turn(1)
            state(0)
            state(1)
            for n in range(2, NC):
                turn(n)
                state(n)

        @block.scalar
        def _(act):
            for n, c in enumerate(order):
                act.wait_ge(tr_done, n + 1)
                act.activation(kt[:, c, :], tr[:, n % 2, :], ACT.Copy).then_inc(k_tok, 1)

        @block.gpsimd
        def _(pool):
            pool.memset(v[:, :, :, DV:DV1], 1.0).then_inc(one, 1)
            pool.wait_ge(one, 1)
            for n, (c, d) in enumerate(jobs):
                pool.wait_ge(v_in[c], 16)
                if n >= 2:
                    pool.wait_ge(st_done, n - 1)
                w = spread(g["eend"][:, c, 32 + 8 * d:40 + 8 * d].unsqueeze(2), [P, MH, DV1])
                pool.tensor_tensor(vw[:, n % 2, :, :], v[:, c, :, :], w, ALU.mult).then_inc(vw_ready, 1)

        @block.vector
        def _(dve):
            link = Chain(dve, chain)
            dve.wait_ge(c0_in, 16)
            for n, (c, d) in enumerate(jobs):
                dve.wait_ge(st_done, n + 1)
                if c == 0:
                    for j in range(2):
                        link(dve.tensor_copy(fin[:, d, 2 * j:2 * j + 2, :],
                                             st[:, n % 2, j, 0:2 * DV1].rearrange("p (a x) -> p a x", a=2)))
                else:
                    for half in range(2):
                        r = slice(64 * half, 64 * half + 64)
                        link(dve.tensor_tensor(snap[r, c - 2, :, :], snap[r, c - 1, :, :],
                                               ml_decay(g, 1, c, 0, 4, half), ALU.mult))
                    for j in range(2):
                        link(dve.tensor_tensor(snap[:, c - 2, 2 * j:2 * j + 2, :], snap[:, c - 2, 2 * j:2 * j + 2, :],
                                               st[:, n % 2, j, 0:2 * DV1].rearrange("p (a x) -> p a x", a=2),
                                               ALU.add))
                dve.sem_inc(st_used, 1)


def mlstm_forward(nc, a, k, g, scr, v, kt, snap):
    with ExitStack() as ctx:
        U = NC * 4
        qk = ctx.enter_context(nc.sbuf_tensor("qk", [P, 2, 8, C], F32))
        qm = ctx.enter_context(nc.sbuf_tensor("qm", [P, 2, 2, 4, C], F32))
        og = ctx.enter_context(nc.sbuf_tensor("og", [P, 2, D], F32))
        lm = ctx.enter_context(nc.sbuf_tensor("lm", [P, 2, 2, 4, C], F32R))
        fh = ctx.enter_context(nc.sbuf_tensor("f_hi", [P, NC, 16], F32R))
        fl = ctx.enter_context(nc.sbuf_tensor("f_lo", [P, NC, 16], F32))
        after = ctx.enter_context(nc.sbuf_tensor("after", [P, 2, P], F32R))
        e = ctx.enter_context(nc.sbuf_tensor("e_m", [P, 2, 4, C], F32))
        wm = ctx.enter_context(nc.sbuf_tensor("wm_m", [P, 2, 4, C], F32))
        qw = ctx.enter_context(nc.sbuf_tensor("qw", [P, 2, 2, 4, C], F32))
        vw = ctx.enter_context(nc.sbuf_tensor("vwf", [P, MH, DV1], F32))
        hb = ctx.enter_context(nc.sbuf_tensor("hb", [P, 2, 2, MH, DV1], F32))
        hs = ctx.enter_context(nc.sbuf_tensor("hs", [P, 2, D], F32))
        sqb = ctx.enter_context(nc.sbuf_tensor("sqm", [P, D], F32))
        den = ctx.enter_context(nc.sbuf_tensor("den", [P, 2, MH], F32))
        ss = ctx.enter_context(nc.sbuf_tensor("ss_m", [P, 2, MH], F32))
        cf = ctx.enter_context(nc.sbuf_tensor("cf", [P, 2, 4, DV1], F32))
        ho = ctx.enter_context(nc.sbuf_tensor("ho", [P, 2, KD, C], F32))
        selm = ctx.enter_context(nc.sbuf_tensor("selm", [48, 16, P], F32))
        selq = ctx.enter_context(nc.sbuf_tensor("selq", [48, 8, P], F32))
        wir = ctx.enter_context(nc.sbuf_tensor("wir", [48, T], F32))
        negi = ctx.enter_context(nc.sbuf_tensor("negi", [P, P], BF16))
        mk = ctx.enter_context(nc.sbuf_tensor("mk", [P, 2, 4, C], BF16))
        arg = ctx.enter_context(nc.psum_tensor("arg_m", [P, 2, 4, C], F32))
        sc = ctx.enter_context(nc.psum_tensor("sc_m", [P, 2, 4, C], F32))
        qb = ctx.enter_context(nc.psum_tensor("qb", [P, 4, C], F32))
        misc = ctx.enter_context(nc.psum_tensor("misc_m", [P, 512], F32))
        num = ctx.enter_context(nc.psum_tensor("num", [P, 2, 512], F32))
        (lm_ready, arg_done, exp_done, sc_done, wm_done, qb_done, qw_done, num_done, h_copied, vw_ready,
         hm_done, ss_done, rs_done, hn_done, misc_done, misc_used, c0_in, sel_in, wi_done, wi_row, mk_ready,
         chain, act_c, split_hi, split_lo, after_ready) = open_sems(
            nc, ctx, *["m_" + n for n in (
                "lm_ready", "arg_done", "exp_done", "sc_done", "wm_done", "qb_done", "qw_done", "num_done",
                "h_copied", "vw_ready", "hm_done", "ss_done", "rs_done", "hn_done", "misc_done",
                "misc_used", "c0_in", "sel_in", "wi_done", "wi_row", "mk_ready", "chain", "act", "split_hi", "split_lo",
                "after_ready")])
        qk_in = open_sems(nc, ctx, "qk_in0", "qk_in1")
        qm_ready, = open_sems(nc, ctx, "qm_ready")
        og_in = open_sems(nc, ctx, "og_in0", "og_in1")
        ho_out = open_sems(nc, ctx, "ho_out0", "ho_out1")
        block = ctx.enter_context(nc.Block())
        ML = slice(32, 48)

        uses = []
        for w in range(U + 7):
            c, r = w // 4, w % 4
            if r == 0 and 2 <= c <= NC - 1:
                uses.append(("st1", c - 1))
            if r in (1, 2) and 2 <= c <= NC + 1:
                uses.append((f"tr{r - 1}", c - 2))
            if r == 3 and 1 <= c <= NC - 2:
                uses.append(("st0", c))
        misc_at = {name: n for n, name in enumerate(uses)}

        def store(sp, c):
            sp.wait_ge(misc_used, misc_at["tr1", c] + 1)
            sp.dma_start(scr["hm"][:, :, c * C:(c + 1) * C], ho[:, c % 2, :, :]).then_inc(ho_out[c % 2], 16)

        @block.sync
        def _(sp):
            sp.dma_start(selm[:, :, :], a["selm"]).then_inc(sel_in, 16)
            sp.dma_start(selq[:, :, :], a["selq"]).then_inc(sel_in, 16)
            sp.dma_start(cf[:, 1, :, :], a["s_ml"][:, 0, :, :]).then_inc(c0_in, 16)
            for c in range(NC):
                if c >= 2:
                    sp.wait_ge(sc_done, 2 * (c - 1))
                    sp.wait_ge(qm_ready, 2 * (c - 1))
                sp.dma_start(qk[:, c % 2, :, :],
                             scr["qk"][:, :, c * C:(c + 1) * C].rearrange("i p t -> p i t")
                             ).then_inc(qk_in[c % 2], 16)
                if c >= 2:
                    sp.wait_ge(hn_done, c - 1)
                sp.dma_start(og[:, c % 2, :], scr["zvo"][2][c]).then_inc(og_in[c % 2], 16)
                if c >= 3:
                    store(sp, c - 3)
            for c in range(NC - 3, NC):
                store(sp, c)
            for s in range(2):
                sp.wait_ge(ho_out[s], 16 * len(range(s, NC, 2)))

        @block.gpsimd
        def _(pool):
            for w in range(U + 7):
                c, r = w // 4, w % 4
                if w < U:
                    hg, d = r // 2, r % 2
                    if w >= 2:
                        pool.wait_ge(arg_done, w - 1)
                    if w == 0:
                        pool.wait_ge(split_lo, 1)
                    for q, f in enumerate((fh, fl)):
                        f = f[:, c, 8 * d + 4 * hg:8 * d + 4 * hg + 4]
                        f = f.bitcast(F32) if q == 0 else f
                        m = pool.tensor_tensor(lm[:, w % 2, q, :, :], spread(f.unsqueeze(2), [P, 4, C]),
                                               spread(const(k, "le" if d == 0 else "ge").unsqueeze(1), [P, 4, C]),
                                               ALU.mult)
                    m.then_inc(lm_ready, 1)
                if r == 1 and 1 <= c <= NC - 2:
                    if c >= 2:
                        pool.wait_ge(misc_done, misc_at["st1", c - 1] + 1)
                    pool.tensor_tensor(vw[:, :, :], v[:, c, :, :],
                                       spread(g["eend"][:, c, 32:40].unsqueeze(2), [P, MH, DV1]),
                                       ALU.mult).then_inc(vw_ready, 1)

        @block.tensor
        def _(pe):
            for n, c0 in enumerate(range(0, NC, 3)):
                if n:
                    pe.wait_ge(wi_row, n)
                for c in range(c0, c0 + 3):
                    m = pe.transpose(misc[0:48, (c - c0) * C:(c - c0 + 1) * C], g["ecum"][:, c, :],
                                     const(k, "ident"))
                m.then_inc(wi_done, 1)
            pe.wait_ge(wi_row, NC // 3)

            def shared(name):
                n = misc_at[name]
                if n:
                    pe.wait_ge(misc_used, n)

            pe.wait_ge(mk_ready, 3)
            pe.wait_ge(after_ready, 2)
            pe.wait_ge(sel_in, 32)
            for w in range(U + 7):
                c, r = w // 4, w % 4
                if w < U:
                    hg, d, s = r // 2, r % 2, c % 2
                    if d == 0:
                        x = w // 2
                        if r == 0:
                            pe.wait_ge(qk_in[s], 16 * (c // 2 + 1))
                            pe.wait_ge(qm_ready, 2 * (c + 1))
                        if x >= 2:
                            pe.wait_ge(wm_done, 2 * (x - 1))
                        for i in range(4):
                            h = 4 * hg + i
                            m = pe.matmul(sc[:, x % 2, i, :], qk[:, s, 4 + h // 2, :], qm[:, s, h % 2, h // 2, :],
                                          start=True, stop=True)
                        m.then_inc(sc_done, 1)
                    if r < 2 and c >= 1:
                        n = 2 * (c - 1) + r
                        if n:
                            pe.wait_ge(qw_done, n + 2)
                        for hp in range(4):
                            m = pe.matmul(qb[:, hp, :], selq[ML, 4 * r + hp, :], wir[ML, c * C:(c + 1) * C],
                                          start=True, stop=True, skip_group_check=True)
                        m.then_inc(qb_done, 1)
                    pe.wait_ge(lm_ready, w + 1)
                    if w >= 2:
                        pe.wait_ge(exp_done, w - 1)
                    for q in range(2):
                        pe.matmul(arg[:, w % 2, :, :], after[:, d, :], lm[:, w % 2, q, :, :], start=(q == 0),
                                  stop=False, skip_group_check=True)
                    for i in range(4):
                        pe.matmul(arg[:, w % 2, i, :], selm[ML, 8 * d + 4 * hg + i, :],
                                  g["negm"][ML, c * C:(c + 1) * C], start=False, stop=False, skip_group_check=True)
                    pe.matmul(arg[:, w % 2, :, :], negi[:, :], mk[:, d, :, :], start=False, stop=True,
                              skip_group_check=True).then_inc(arg_done, 1)
                if 1 <= w <= U:
                    wn = w - 1
                    cn, hg, d = wn // 4, (wn % 4) // 2, wn % 2
                    pe.wait_ge(wm_done, wn + 1)
                    if cn >= 1:
                        pe.wait_ge(qw_done, 2 * cn + d + 1)
                        if cn == 1:
                            pe.wait_ge(c0_in, 16)
                        else:
                            pe.wait_ge(misc_used, misc_at[f"st{hg}", cn - 1] + 1)
                    for j in range(2):
                        n = 2 * wn + j
                        if n >= 2:
                            pe.wait_ge(h_copied, n - 1)
                        for i in range(2):
                            h = 4 * hg + 2 * j + i
                            dst = num[:, n % 2, i * DV1:(i + 1) * DV1]
                            m = pe.matmul(dst, wm[:, wn % 2, 2 * j + i, :], v[:, cn, h, :], start=True,
                                          stop=(cn == 0), skip_group_check=True)
                            if cn >= 1:
                                st = cf[:, cn % 2, h // 2, :] if d == 0 else snap[:, cn - 1, h // 2, :]
                                m = pe.matmul(dst, qw[:, d, h % 2, h // 2, :], st, start=False, stop=True,
                                              skip_group_check=True)
                        m.then_inc(num_done, 1)
                if (r == 3 and 1 <= c <= NC - 2) or (r == 0 and 2 <= c <= NC - 1):
                    j = 0 if r == 3 else 1
                    cs = c - j
                    pe.wait_ge(vw_ready, cs)
                    shared((f"st{j}", cs))
                    for h in range(4 * j, 4 * j + 4):
                        p0 = slice(64 * (h % 2), 64 * (h % 2) + 64)
                        i = (h // 2) % 2
                        m = pe.matmul(misc[p0, i * DV1:(i + 1) * DV1], kt[:, cs, h * DK:(h + 1) * DK], vw[:, h, :],
                                      start=True, stop=True, skip_group_check=True)
                    m.then_inc(misc_done, 1)
                for name, j, r0, back in (("tr0", 0, 1, 2), ("tr1", 1, 2, 2)):
                    if r == r0 and back <= c <= NC - 1 + back:
                        cc = c - back
                        pe.wait_ge(hn_done, cc + 1)
                        shared((name, cc))
                        for i in range(4):
                            m = pe.transpose(misc[:, i * P:(i + 1) * P],
                                             hs[:, cc % 2, (4 * j + i) * P:(4 * j + i + 1) * P], const(k, "ident"))
                        m.then_inc(misc_done, 1)

        @block.scalar
        def _(act):
            link = Chain(act, act_c)
            act.activation(fh[:, :, :], g["dec"][:, :, 32:48], ACT.Copy).then_inc(split_hi, 1)
            for d, mask in enumerate(("gt", "lt")):
                act.activation(after[:, d, :], const(k, mask), ACT.Copy).then_inc(after_ready, 1)
            for n in range(NC // 3):
                act.wait_ge(wi_done, n + 1)
                act.activation(wir[ML, 3 * n * C:3 * (n + 1) * C], misc[ML, 0:3 * C], ACT.Copy).then_inc(wi_row, 1)

            def one_head(c):
                act.wait_ge(qk_in[c % 2], 16 * (c // 2 + 1))
                if c >= 2:
                    act.wait_ge(sc_done, 2 * (c - 1))
                    act.wait_ge(qw_done, 2 * (c - 1))
                for half in range(2):
                    act.activation(qm[:, c % 2, half, :, :], qk[:, c % 2, 0:4, :], ACT.Copy,
                                   scale=const(k, f"half{half}")).then_inc(qm_ready, 1)

            one_head(0)
            for w in range(U + 7):
                c, r = w // 4, w % 4
                if w < U:
                    hg, d = r // 2, r % 2
                    act.wait_ge(arg_done, w + 1)
                    if w >= 2:
                        act.wait_ge(wm_done, w - 1)
                    for i in range(4):
                        j = 32 + 8 * d + 4 * hg + i
                        m = act.activation(e[:, w % 2, i, :], arg[:, w % 2, i, :], ACT.Exp,
                                           bias=g["dt_ig"][:, c, j:j + 1])
                    m.then_inc(exp_done, 1)
                if r == 2 and c + 1 < NC:
                    one_head(c + 1)
                if 1 <= w <= U:
                    wn = w - 1
                    cn, hg, d = wn // 4, (wn % 4) // 2, wn % 2
                    if cn >= 2 and wn % 4 == 0:
                        act.wait_ge(hm_done, cn - 1)
                    for j in range(2):
                        n = 2 * wn + j
                        act.wait_ge(num_done, n + 1)
                        act.activation(hb[:, cn % 2, d, 4 * hg + 2 * j:4 * hg + 2 * j + 2, :],
                                       num[:, n % 2, 0:2 * DV1].rearrange("p (a x) -> p a x", a=2),
                                       ACT.Copy).then_inc(h_copied, 1)
                if r in (1, 2) and 2 <= c <= NC + 1:
                    j, cc = r - 1, c - 2
                    act.wait_ge(misc_done, misc_at[f"tr{j}", cc] + 1)
                    if cc >= 2:
                        act.wait_ge(ho_out[cc % 2], 16 * (cc // 2))
                    for i in range(4 * j, 4 * j + 4):
                        m = act.activation(ho[:, cc % 2, i, :], misc[:, (i % 4) * P:(i % 4 + 1) * P], ACT.Copy,
                                           scale=col(k, "ml_norm", i))
                    m.then_inc(misc_used, 1)
                if r == 3 and 1 <= c <= NC:
                    cc = c - 1
                    act.wait_ge(ss_done, cc + 1)
                    link(act.activation(ss[:, cc % 2, :], ss[:, cc % 2, :], ACT.Ln, bias=const(k, "eps"),
                                        scale=1.0 / DV))
                    act.activation(ss[:, cc % 2, :], ss[:, cc % 2, :], ACT.Exp, scale=-0.5).then_inc(rs_done, 1)

        @block.vector
        def _(dve):
            link = Chain(dve, chain)
            dve.wait_ge(split_hi, 1)
            dve.tensor_tensor(fl[:, :, :], g["dec"][:, :, 32:48], fh[:, :, :].bitcast(F32),
                              ALU.subtract).then_inc(split_lo, 1)
            dve.tensor_scalar(negi[:, :], const(k, "ident"), NEG, None, ALU.mult).then_inc(mk_ready, 1)
            for d, mask in enumerate(("gt", "lt")):
                dve.tensor_copy(mk[:, d, :, :], spread(const(k, mask).unsqueeze(1), [P, 4, C])).then_inc(mk_ready, 1)

            def cf_view(c, j):
                return cf[:, (c + 1) % 2, 2 * j:2 * j + 2, :]

            def decay_state(c, j):
                if c == 1:
                    dve.wait_ge(c0_in, 16)
                else:
                    dve.wait_ge(num_done, 8 * c)
                    dve.wait_ge(misc_used, misc_at[f"st{j}", c - 1] + 1)
                for half in range(2):
                    p0 = slice(64 * half, 64 * half + 64)
                    link(dve.tensor_tensor(cf_view(c, j)[p0], cf_view(c - 1, j)[p0], ml_decay(g, 0, c, 2 * j, 2, half),
                                           ALU.mult))

            def add_state(c, j):
                dve.wait_ge(misc_done, misc_at[f"st{j}", c] + 1)
                dve.tensor_tensor(cf_view(c, j), cf_view(c, j),
                                  misc[:, 0:2 * DV1].rearrange("p (a x) -> p a x", a=2),
                                  ALU.add).then_inc(misc_used, 1)

            for w in range(U + 7):
                c, r = w // 4, w % 4
                if r < 2 and 2 <= c <= NC - 1:
                    add_state(c - 1, r)
                if w < U:
                    hg, d, s = r // 2, r % 2, c % 2
                    if r < 2:
                        if c >= 1:
                            dve.wait_ge(qb_done, 2 * (c - 1) + r + 1)
                            if c >= 2:
                                dve.wait_ge(num_done, 2 * (4 * (c - 1) + 2 + r) + 2)
                            for half in range(2):
                                m = dve.tensor_tensor(qw[:, r, half, :, :], qm[:, s, half, :, :], qb[:, :, :],
                                                      ALU.mult)
                            m.then_inc(qw_done, 1)
                        else:
                            dve.sem_inc(qw_done, 1)
                    dve.wait_ge(exp_done, w + 1)
                    if w >= 2:
                        dve.wait_ge(num_done, 2 * (w - 1))
                    dve.wait_ge(sc_done, w // 2 + 1)
                    dve.tensor_tensor(wm[:, w % 2, :, :], e[:, w % 2, :, :], sc[:, (w // 2) % 2, :, :],
                                      ALU.mult).then_inc(wm_done, 1)
                if r == 1 and 1 <= c <= NC:
                    cc = c - 1
                    q = cc % 2
                    dve.wait_ge(h_copied, 8 * (cc + 1))
                    dn = hb[:, q, :, :, DV]
                    link(dve.scalar_tensor_tensor(out=den[:, :, :], in0=dn, scalar=-1.0, in1=dn, op0=ALU.mult,
                                                  op1=ALU.max))
                    link(dve.tensor_tensor(den[:, :, :], den[:, :, :],
                                           g["em"][:, cc, :].rearrange("p (d h) -> p d h", d=2), ALU.max))
                    link(dve.reciprocal(den[:, :, :], den[:, :, :]))
                    h3 = hs[:, q, :].rearrange("p (h x) -> p h x", h=MH)
                    s3 = sqb[:, :].rearrange("p (h x) -> p h x", h=MH)
                    if cc >= 2:
                        dve.wait_ge(misc_done, misc_at["tr1", cc - 2] + 1)
                    link(dve.tensor_tensor(h3, hb[:, q, 0, :, 0:DV], spread(den[:, 0, :].unsqueeze(2), [P, MH, DV]),
                                           ALU.mult))
                    link(dve.tensor_tensor(s3, hb[:, q, 1, :, 0:DV], spread(den[:, 1, :].unsqueeze(2), [P, MH, DV]),
                                           ALU.mult))
                    dve.sem_inc(hm_done, 1)
                if r == 2 and 1 <= c <= NC:
                    cc = c - 1
                    q = cc % 2
                    s3 = sqb[:, :].rearrange("p (h x) -> p h x", h=MH)
                    link(dve.tensor_tensor(hs[:, q, :], hs[:, q, :], sqb[:, :], ALU.add))
                    link(dve.tensor_tensor(sqb[:, :], hs[:, q, :], hs[:, q, :], ALU.mult))
                    dve.tensor_reduce(ss[:, q, :], s3, AX.X, ALU.add).then_inc(ss_done, 1)
                    dve.wait_ge(ss_done, cc + 1)
                if r == 0 and 2 <= c <= NC + 1:
                    cc = c - 2
                    q = cc % 2
                    h3 = hs[:, q, :].rearrange("p (h x) -> p h x", h=MH)
                    dve.wait_ge(rs_done, cc + 1)
                    link(dve.tensor_tensor(h3, h3, spread(ss[:, q, :].unsqueeze(2), [P, MH, DV]), ALU.mult))
                    dve.wait_ge(og_in[q], 16 * (cc // 2 + 1))
                    dve.tensor_tensor(hs[:, q, :], hs[:, q, :], og[:, q, :], ALU.mult).then_inc(hn_done, 1)
                if (r == 3 and 1 <= c <= NC - 2) or (r == 0 and 2 <= c <= NC - 1):
                    decay_state(c if r == 3 else c - 1, 0 if r == 3 else 1)


def out_proj(nc, a, k, h, ah, al, up, scr):
    with ExitStack() as ctx:
        NT3 = 3 * KD
        raw = ctx.enter_context(nc.sbuf_tensor("raw_o", [P, 4, KD, P], F32))
        wh = ctx.enter_context(nc.sbuf_tensor("wh_o", [P, 2, KD, P], F32R))
        wl = ctx.enter_context(nc.sbuf_tensor("wl_o", [P, 2, KD, P], F32R))
        XR = 5
        xr = ctx.enter_context(nc.sbuf_tensor("xr", [P, XR, T], F32))
        gt = ctx.enter_context(nc.sbuf_tensor("gt", [P, 2, T], F32))
        tm = ctx.enter_context(nc.sbuf_tensor("tm", [P, T], F32))
        ssq = ctx.enter_context(nc.sbuf_tensor("ssq2", [P, T], F32))
        xs = xr[:, 0:3, :]
        scl = ctx.enter_context(nc.sbuf_tensor("scl2", [P, KD, 2], F32))
        one = ctx.enter_context(nc.sbuf_tensor("one2", [P, P + 1], F32))
        acc = [ctx.enter_context(nc.psum_tensor(f"acc_o{i}", [P, 3, 512], F32))[:, :, 0:TB] for i in range(2)]
        w_hi, w_lo, a_hi, a_lo, tile_done, out_done, chain = open_sems(
            nc, ctx, "o_w_hi", "o_w_lo", "o_a_hi", "o_a_lo", "o_tile", "o_out", "chain_o")
        raw_in = open_sems(nc, ctx, *[f"o_raw{i}" for i in range(4)])
        xr_in = open_sems(nc, ctx, *[f"o_xr{i}" for i in range(XR)])
        gt_in = open_sems(nc, ctx, "o_gt0", "o_gt1")
        one_set, ssq_ready, ss_done, log, rstd_ready, scl_ready, xs_ready, u_ready, hi_done, lo_v, lo_p = open_sems(
            nc, ctx, *["n2_" + n for n in ("one", "ssq", "ss", "log", "rstd", "scl", "xs", "u", "hi", "lo_v",
                                           "lo_p")])
        block = ctx.enter_context(nc.Block())
        PART = ((0, slice(0, CTX)), (1, slice(CTX, T)))

        @block.sync
        def _(sp):
            def weight(i):
                if i >= 4:
                    sp.wait_ge(w_lo, i - 3)
                sp.dma_start(raw[:, i % 4, :, :], a["w_o"][i]).then_inc(raw_in[i % 4], 16)

            def operand(i):
                if i >= XR:
                    sp.wait_ge(a_lo, i - XR + 1)
                src = scr["yn" if i < KD else "hm"][:, i % KD, :]
                sp.dma_start(xr[:, i % XR, :], src).then_inc(xr_in[i % XR], 16)

            for load, i0, i1 in ((weight, 0, 1), (operand, 0, KD), (weight, 1, 4), (operand, KD, KD + XR),
                                 (weight, 4, 12), (operand, KD + XR, 2 * KD), (weight, 12, NT3)):
                for i in range(i0, i1):
                    load(i)
            for i in range(2):
                sp.dma_start(up["raw"][:, i, :, :], a["w_up"][i]).then_inc(up["raw_in"][i], 16)

        @block.gpsimd
        def _(pool):
            for i in range(NT3):
                if i >= 2:
                    pool.wait_ge(out_done, i - 1)
                src = scr["gate"][i] if i < 2 * KD else a["xT"][:, i - 2 * KD, :]
                pool.dma_start(gt[:, i % 2, :], src).then_inc(gt_in[i % 2], 16)
            for i in range(1, KD, 2):
                pool.wait_ge(hi_done, i + 1)
                pool.tensor_tensor(al[:, i, :], xs[:, i % 3, :], ah[:, i, :].bitcast(F32),
                                   ALU.subtract).then_inc(lo_p, 1)
            pool.wait_ge(lo_p, KD // 2)

        @block.scalar
        def _(act):
            def weight(i):
                act.wait_ge(raw_in[i % 4], 16 * (i // 4 + 1))
                if i >= 2:
                    act.wait_ge(tile_done, i - 1)
                act.activation(wh[:, i % 2, :, :], raw[:, i % 4, :, :], ACT.Copy).then_inc(w_hi, 1)

            weight(0)
            for i in range(NT3):
                if i % KD == 0:
                    gi = i // KD
                    if gi:
                        act.wait_ge(tile_done, i)
                    for q in range(KD):
                        n = i + q
                        if gi < 2:
                            act.wait_ge(xr_in[n % XR], 16 * (n // XR + 1))
                        else:
                            act.wait_ge(out_done, KD + q + 1)
                        act.activation(ah[:, q, :], xr[:, n % XR, :] if gi < 2 else h[:, q, :],
                                       ACT.Copy).then_inc(a_hi, 1)
                if i + 1 < NT3:
                    weight(i + 1)
            for i in range(2):
                act.wait_ge(up["raw_in"][i], 16)
                act.activation(up["wh"][:, i, :, :], up["raw"][:, i, :, :], ACT.Copy).then_inc(up["w_hi"], 1)
            act.wait_ge(ss_done, 1)
            act.wait_ge(one_set, 2)
            act.activation(blocks(ssq[:, :]), acc[0], ACT.Ln, bias=one[:, P:P + 1], scale=1.0 / D).then_inc(log, 1)
            act.wait_ge(log, 1)
            act.activation(ssq[:, :], ssq[:, :], ACT.Exp, scale=-0.5).then_inc(rstd_ready, 1)
            for i in range(KD):
                act.wait_ge(xs_ready, i + 1)
                for s, t in PART:
                    dst = xs[:, i % 3, t] if i % 2 else ah[:, i, t]
                    m = act.activation(dst, xs[:, i % 3, t], ACT.Identity, bias=k["mod"][:, 24 + i, s:s + 1])
                if i % 2:
                    m.then_inc(u_ready, 1)
                    act.wait_ge(u_ready, i // 2 + 1)
                    m = act.activation(ah[:, i, :], xs[:, i % 3, :], ACT.Copy)
                m.then_inc(hi_done, 1)

        @block.tensor
        def _(pe):
            for i in range(NT3):
                pe.wait_ge(w_hi, i + 1)
                pe.wait_ge(w_lo, i + 1)
                if i >= 2:
                    pe.wait_ge(out_done, i - 1)
                for kt in range(KD):
                    if i % KD == 0:
                        pe.wait_ge(a_lo, i + kt + 1)
                    m = split_product(pe, acc[i % 2], wh[:, i % 2, kt, :], wl[:, i % 2, kt, :], ah, al, kt,
                                      kt == KD - 1, kt == 0)
                m.then_inc(tile_done, 1)
            pe.wait_ge(ssq_ready, 1)
            pe.wait_ge(one_set, 1)
            for bank, t0, n in BLOCKS:
                m = pe.matmul(acc[0][:, bank, 0:n], one[:, 0:P], ssq[:, t0:t0 + n], start=True, stop=True)
            m.then_inc(ss_done, 1)

        @block.vector
        def _(dve):
            link = Chain(dve, chain)

            def weight(i):
                dve.wait_ge(w_hi, i + 1)
                dve.tensor_tensor(wl[:, i % 2, :, :], raw[:, i % 4, :, :], wh[:, i % 2, :, :].bitcast(F32),
                                  ALU.subtract).then_inc(w_lo, 1)

            def operand(n):
                j = n % KD
                dve.wait_ge(a_hi, n + 1)
                dve.tensor_tensor(al[:, j, :], xr[:, n % XR, :] if n < 2 * KD else h[:, j, :],
                                  ah[:, j, :].bitcast(F32), ALU.subtract).then_inc(a_lo, 1)

            dve.memset(one[:, 0:P], 1.0).then_inc(one_set, 1)
            dve.memset(one[:, P:P + 1], EPS).then_inc(one_set, 1)
            for s in range(2):
                dve.scalar_tensor_tensor(out=scl[:, :, s], in0=k["mod"][:, 32:40, s], scalar=1.0,
                                         in1=col(k, "norm_ffn", 0, KD), op0=ALU.add,
                                         op1=ALU.mult).then_inc(scl_ready, 1)
            weight(0)
            for i in range(NT3):
                gi, q = i // KD, i % KD
                if q == 0:
                    for j in range(2 if i else 0, KD):
                        operand(i + j)
                    if gi == 2:
                        dve.wait_ge(a_lo, NT3)
                if i + 1 < NT3:
                    weight(i + 1)
                else:
                    for j in range(2):
                        dve.wait_ge(up["w_hi"], j + 1)
                        dve.tensor_tensor(up["wl"][:, j, :, :], up["raw"][:, j, :, :],
                                          up["wh"][:, j, :, :].bitcast(F32), ALU.subtract).then_inc(up["w_lo"], 1)
                dve.wait_ge(tile_done, i + 1)
                if q == KD - 1 and gi < 2:
                    operand(i + 1)
                    operand(i + 2)
                dve.wait_ge(gt_in[i % 2], 16 * (i // 2 + 1))
                gate, dst = blocks(gt[:, i % 2, :]), blocks(h[:, q, :])
                if gi == 0:
                    link(dve.tensor_tensor(dst, acc[i % 2], gate, ALU.mult))
                elif gi == 1:
                    link(dve.tensor_tensor(blocks(tm[:, :]), acc[i % 2], gate, ALU.mult))
                    link(dve.tensor_tensor(h[:, q, :], h[:, q, :], tm[:, :], ALU.add))
                else:
                    for s, t, view in PARTS:
                        link(dve.scalar_tensor_tensor(out=part(h[:, q, :], t), in0=view(acc[i % 2]),
                                                      scalar=k["mod"][:, 16 + q, s:s + 1],
                                                      in1=part(gt[:, i % 2, :], t), op0=ALU.mult, op1=ALU.add))
                dve.sem_inc(out_done, 1)
                if gi == 2:
                    link(dve.tensor_tensor(tm[:, :] if q else ssq[:, :], h[:, q, :], h[:, q, :], ALU.mult))
                    if q:
                        link(dve.tensor_tensor(ssq[:, :], ssq[:, :], tm[:, :], ALU.add))
            dve.sem_inc(ssq_ready, 1)
            dve.wait_ge(scl_ready, 2)
            dve.wait_ge(rstd_ready, 1)

            def scaled(i):
                if i >= 3:
                    dve.wait_ge(*((lo_p, (i - 3) // 2 + 1) if (i - 3) % 2 else (lo_v, (i - 3) // 2 + 1)))
                for s, t in PART:
                    m = dve.scalar_tensor_tensor(out=xs[:, i % 3, t], in0=h[:, i, t], scalar=scl[:, i, s:s + 1],
                                                 in1=ssq[:, t], op0=ALU.mult, op1=ALU.mult)
                m.then_inc(xs_ready, 1)

            scaled(0)
            for i in range(KD):
                if i + 1 < KD:
                    scaled(i + 1)
                if i % 2 == 0:
                    dve.wait_ge(hi_done, i + 1)
                    for s, t in PART:
                        m = dve.scalar_tensor_tensor(out=al[:, i, t], in0=xs[:, i % 3, t],
                                                     scalar=k["mod"][:, 24 + i, s:s + 1],
                                                     in1=ah[:, i, t].bitcast(F32), op0=ALU.add, op1=ALU.subtract)
                    m.then_inc(lo_v, 1)
            dve.wait_ge(lo_v, KD // 2)


def ffn(nc, a, k, h, uh, ul, up_, o):
    with ExitStack() as ctx:
        NG, NU, RING, AR = FT // 2, 2 * FT, 2, 3
        PR, PW = ROWS + 2, GRID_W + 2
        PIECES = 3 * KD
        HALF = PIECES // 2
        raw, wh, wl, raw_in, w_hi, w_lo = (up_[n] for n in ("raw", "wh", "wl", "raw_in", "w_hi", "w_lo"))
        dr = ctx.enter_context(nc.sbuf_tensor("raw_d", [P, 2, D], F32))
        dh = ctx.enter_context(nc.sbuf_tensor("wh_d", [P, 2, D], F32R))
        dl = ctx.enter_context(nc.sbuf_tensor("wl_d", [P, 2, D], F32R))
        fh = ctx.enter_context(nc.sbuf_tensor("fh", [P, AR, T], F32R))
        fl = ctx.enter_context(nc.sbuf_tensor("fl", [P, AR, T], F32R))
        gp = ctx.enter_context(nc.sbuf_tensor("gp", [P, PR, PW], F32))
        gc = ctx.enter_context(nc.sbuf_tensor("gc", [P, CTX + 2], F32))
        y = ctx.enter_context(nc.sbuf_tensor("y", [P, 2, T], F32))
        piece = ctx.enter_context(nc.sbuf_tensor("piece", [P, 2, TB], F32))
        one = ctx.enter_context(nc.sbuf_tensor("one3", [P, P + 1], F32))
        ssq, rstd = y[:, 0, :], y[:, 1, :]
        acc = [ctx.enter_context(nc.psum_tensor(f"acc_u{i}", [P, 3, 512], F32))[:, :, 0:TB] for i in range(2)]
        dacc = ctx.enter_context(nc.psum_tensor("dacc", [P, 2, 512], F32))
        (d_in, d_hi, d_lo, up_done, g_evac, pad_zero, conv_done, silu_done, act_done, f_hi, f_lo,
         piece_done, piece_out, piece_added, chain) = open_sems(
            nc, ctx, *["u_" + n for n in (
                "d_in", "d_hi", "d_lo", "up_done", "g_evac", "pad_zero", "conv_done", "silu_done",
                "act_done", "f_hi", "f_lo", "piece_done", "piece_out", "piece_added", "chain")])
        one_set, ssq_ready, ss_done, log, rstd_ready, y_ready = open_sems(
            nc, ctx, *["n3_" + n for n in ("one", "ssq", "ss", "log", "rstd", "y")])
        y_out = o["y0_out"], o["y1_out"]
        block = ctx.enter_context(nc.Block())

        @block.sync
        def _(sp):
            for i in range(NU):
                if i >= RING:
                    sp.wait_ge(w_lo, i - RING + 1)
                    sp.dma_start(raw[:, i % RING, :, :], a["w_up"][i]).then_inc(raw_in[i % RING], 16)
                if i % 4 == 1:
                    if i // 4:
                        sp.wait_ge(d_lo, i // 4)
                    sp.dma_start(dr[:, :, :], a["w_down"][i // 4]).then_inc(d_in, 16)
            for i in range(KD):
                sp.wait_ge(y_ready, i + 1)
                sp.dma_start(o["y"][:, i, :], h[:, i, :]).then_inc(y_out[i % 2], 16)
            for s in range(2):
                sp.wait_ge(y_out[s], 16 * (KD // 2))

        @block.tensor
        def _(pe):
            def up(i):
                pe.wait_ge(w_hi, i + 1)
                pe.wait_ge(w_lo, i + 1)
                f = i // 2
                if f >= 1:
                    if i % 2 == 0:
                        pe.wait_ge(g_evac, f)
                    else:
                        pe.wait_ge(act_done, f)
                for kt in range(KD):
                    m = split_product(pe, acc[i % 2], wh[:, i % 2, kt, :], wl[:, i % 2, kt, :], uh, ul, kt,
                                      kt == KD - 1, kt == 0)
                m.then_inc(up_done, 1)

            def down(q0, q1):
                j = q0 // PIECES
                pe.wait_ge(d_hi, j + 1)
                pe.wait_ge(d_lo, j + 1)
                pe.wait_ge(f_hi, 2 * j + 2)
                pe.wait_ge(f_lo, 2 * j + 2)
                for q in range(q0, q1):
                    m_, (bank, t0, n) = q % PIECES // 3, BLOCKS[q % 3]
                    if q >= 2:
                        pe.wait_ge(piece_out, q - 1)
                    cols = slice(m_ * P, m_ * P + P)
                    for r in range(2):
                        s = (2 * j + r) % AR
                        for p_, (w, x) in enumerate(((dh, fh), (dh, fl), (dl, fh))):
                            m = pe.matmul(dacc[:, q % 2, 0:n], w[:, r, cols], x[:, s, t0:t0 + n],
                                          start=(r == 0 and p_ == 0), stop=(r == 1 and p_ == 2))
                    m.then_inc(piece_done, 1)

            for f in range(FT):
                up(2 * f)
                if f >= 2:
                    down(HALF * (f - 2), HALF * (f - 1))
                up(2 * f + 1)
            down(HALF * (FT - 2), HALF * FT)
            pe.wait_ge(ssq_ready, 1)
            pe.wait_ge(one_set, 1)
            pe.wait_ge(g_evac, FT)
            for bank, t0, n in BLOCKS:
                m = pe.matmul(acc[0][:, bank, 0:n], one[:, 0:P], ssq[:, t0:t0 + n], start=True, stop=True)
            m.then_inc(ss_done, 1)

        @block.scalar
        def _(act):
            def high(i):
                act.wait_ge(raw_in[i % RING], 16 * (i // RING + 1))
                if i >= 2:
                    act.wait_ge(up_done, i - 1)
                act.activation(wh[:, i % 2, :, :], raw[:, i % RING, :, :], ACT.Copy).then_inc(w_hi, 1)

            def high_down(j):
                act.wait_ge(d_in, 16 * (j + 1))
                if j:
                    act.wait_ge(piece_done, 3 * KD * j)
                act.activation(dh[:, :, :], dr[:, :, :], ACT.Copy).then_inc(d_hi, 1)

            def evac(f):
                act.wait_ge(up_done, 2 * f + 1)
                if f == 0:
                    act.wait_ge(pad_zero, 2)
                else:
                    act.wait_ge(conv_done, f)
                act.activation(gc[:, 1:1 + CTX], PARTS[0][2](acc[0]), ACT.Copy)
                r = (TB - CTX) // GRID_W
                act.activation(gp[:, 1:1 + r, 1:1 + GRID_W],
                               PARTS[1][2](acc[0]).rearrange("p (r w) -> p r w", w=GRID_W), ACT.Copy)
                for b in (1, 2):
                    r0 = 1 + (b * TB - CTX) // GRID_W
                    m = act.activation(gp[:, r0:r0 + TB // GRID_W, 1:1 + GRID_W],
                                       acc[0][:, b, :].rearrange("p (r w) -> p r w", w=GRID_W), ACT.Copy)
                m.then_inc(g_evac, 1)

            def silu(f):
                act.wait_ge(conv_done, f + 1)
                act.activation(y[:, f % 2, :], y[:, f % 2, :], ACT.Silu,
                               bias=col(k, "ffn_b", f)).then_inc(silu_done, 1)

            def act_high(f):
                act.wait_ge(act_done, f + 1)
                if f >= AR:
                    act.wait_ge(piece_done, 3 * KD * ((f - AR) // 2 + 1))
                act.activation(fh[:, f % AR, :], y[:, f % 2, :], ACT.Copy).then_inc(f_hi, 1)

            def pieces(q0, q1):
                for q in range(q0, q1):
                    m_, bank = q % PIECES // 3, q % 3
                    act.wait_ge(piece_done, q + 1)
                    if q >= 2:
                        act.wait_ge(piece_added, q - 1)
                    for s_, p0, p1 in (((0, 0, CTX), (1, CTX, TB)) if bank == 0 else ((1, 0, TB),)):
                        m = act.activation(piece[:, q % 2, p0:p1], dacc[:, q % 2, p0:p1], ACT.Copy,
                                           scale=k["mod"][:, 40 + m_, s_:s_ + 1])
                    m.then_inc(piece_out, 1)

            for f in range(FT):
                evac(f)
                if f >= 2:
                    pieces(HALF * (f - 2), HALF * (f - 1))
                if 2 * f + 2 < NU:
                    high(2 * f + 2)
                silu(f)
                if 2 * f + 3 < NU:
                    high(2 * f + 3)
                act_high(f)
                if f % 2 == 1:
                    high_down(f // 2)
            pieces(HALF * (FT - 2), HALF * FT)
            act.wait_ge(ss_done, 1)
            act.wait_ge(one_set, 2)
            act.activation(blocks(rstd), acc[0], ACT.Ln, bias=one[:, P:P + 1], scale=1.0 / D).then_inc(log, 1)
            act.wait_ge(log, 1)
            act.activation(rstd, rstd, ACT.Exp, scale=-0.5).then_inc(rstd_ready, 1)

        @block.vector
        def _(dve):
            link = Chain(dve, chain)
            dve.memset(gp[:, :, :], 0.0).then_inc(pad_zero, 1)
            dve.memset(gc[:, :], 0.0).then_inc(pad_zero, 1)
            dve.memset(one[:, 0:P], 1.0).then_inc(one_set, 1)
            dve.memset(one[:, P:P + 1], EPS).then_inc(one_set, 1)

            def conv(f):
                dve.wait_ge(g_evac, f + 1)
                if f >= 2:
                    dve.wait_ge(f_lo, f - 1)
                yc = y[:, f % 2, 0:CTX]
                yl = y[:, f % 2, CTX:T].rearrange("p (r w) -> p r w", w=GRID_W)
                for n, (dx, tap) in enumerate(((0, 3), (1, 4), (2, 5))):
                    w = col(k, "ffn_w", 9 * f + tap)
                    x = gc[:, dx:dx + CTX]
                    link(dve.tensor_scalar(yc, x, w, None, ALU.mult) if n == 0 else
                         dve.scalar_tensor_tensor(out=yc, in0=x, scalar=w, in1=yc, op0=ALU.mult, op1=ALU.add))
                for tap in range(9):
                    if tap == 4 and 2 * f + 2 < NU:
                        low(2 * f + 2)
                    w = col(k, "ffn_w", 9 * f + tap)
                    x = gp[:, tap // 3:tap // 3 + ROWS, tap % 3:tap % 3 + GRID_W]
                    if tap == 0:
                        link(dve.tensor_scalar(yl, x, w, None, ALU.mult))
                    else:
                        ins = dve.scalar_tensor_tensor(out=yl, in0=x, scalar=w, in1=yl, op0=ALU.mult, op1=ALU.add)
                        if tap < 8:
                            link(ins)
                ins.then_inc(conv_done, 1)

            def low(i):
                dve.wait_ge(w_hi, i + 1)
                dve.tensor_tensor(wl[:, i % 2, :, :], raw[:, i % RING, :, :], wh[:, i % 2, :, :].bitcast(F32),
                                  ALU.subtract).then_inc(w_lo, 1)

            def times_value(f):
                dve.wait_ge(silu_done, f + 1)
                dve.wait_ge(up_done, 2 * f + 2)
                yb = blocks(y[:, f % 2, :])
                dve.tensor_tensor(yb, yb, acc[1], ALU.mult).then_inc(act_done, 1)

            def low_down(j):
                dve.wait_ge(d_hi, j + 1)
                dve.tensor_tensor(dl[:, :, :], dr[:, :, :], dh[:, :, :].bitcast(F32),
                                  ALU.subtract).then_inc(d_lo, 1)

            for f in range(FT):
                conv(f)
                times_value(f)
                if 2 * f + 3 < NU:
                    low(2 * f + 3)
                if f % 2 == 1:
                    low_down(f // 2)
            dve.wait_ge(f_hi, FT)
            dve.wait_ge(f_lo, FT - 1)
            dve.wait_ge(piece_done, 3 * KD * ((FT - 1 - AR) // 2 + 1))
            dve.tensor_tensor(fl[:, (FT - 1) % AR, :], y[:, (FT - 1) % 2, :], fh[:, (FT - 1) % AR, :].bitcast(F32),
                              ALU.subtract).then_inc(f_lo, 1)
            dve.wait_ge(f_lo, FT)
            for i in range(KD):
                dve.wait_ge(piece_added, HALF * (FT - 2) + 3 * (i + 1))
                link(dve.tensor_tensor(rstd if i else ssq, h[:, i, :], h[:, i, :], ALU.mult))
                if i:
                    link(dve.tensor_tensor(ssq, ssq, rstd, ALU.add))
            dve.sem_inc(ssq_ready, 1)
            dve.wait_ge(rstd_ready, 1)
            for i in range(KD):
                dve.scalar_tensor_tensor(out=h[:, i, :], in0=h[:, i, :], scalar=col(k, "final_norm", i),
                                         in1=rstd, op0=ALU.mult, op1=ALU.mult).then_inc(y_ready, 1)

        @block.gpsimd
        def _(pool):
            def add_pieces(q0, q1):
                for q in range(q0, q1):
                    m_, (bank, t0, n) = q % PIECES // 3, BLOCKS[q % 3]
                    pool.wait_ge(piece_out, q + 1)
                    x = h[:, m_, t0:t0 + n]
                    pool.tensor_tensor(x, x, piece[:, q % 2, :], ALU.add).then_inc(piece_added, 1)

            for f in range(FT):
                if f >= 2:
                    add_pieces(HALF * (f - 2), HALF * (f - 1))
                if f == FT - 1:
                    continue
                pool.wait_ge(f_hi, f + 1)
                if f >= AR:
                    pool.wait_ge(piece_done, 3 * KD * ((f - AR) // 2 + 1))
                pool.tensor_tensor(fl[:, f % AR, :], y[:, f % 2, :], fh[:, f % AR, :].bitcast(F32),
                                   ALU.subtract).then_inc(f_lo, 1)
            add_pieces(HALF * (FT - 2), HALF * FT)
            pool.wait_ge(piece_added, HALF * FT)
            pool.wait_ge(f_lo, FT - 1)


def constants():
    i, j = np.arange(P)[:, None], np.arange(P)[None, :]
    con = np.zeros((P, NCON), np.float32)
    for name, m in (("ident", i == j), ("le", i <= j), ("gt", i > j), ("ge", i >= j), ("lt", i < j),
                    ("ones", i >= 0), ("row127", i == P - 1), ("row0", i == 0)):
        con[:, CC[name]:CC[name] + P] = np.broadcast_to(m, (P, P))
    r = np.arange(P)
    con[:, CC["sign"]] = np.where(r < 32, 1.0, -1.0)
    con[:, CC["fwd"]] = (r >= 32) & (r < 40)
    con[:, CC["bwd"]] = (r >= 40) & (r < 48)
    con[:, CC["eps"]] = EPS
    con[:, CC["half0"]] = r < 64
    con[:, CC["half1"]] = r >= 64
    for q in range(16):
        con[32 + q, CC["i16"] + q] = 1.0
    for q in range(4):
        con[q, CC["s4"] + q % 2] = 1.0
    selm = np.zeros((48, 16, P), np.float32)
    selq = np.zeros((48, 8, P), np.float32)
    for q in range(16):
        selm[32 + q, q, :] = 1.0
        selq[32 + q, q // 2, 64 * (q % 2):64 * (q % 2) + 64] = 1.0
    return con, selm, selq


def tiles(w, cols, width):
    w = np.ascontiguousarray(w[:, cols] if cols is not None else w)
    return w.reshape(-1, P, w.shape[1] // width, width).transpose(2, 1, 0, 3)


def lay_out(i):
    f = {n: np.asarray(v) for n, v in i.items()}
    x = np.concatenate([f["x_prompt"][0], f["x_sample"][0]], 0)
    a = {"xT": x.T.reshape(KD, P, T).transpose(1, 0, 2)}
    a["cond"] = np.stack([f["c_ctx"], f["c"][0]], 1).reshape(KD, P, 2).transpose(1, 0, 2)
    a["w_ada"] = f["w_ada"][0].reshape(4, 2, P, 12, 512).transpose(3, 0, 2, 1, 4).reshape(48, P, KD, P)
    w = f["w_in"][0]
    at = {}
    n0 = 0
    for name, n in (("z", D), ("xbc", XBC), ("dt", 32), ("q", 512), ("k", 512), ("v", D), ("o", D), ("i", 16),
                    ("f", 16), ("g", 2 * D)):
        at[name] = w[:, n0:n0 + n]
        n0 += n
    zero = np.zeros((D, P), np.float32)
    per_head = np.concatenate([at["dt"], at["f"], zero[:, :16], at["i"], zero[:, 80:]], 1)
    a["w_in_ch"] = tiles(np.concatenate([per_head, at["xbc"], at["q"], at["k"], at["g"]], 1), None, P)
    a["w_in_tok"] = tiles(np.concatenate([at["z"], at["v"], at["o"]], 1), None, 512)
    a["w_o"] = np.concatenate([tiles(f[n][0], None, P) for n in ("w_o_ssd", "w_o_ml", "w_out")], 0)
    up = f["w_up"][0]
    a["w_up"] = np.stack([tiles(up[:, :FF], None, P), tiles(up[:, FF:], None, P)], 1).reshape(2 * FT, P, KD, P)
    a["w_down"] = f["w_down"][0].reshape(FT // 2, 2, P, D).transpose(0, 2, 1, 3)

    par = np.zeros((P, NPAR), np.float32)

    def put(name, v):
        v = v.reshape(-1, P).T
        par[:, PC[name]:PC[name] + v.shape[1]] = v

    for name in ("norm_mix", "b_ada", "norm_ffn", "ssd_norm", "ml_norm"):
        put(name, f[name][0])
    put("final_norm", f["final_norm"])
    put("conv_b", f["ssd_conv_b"][0])
    put("conv_w", f["ssd_conv_w"][0].reshape(3, XT, P).transpose(1, 0, 2))
    put("ffn_b", f["ffn_conv_b"][0])
    put("ffn_w", f["ffn_conv_w"][0].reshape(9, FT, P).transpose(1, 0, 2))
    par[0:32, PC["gate_bias"]] = f["ssd_dt_bias"][0].reshape(-1)
    par[32:48, PC["gate_bias"]] = f["ml_f_bias"][0].reshape(-1)
    par[32:48, PC["i_bias"]] = f["ml_i_bias"][0].reshape(-1)
    par[0:32, PC["a_log"]] = f["ssd_a_log"][0].reshape(-1)
    par[32:48, PC["m0"]] = f["state_mlstm_m"][0, 0].reshape(-1)
    a["params"] = par
    a["ssd_d"] = np.broadcast_to(np.repeat(f["ssd_d"][0], SP)[None], (P, D))
    s = f["state_ssd"][0, 0].reshape(2, 2, 2, HG, SP, SN).transpose(2, 5, 0, 1, 3, 4)
    a["s_ssd"] = s.reshape(P, 2, 512)
    cn = np.concatenate([f["state_mlstm_C"][0, 0], f["state_mlstm_n"][0, 0][:, :, None, :]], 2)
    a["s_ml"] = cn.reshape(2, 4, 2, DV1, DK).transpose(2, 4, 0, 1, 3).reshape(P, 2, 4, DV1)
    a["consts"], a["selm"], a["selq"] = constants()
    return {n: np.ascontiguousarray(v) for n, v in a.items()}


OUTS = {"y": (P, KD, T), "ssd": (P, 2, 512), "ml": (P, 2, 4, DV1), "m": (16, 1)}


def kernel(**inputs):
    import concourse.bacc as bacc
    from concourse.bass_utils import run_bass_kernel_spmd

    nc = bacc.Bacc("TRN2", target_bir_lowering=False, num_devices=1)
    arrays = {f"in_{n}": v for n, v in lay_out(inputs).items()}
    a = {n[3:]: nc.dram_tensor(n, v.shape, F32, kind="ExternalInput").ap() for n, v in arrays.items()}
    o = {n: nc.dram_tensor(f"out_{n}", s, F32, kind="ExternalOutput").ap() for n, s in OUTS.items()}
    build(nc, a, o)
    got = run_bass_kernel_spmd(nc, [arrays], core_ids=[0]).results[0]
    y = got["out_y"].transpose(2, 1, 0).reshape(T, D)
    s = got["out_ssd"].reshape(2, SN, 2, 2, HG, SP).transpose(2, 3, 0, 4, 5, 1).reshape(1, 1, 2, SH, SP, SN)
    cn = got["out_ml"].reshape(2, DK, 2, 4, DV1).transpose(2, 3, 0, 4, 1).reshape(1, 1, 2, MH, DV1, DK)
    c = np.ascontiguousarray
    return (c(y[None, :CTX]), c(y[None, CTX:]), c(s), c(cn[:, :, :, :, :DV]), c(cn[:, :, :, :, DV]),
            c(got["out_m"].reshape(1, 1, 2, MH)))
```
